# Optimizing a Trainium2 kernel written in Bass

```python
import jax, jax.numpy as jnp
from jax import lax
import numpy as np
import math

D_MODEL = 1024
BATCH = 1
SEQ = 256
DEPTH = 1

CHUNK = 64
P_DIM = 256
SB_HEAD_DIM = 64
SB_WIDTH = 3 * D_MODEL // 8
SB_HEADS = SB_WIDTH // SB_HEAD_DIM
SB_QBLOCK = 128
ML_HEADS = 4
ML_WIDTH = 3 * D_MODEL // 8
ML_HEAD_DIM = ML_WIDTH // ML_HEADS
CONV_K = 4
SGU_WIDTH = D_MODEL - SB_WIDTH - ML_WIDTH
SGU_GROUPS = 4
SGU_GROUP_DIM = SGU_WIDTH // SGU_GROUPS
SGU_BLOCK = 128
IN_SPLITS = (SB_WIDTH, SB_WIDTH, SB_WIDTH, ML_WIDTH, ML_WIDTH, ML_WIDTH, ML_WIDTH, ML_HEADS, ML_HEADS, SGU_WIDTH, SGU_WIDTH)
N_IN = 3 * SB_WIDTH + 4 * ML_WIDTH + 2 * ML_HEADS + 2 * SGU_WIDTH
N_GROUPS = 4
EXPERTS_PER_GROUP = 8
N_EXPERTS = N_GROUPS * EXPERTS_PER_GROUP
TOP_K = 2
D_EXPERT = D_MODEL // 4
MOE_BLOCK = 512
EPS = 1e-6


F32 = jnp.float32

def rms_norm(x, g):
    x32 = x.astype(F32)
    return x32 * lax.rsqrt(jnp.mean(x32 * x32, axis=-1, keepdims=True) + EPS) * g.astype(F32)

def split_cols(z, sizes):
    idx = np.cumsum(sizes)[:-1].tolist()
    return jnp.split(z, idx, axis=-1)

def causal_depthwise_conv(x, w, b):
    y = lax.conv_general_dilated(x.astype(F32), w.astype(F32)[:, None, :], window_strides=(1,),
                                 padding=[(CONV_K - 1, 0)], dimension_numbers=('NWC', 'WIO', 'NWC'),
                                 feature_group_count=x.shape[-1])
    return y + b.astype(F32)

def stick_breaking_attention(q, k, v):
    S = q.shape[1]
    scale = q.shape[-1] ** -0.5
    outs = []
    for n in range(S // SB_QBLOCK):
        t0 = n * SB_QBLOCK
        kend = t0 + SB_QBLOCK
        z = jnp.einsum('bthd,bshd->bhts', q[:, t0:kend], k[:, :kend]) * scale
        tpos = t0 + jnp.arange(SB_QBLOCK)
        spos = jnp.arange(kend)
        mask = spos[None, :] < tpos[:, None]
        log_1m = jnp.where(mask, -jax.nn.softplus(z), 0.0)
        after = lax.cumsum(log_1m, axis=3, reverse=True) - log_1m
        a = jnp.where(mask, jnp.exp(jax.nn.log_sigmoid(z) + after), 0.0)
        outs.append(jnp.einsum('bhts,bshd->bthd', a, v[:, :kend]))
    return jnp.concatenate(outs, axis=1)

def mlstm_chunkwise(q, k, v, i_pre, f_pre):
    Bn, S, H, d = q.shape
    N, L = S // CHUNK, CHUNK
    q = q.reshape(Bn, N, L, H, d)
    k = k.reshape(Bn, N, L, H, d) * (d ** -0.5)
    v = v.reshape(Bn, N, L, H, d)
    ig = i_pre.reshape(Bn, N, L, H)
    bcum = jnp.cumsum(jax.nn.log_sigmoid(f_pre.reshape(Bn, N, L, H)), axis=2)
    btot = bcum[:, :, -1]
    a = btot[:, :, None] - bcum + ig

    def step(carry, xs):
        c, nvec, m = carry
        k_c, v_c, a_c, bt_c = xs
        m_new = jnp.maximum(bt_c + m, a_c.max(axis=1))
        decay = jnp.exp(bt_c + m - m_new)
        w = jnp.exp(a_c - m_new[:, None])
        c_new = decay[..., None, None] * c + jnp.einsum('blh,blhd,blhe->bhde', w, k_c, v_c)
        n_new = decay[..., None] * nvec + jnp.einsum('blh,blhd->bhd', w, k_c)
        return (c_new, n_new, m_new), (c, nvec, m)

    init = (jnp.zeros((Bn, H, d, d), F32), jnp.zeros((Bn, H, d), F32), jnp.zeros((Bn, H), F32))
    xs = (jnp.moveaxis(k, 1, 0), jnp.moveaxis(v, 1, 0), jnp.moveaxis(a, 1, 0), jnp.moveaxis(btot, 1, 0))
    _, (c_in, n_in, m_in) = lax.scan(step, init, xs)
    c_in = jnp.moveaxis(c_in, 0, 1)
    n_in = jnp.moveaxis(n_in, 0, 1)
    m_in = jnp.moveaxis(m_in, 0, 1)

    bT = jnp.moveaxis(bcum, 2, -1)
    igT = jnp.moveaxis(ig, 2, -1)
    causal = jnp.tril(jnp.ones((L, L), dtype=bool))
    dmat = jnp.where(causal, bT[..., :, None] - bT[..., None, :] + igT[..., None, :], -jnp.inf)
    m_inter = bT + m_in[..., None]
    m_t = jnp.maximum(m_inter, dmat.max(axis=-1))
    wd = jnp.where(causal, jnp.exp(dmat - m_t[..., None]), 0.0)
    s = jnp.einsum('bnthd,bnshd->bnhts', q, k) * wd
    inter = jnp.exp(m_inter - m_t)
    num = jnp.einsum('bnhts,bnshd->bnthd', s, v) + jnp.einsum('bnhl,bnlhd,bnhde->bnlhe', inter, q, c_in)
    den = s.sum(axis=-1) + inter * jnp.einsum('bnlhd,bnhd->bnhl', q, n_in)
    den = jnp.maximum(jnp.abs(den), jnp.exp(-m_t))
    h = num / jnp.moveaxis(den, 2, -1)[..., None]
    return h.reshape(Bn, S, H, d)

def spatial_gating(u, v, ln_g, ln_b, w_s, b_s):
    Bn, S, _ = u.shape
    v = v.reshape(Bn, S, SGU_GROUPS, SGU_GROUP_DIM)
    mu = v.mean(axis=-1, keepdims=True)
    var = jnp.mean(jnp.square(v - mu), axis=-1, keepdims=True)
    v = (v - mu) * lax.rsqrt(var + EPS) * ln_g.reshape(SGU_GROUPS, SGU_GROUP_DIM) + ln_b.reshape(SGU_GROUPS, SGU_GROUP_DIM)
    v = v.reshape(Bn, S // SGU_BLOCK, SGU_BLOCK, SGU_GROUPS, SGU_GROUP_DIM)
    cpos = jnp.arange(SGU_BLOCK) // CHUNK
    mask = cpos[None, :] <= cpos[:, None]
    w = jnp.where(mask[None], w_s.astype(F32), 0.0)
    mixed = jnp.einsum('gts,bnsgc->bntgc', w, v) + b_s.astype(F32).T[:, :, None]
    return u * mixed.reshape(Bn, S, SGU_WIDTH)

def routed_experts(xt, e_idx, e_w, w_gate, w_up, w_down):
    T, D = xt.shape
    M = T * TOP_K
    flat_e = e_idx.reshape(M)
    order = jnp.argsort(flat_e)
    sorted_e = flat_e[order]
    sorted_tok = order // TOP_K
    sorted_w = e_w.reshape(M)[order]
    sizes = jnp.bincount(flat_e, length=N_EXPERTS)
    padded = (sizes + MOE_BLOCK - 1) // MOE_BLOCK * MOE_BLOCK
    start = jnp.cumsum(sizes) - sizes
    pend = jnp.cumsum(padded)
    pstart = pend - padded
    dest = pstart[sorted_e] + jnp.arange(M) - start[sorted_e]
    n_blocks = -(-(M + N_EXPERTS * (MOE_BLOCK - 1)) // MOE_BLOCK)
    rows = n_blocks * MOE_BLOCK
    row_tok = jnp.zeros((rows,), jnp.int32).at[dest].set(sorted_tok.astype(jnp.int32))
    row_w = jnp.zeros((rows,), F32).at[dest].set(sorted_w)
    block_e = jnp.minimum(jnp.searchsorted(pend, jnp.arange(n_blocks) * MOE_BLOCK, side='right'), N_EXPERTS - 1)

    def block_ffn(args):
        tok, wt, e = args
        xb = xt[tok]
        hb = jax.nn.silu(xb @ w_gate[e]) * (xb @ w_up[e])
        return (hb @ w_down[e]).astype(F32) * wt[:, None]

    yb = lax.map(block_ffn, (row_tok.reshape(n_blocks, MOE_BLOCK), row_w.reshape(n_blocks, MOE_BLOCK), block_e))
    return jnp.zeros((T, D), F32).at[row_tok].add(yb.reshape(rows, D))

def hierarchical_moe(h, rg_w, rg_b, re_w, re_b, w_gate, w_up, w_down):
    Bn, S, D = h.shape
    xt = h.reshape(Bn * S, D)
    g_logits = (xt @ rg_w + rg_b).astype(F32)
    g_prob = jax.nn.softmax(g_logits, axis=-1)
    g_top = jnp.argmax(g_logits, axis=-1)
    g_w = jnp.take_along_axis(g_prob, g_top[:, None], axis=-1)[:, 0]
    e_logits = (xt @ re_w + re_b).astype(F32).reshape(-1, N_GROUPS, EXPERTS_PER_GROUP)
    e_in = jnp.take_along_axis(e_logits, g_top[:, None, None], axis=1)[:, 0]
    e_val, e_loc = lax.top_k(e_in, TOP_K)
    e_w = jax.nn.softmax(e_val, axis=-1) * g_w[:, None]
    e_idx = g_top[:, None].astype(jnp.int32) * EXPERTS_PER_GROUP + e_loc.astype(jnp.int32)
    y = routed_experts(xt, e_idx, e_w, w_gate, w_up, w_down)
    return y.reshape(Bn, S, D)

def first_inputs(seed: int = 0) -> dict:
    key = jax.random.key(seed)
    ks = jax.random.split(key, 32)

    def nrm(k, shape, scale):
        return jax.random.normal(k, shape, F32) * scale

    def gain(k, shape):
        return 1.0 + 0.05 * jax.random.normal(k, shape, F32)

    D = D_MODEL
    return {
        "x": nrm(ks[0], (BATCH, SEQ, D), 1.0),
        "p": nrm(ks[1], (DEPTH, BATCH, SEQ, P_DIM), 1.0),
        "norm1_g": gain(ks[2], (DEPTH, D)),
        "w_in": nrm(ks[3], (DEPTH, D, N_IN), D ** -0.5),
        "conv_w": nrm(ks[4], (DEPTH, CONV_K, 2 * ML_WIDTH), CONV_K ** -0.5),
        "conv_b": nrm(ks[5], (DEPTH, 2 * ML_WIDTH), 0.01),
        "igate_b": nrm(ks[6], (DEPTH, ML_HEADS), 0.1),
        "fgate_b": jnp.linspace(3.0, 6.0, ML_HEADS, dtype=F32)[None, :] + nrm(ks[7], (DEPTH, ML_HEADS), 0.1),
        "mnorm_g": gain(ks[8], (DEPTH, ML_WIDTH)),
        "sb_out_g": gain(ks[9], (DEPTH, SB_WIDTH)),
        "sgu_ln_g": gain(ks[10], (DEPTH, SGU_WIDTH)),
        "sgu_ln_b": nrm(ks[11], (DEPTH, SGU_WIDTH), 0.01),
        "sgu_w": nrm(ks[12], (DEPTH, SGU_GROUPS, SGU_BLOCK, SGU_BLOCK), SGU_BLOCK ** -0.5),
        "sgu_b": gain(ks[13], (DEPTH, SGU_GROUPS, SGU_BLOCK)),
        "sgu_out_g": gain(ks[14], (DEPTH, SGU_WIDTH)),
        "w_out": nrm(ks[15], (DEPTH, D, D), D ** -0.5),
        "norm2_g": gain(ks[16], (DEPTH, D)),
        "router_gw": nrm(ks[17], (DEPTH, D, N_GROUPS), D ** -0.5),
        "router_gb": nrm(ks[18], (DEPTH, N_GROUPS), 0.01),
        "router_ew": nrm(ks[19], (DEPTH, D, N_EXPERTS), D ** -0.5),
        "router_eb": nrm(ks[20], (DEPTH, N_EXPERTS), 0.01),
        "w_gate": nrm(ks[21], (DEPTH, N_EXPERTS, D, D_EXPERT), D ** -0.5),
        "w_up": nrm(ks[22], (DEPTH, N_EXPERTS, D, D_EXPERT), D ** -0.5),
        "w_down": nrm(ks[23], (DEPTH, N_EXPERTS, D_EXPERT, D), D_EXPERT ** -0.5),
        "ple_norm_g": gain(ks[24], (DEPTH, D)),
        "ple_gate_w": nrm(ks[25], (DEPTH, D, D), D ** -0.5),
        "ple_proj_w": nrm(ks[26], (DEPTH, P_DIM, D), P_DIM ** -0.5),
        "final_g": gain(ks[27], (D,)),
    }

def first_block(x, p, norm1_g, w_in, conv_w, conv_b, igate_b, fgate_b, mnorm_g, sb_out_g,
              sgu_ln_g, sgu_ln_b, sgu_w, sgu_b, sgu_out_g, w_out, norm2_g,
              router_gw, router_gb, router_ew, router_eb, w_gate, w_up, w_down,
              ple_norm_g, ple_gate_w, ple_proj_w, final_g):
    Bn, S, D = x.shape
    h = x.astype(F32)
    for i in range(DEPTH):
        hn = rms_norm(h, norm1_g[i])
        z = hn @ w_in[i]
        qa, ka, va, qb, kb, vb, ob, ib, fb, uc, vc = split_cols(z, IN_SPLITS)
        ya = stick_breaking_attention(qa.reshape(Bn, S, SB_HEADS, SB_HEAD_DIM),
                                      ka.reshape(Bn, S, SB_HEADS, SB_HEAD_DIM),
                                      va.reshape(Bn, S, SB_HEADS, SB_HEAD_DIM)).reshape(Bn, S, SB_WIDTH)
        ya = rms_norm(ya, sb_out_g[i])
        qk = jax.nn.silu(causal_depthwise_conv(jnp.concatenate([qb, kb], axis=-1), conv_w[i], conv_b[i]))
        qb, kb = jnp.split(qk, 2, axis=-1)
        hb = mlstm_chunkwise(qb.reshape(Bn, S, ML_HEADS, ML_HEAD_DIM),
                             kb.reshape(Bn, S, ML_HEADS, ML_HEAD_DIM),
                             vb.astype(F32).reshape(Bn, S, ML_HEADS, ML_HEAD_DIM),
                             ib + igate_b[i], fb + fgate_b[i])
        hb = rms_norm(hb, mnorm_g[i].reshape(ML_HEADS, ML_HEAD_DIM)).reshape(Bn, S, ML_WIDTH)
        yb = hb * jax.nn.sigmoid(ob)
        yc = spatial_gating(jax.nn.gelu(uc), jax.nn.gelu(vc), sgu_ln_g[i], sgu_ln_b[i], sgu_w[i], sgu_b[i])
        yc = rms_norm(yc, sgu_out_g[i])
        h = h + jnp.concatenate([ya, yb, yc], axis=-1) @ w_out[i]
        h = h + hierarchical_moe(rms_norm(h, norm2_g[i]), router_gw[i], router_gb[i], router_ew[i], router_eb[i],
                                 w_gate[i], w_up[i], w_down[i])
        gate = jax.nn.sigmoid(rms_norm(h, ple_norm_g[i]) @ ple_gate_w[i])
        h = h + gate * (p[i] @ ple_proj_w[i]).astype(F32)
    return rms_norm(h, final_g).astype(x.dtype)


CONV_WIDTH = D_MODEL
CONV_TAPS = 31
DIFF_HEADS = 8
DIFF_HEAD_DIM = 64
DIFF_V_DIM = 2 * DIFF_HEAD_DIM
QK_WIDTH = DIFF_HEADS * 2 * DIFF_HEAD_DIM
ATTN_WIDTH = DIFF_HEADS * DIFF_V_DIM
ROPE_THETA = 500000.0
ROPE_DIM = DIFF_HEAD_DIM // 4
Q_BLOCK = 128
IN_SIZES = (CONV_WIDTH, CONV_WIDTH, QK_WIDTH, QK_WIDTH, ATTN_WIDTH, D_MODEL, D_MODEL)
IN_WIDTH = 2 * CONV_WIDTH + 2 * QK_WIDTH + ATTN_WIDTH + 2 * D_MODEL
N_EXPERTS_2 = 64
N_GROUPS_2 = 8
TOPK_GROUPS = 4
TOP_K_2 = 8
EXPERT_DIM = 256
SHARED_DIM = 256
ROUTED_SCALE = 2.5
MOE_CHUNK = 128


def rms_norm_2(x, g):
    x32 = x.astype(jnp.float32)
    y = x32 * lax.rsqrt(jnp.mean(x32 * x32, axis=-1, keepdims=True) + EPS)
    return y.astype(x.dtype) * g

def layer_norm(x, g, b):
    x32 = x.astype(jnp.float32)
    mu = jnp.mean(x32, axis=-1, keepdims=True)
    xc = x32 - mu
    y = xc * lax.rsqrt(jnp.mean(xc * xc, axis=-1, keepdims=True) + EPS)
    return y.astype(x.dtype) * g + b

def rope(x, cos, sin):
    half = ROPE_DIM // 2
    x1, x2, xp = x[..., :half], x[..., half:ROPE_DIM], x[..., ROPE_DIM:]
    return jnp.concatenate([x1 * cos - x2 * sin, x2 * cos + x1 * sin, xp], axis=-1)

def conformer_conv(a, b, w_dw, b_dw, ln_g, ln_b, w_pw2, b_pw2):
    u = a * jax.nn.sigmoid(b)
    u = lax.conv_general_dilated(
        u, w_dw[:, None, :], window_strides=(1,), padding=[(CONV_TAPS - 1, 0)],
        dimension_numbers=('NWC', 'WIO', 'NWC'), feature_group_count=CONV_WIDTH) + b_dw
    u = jax.nn.silu(layer_norm(u, ln_g, ln_b))
    return u @ w_pw2 + b_pw2

def diff_attention(q, k, v, cos, sin, q_g, k_g, lq1, lk1, lq2, lk2, subln_g, lambda_init):
    B, S, _ = q.shape
    H, d = DIFF_HEADS, DIFF_HEAD_DIM
    q = q.reshape(B, S, H, 2, d).transpose(0, 2, 3, 1, 4)
    k = k.reshape(B, S, H, 2, d).transpose(0, 2, 3, 1, 4)
    v = v.reshape(B, S, H, DIFF_V_DIM).transpose(0, 2, 1, 3)
    q = rope(rms_norm_2(q, q_g), cos, sin)
    k = rope(rms_norm_2(k, k_g), cos, sin)
    f32 = jnp.float32
    lam = (jnp.exp(jnp.sum(lq1.astype(f32) * lk1.astype(f32)))
           - jnp.exp(jnp.sum(lq2.astype(f32) * lk2.astype(f32))) + lambda_init)
    nb = S // Q_BLOCK
    q_blocks = jnp.moveaxis(q.reshape(B, H, 2, nb, Q_BLOCK, d), 3, 0)
    starts = jnp.arange(nb, dtype=jnp.int32) * Q_BLOCK
    k_idx = jnp.arange(S, dtype=jnp.int32)
    scale = d ** -0.5

    def block(args):
        qb, start = args
        s = jnp.einsum('bhmqd,bhmkd->bhmqk', qb, k).astype(f32) * scale
        causal = k_idx[None, :] <= (start + jnp.arange(Q_BLOCK, dtype=jnp.int32))[:, None]
        p = jax.nn.softmax(jnp.where(causal, s, -jnp.inf), axis=-1)
        a = p[:, :, 0] - lam * p[:, :, 1]
        return jnp.einsum('bhqk,bhkv->bhqv', a.astype(v.dtype), v)

    o = lax.map(block, (q_blocks, starts))
    o = jnp.moveaxis(o, 0, 2).reshape(B, H, S, DIFF_V_DIM)
    o = rms_norm_2(o, subln_g) * (1.0 - lambda_init)
    return o.transpose(0, 2, 1, 3).reshape(B, S, ATTN_WIDTH)

def moe_ffn(h, w_router, router_bias, w_gu, w_down, w_sh_gu, w_sh_down):
    B, S, D = h.shape
    f32 = jnp.float32
    t = h.reshape(B * S, D)
    scores = jax.nn.sigmoid((t @ w_router).astype(f32))
    choice = scores + router_bias.astype(f32)
    per_group = N_EXPERTS_2 // N_GROUPS_2
    group_score = lax.top_k(choice.reshape(-1, N_GROUPS_2, per_group), 2)[0].sum(-1)
    _, gidx = lax.top_k(group_score, TOPK_GROUPS)
    gmask = jax.nn.one_hot(gidx, N_GROUPS_2, dtype=f32).sum(-2)
    emask = jnp.repeat(gmask, per_group, axis=-1) > 0
    _, eidx = lax.top_k(jnp.where(emask, choice, -jnp.inf), TOP_K_2)
    w = jnp.take_along_axis(scores, eidx, axis=-1)
    w = w / jnp.sum(w, axis=-1, keepdims=True) * ROUTED_SCALE
    gates = jnp.einsum('tk,tke->te', w, jax.nn.one_hot(eidx, N_EXPERTS_2, dtype=f32)).astype(h.dtype)
    nc = t.shape[0] // MOE_CHUNK

    def chunk(args):
        tc, gc = args
        g, u = jnp.split(jnp.einsum('td,edf->tef', tc, w_gu), 2, axis=-1)
        return jnp.einsum('tef,efd->td', jax.nn.silu(g) * u * gc[..., None], w_down)

    routed = lax.map(chunk, (t.reshape(nc, MOE_CHUNK, D),
                             gates.reshape(nc, MOE_CHUNK, N_EXPERTS_2))).reshape(B * S, D)
    sg, su = jnp.split(t @ w_sh_gu, 2, axis=-1)
    shared = (jax.nn.silu(sg) * su) @ w_sh_down
    return (routed + shared).reshape(B, S, D)

def second_inputs(seed: int = 0) -> dict:
    key = jax.random.key(seed)
    ks = jax.random.split(key, 32)
    L, D, C = DEPTH, D_MODEL, CONV_WIDTH
    f32 = jnp.float32

    def nrm(k, shape, scale):
        return jax.random.normal(k, shape, f32) * scale

    def gain(k, shape):
        return 1.0 + 0.05 * jax.random.normal(k, shape, f32)

    return {
        'x': nrm(ks[0], (BATCH, SEQ, D), 1.0),
        'c': nrm(ks[1], (BATCH, D), 1.0),
        'positions': jnp.broadcast_to(jnp.arange(SEQ, dtype=jnp.int32), (BATCH, SEQ)),
        'w_ada': nrm(ks[2], (L, D, 6 * D), 0.5 * D ** -0.5),
        'b_ada': nrm(ks[3], (L, 6 * D), 0.02),
        'norm1_g': gain(ks[4], (L, D)),
        'w_in': nrm(ks[5], (L, D, IN_WIDTH), D ** -0.5),
        'conv_dw': nrm(ks[6], (L, CONV_TAPS, C), CONV_TAPS ** -0.5),
        'conv_dw_b': nrm(ks[7], (L, C), 0.02),
        'conv_ln_g': gain(ks[8], (L, C)),
        'conv_ln_b': nrm(ks[9], (L, C), 0.02),
        'w_pw2': nrm(ks[10], (L, C, D), C ** -0.5),
        'b_pw2': nrm(ks[11], (L, D), 0.02),
        'q_norm_g': gain(ks[12], (L, DIFF_HEAD_DIM)),
        'k_norm_g': gain(ks[13], (L, DIFF_HEAD_DIM)),
        'lambda_q1': nrm(ks[14], (L, DIFF_HEAD_DIM), 0.1),
        'lambda_k1': nrm(ks[15], (L, DIFF_HEAD_DIM), 0.1),
        'lambda_q2': nrm(ks[16], (L, DIFF_HEAD_DIM), 0.1),
        'lambda_k2': nrm(ks[17], (L, DIFF_HEAD_DIM), 0.1),
        'subln_g': gain(ks[18], (L, DIFF_V_DIM)),
        'w_out': nrm(ks[19], (L, D, D), D ** -0.5),
        'norm2_g': gain(ks[20], (L, D)),
        'w_router': nrm(ks[21], (L, D, N_EXPERTS_2), D ** -0.5),
        'router_bias': nrm(ks[22], (L, N_EXPERTS_2), 0.01),
        'w_exp_gu': nrm(ks[23], (L, N_EXPERTS_2, D, 2 * EXPERT_DIM), D ** -0.5),
        'w_exp_down': nrm(ks[24], (L, N_EXPERTS_2, EXPERT_DIM, D), EXPERT_DIM ** -0.5),
        'w_sh_gu': nrm(ks[25], (L, D, 2 * SHARED_DIM), D ** -0.5),
        'w_sh_down': nrm(ks[26], (L, SHARED_DIM, D), SHARED_DIM ** -0.5),
    }

def second_block(x, c, positions, w_ada, b_ada, norm1_g, w_in, conv_dw, conv_dw_b, conv_ln_g,
              conv_ln_b, w_pw2, b_pw2, q_norm_g, k_norm_g, lambda_q1, lambda_k1, lambda_q2,
              lambda_k2, subln_g, w_out, norm2_g, w_router, router_bias, w_exp_gu, w_exp_down,
              w_sh_gu, w_sh_down):
    inv_freq = ROPE_THETA ** (-jnp.arange(0, ROPE_DIM, 2, dtype=jnp.float32) / ROPE_DIM)
    ang = positions.astype(jnp.float32)[:, None, None, :, None] * inv_freq
    cos = jnp.cos(ang).astype(x.dtype)
    sin = jnp.sin(ang).astype(x.dtype)
    c_act = jax.nn.silu(c)
    offsets = []
    acc = 0
    for s in IN_SIZES[:-1]:
        acc += s
        offsets.append(acc)
    for l in range(DEPTH):
        lambda_init = 0.8 - 0.6 * math.exp(-0.3 * l)
        mod = c_act @ w_ada[l] + b_ada[l]
        sh1, sc1, g1, sh2, sc2, g2 = [m[:, None, :] for m in jnp.split(mod, 6, axis=-1)]
        h = rms_norm_2(x, norm1_g[l]) * (1 + sc1) + sh1
        proj = h @ w_in[l]
        ca, cb, q, k, v, gate_conv, gate_attn = jnp.split(proj, offsets, axis=-1)
        y_conv = conformer_conv(ca, cb, conv_dw[l], conv_dw_b[l], conv_ln_g[l], conv_ln_b[l],
                                w_pw2[l], b_pw2[l])
        y_attn = diff_attention(q, k, v, cos, sin, q_norm_g[l], k_norm_g[l], lambda_q1[l],
                                lambda_k1[l], lambda_q2[l], lambda_k2[l], subln_g[l], lambda_init)
        merged = jax.nn.sigmoid(gate_conv) * y_conv + jax.nn.sigmoid(gate_attn) * y_attn
        x = x + g1 * (merged @ w_out[l])
        h2 = rms_norm_2(x, norm2_g[l]) * (1 + sc2) + sh2
        x = x + g2 * moe_ffn(h2, w_router[l], router_bias[l], w_exp_gu[l], w_exp_down[l],
                             w_sh_gu[l], w_sh_down[l])
    return x


def setup_inputs(seed=0):
    out = dict(first_inputs(seed))
    for name, value in second_inputs(seed + 1).items():
        if name != "x":
            out[name + "_2"] = value
    return out


def reference(
    x, p, norm1_g, w_in, conv_w, conv_b, igate_b, fgate_b, mnorm_g, sb_out_g, sgu_ln_g,
    sgu_ln_b, sgu_w, sgu_b, sgu_out_g, w_out, norm2_g, router_gw, router_gb, router_ew,
    router_eb, w_gate, w_up, w_down, ple_norm_g, ple_gate_w, ple_proj_w, final_g, c_2,
    positions_2, w_ada_2, b_ada_2, norm1_g_2, w_in_2, conv_dw_2, conv_dw_b_2, conv_ln_g_2,
    conv_ln_b_2, w_pw2_2, b_pw2_2, q_norm_g_2, k_norm_g_2, lambda_q1_2, lambda_k1_2,
    lambda_q2_2, lambda_k2_2, subln_g_2, w_out_2, norm2_g_2, w_router_2, router_bias_2,
    w_exp_gu_2, w_exp_down_2, w_sh_gu_2, w_sh_down_2,
):
    x = first_block(
        x, p, norm1_g, w_in, conv_w, conv_b, igate_b, fgate_b, mnorm_g, sb_out_g, sgu_ln_g,
        sgu_ln_b, sgu_w, sgu_b, sgu_out_g, w_out, norm2_g, router_gw, router_gb, router_ew,
        router_eb, w_gate, w_up, w_down, ple_norm_g, ple_gate_w, ple_proj_w, final_g,
    )
    return second_block(
        x, c_2, positions_2, w_ada_2, b_ada_2, norm1_g_2, w_in_2, conv_dw_2, conv_dw_b_2,
        conv_ln_g_2, conv_ln_b_2, w_pw2_2, b_pw2_2, q_norm_g_2, k_norm_g_2, lambda_q1_2,
        lambda_k1_2, lambda_q2_2, lambda_k2_2, subln_g_2, w_out_2, norm2_g_2, w_router_2,
        router_bias_2, w_exp_gu_2, w_exp_down_2, w_sh_gu_2, w_sh_down_2,
    )


_drawn_inputs = setup_inputs


def setup_inputs(seed=0):
    import zlib

    import numpy as np

    out = dict(_drawn_inputs(seed))
    spreads = {}
    factors = {'conv_b': 3.664,
     'igate_b': 46.644,
     'sgu_ln_b': 3.869,
     'router_gb': 3.415,
     'router_eb': 2.961,
     'ple_norm_g': 2.904,
     'norm1_g_2': 2.667,
     'conv_dw_b_2': 4.176,
     'conv_ln_g_2': 3.118,
     'conv_ln_b_2': 7.364,
     'b_pw2_2': 5.397,
     'q_norm_g_2': 4.268,
     'k_norm_g_2': 5.502,
     'lambda_q1_2': 124.96,
     'lambda_k1_2': 124.312,
     'lambda_q2_2': 7.469,
     'lambda_k2_2': 4.346,
     'subln_g_2': 2.757}
    for name, (base, spread) in spreads.items():
        noise = np.random.default_rng([zlib.crc32(name.encode()), seed]).standard_normal(out[name].shape)
        drawn = base * np.exp(spread * noise) if base else spread * noise
        out[name] = __import__('jax').numpy.asarray(drawn.astype(out[name].dtype))
    for name, factor in factors.items():
        out[name] = (out[name] * factor).astype(out[name].dtype)
    return out
```

```python
import contextlib
import math

import numpy as np

import concourse.bass as bass
from concourse import mybir

F32 = mybir.dt.float32
I32 = mybir.dt.int32
ALU = mybir.AluOpType
ACT = mybir.ActivationFunctionType
AX = mybir.AxisListType

P = 128
T = 256
TT = T // P
D = 1024
KC = D // P
EPS = 1e-6
RING = 6
SLOT = KC * 512

SBW, SBH, SBD = 384, 6, 64
MLW, MLH, MLD = 384, 4, 96
SGW, SGG, SGD = 256, 4, 64
CONV_K = 4
TAPS = 31
AH, AD = 8, 64
ROT = 8
THETA = 500000.0
LAMBDA0 = 0.2
ROUTED_SCALE = 2.5
TWO_PI = 2 * math.pi
R_N1, R_YG, R_PLE, R_SGB, R_C = 0, 8, 16, 24, 28
N_ROWS = 36


OFF = 1024


SLOTS = 64
ACC, BG, BT, BD = 0, 4, 5, 6


class Moe:
    pass


def steps(eng, n, body):
    body(0, 0)
    body(1, 1)
    with eng.Fori(1, n // 2 - 1) as it:
        for par in range(2):
            body(it * 2 + par, par, it)
    body(n - 2, 0)
    body(n - 1, 1)


def here(i, n, ahead):
    return not isinstance(i, int) or 0 <= i + ahead < n


def wait_if(eng, sem, value):
    if not isinstance(value, int) or value > 0:
        eng.wait_ge(sem, value)


def overflow(eng, m, ev, body):
    eng.wait_ge(ev(m.p + "list"), 1)
    n = eng.value_load(m.lst[0:1, 2 * P:2 * P + 1], min_val=0, max_val=2 * m.NOV)
    with eng.Fori(0, m.NOV // 2) as q:
        for par in range(2):
            with eng.If(n > q * 4 + 2 * par):
                body(q * 2 + par, q, par)


def listed(eng, m, o, which):
    e = eng.value_load(m.lst[0:1, bass.ds(o * 2 + which, 1)], min_val=0, max_val=m.E - 1)
    c = eng.value_load(m.lst[0:1, bass.ds(o * 2 + (P + which), 1)], min_val=0, max_val=4 * SLOTS)
    return e, c


def moe_sp(sp, m, ev):
    def pair(i, par, it=0):
        for r in range(3):
            slot = m.slots[par][r]
            if isinstance(i, int) and i < 2:
                if m.before[par][r]:
                    sp.wait_ge(ev(m.before[par][r][0]), m.before[par][r][1])
            elif r < 2:
                sp.wait_ge(ev(m.p + "gu"), i - 1)
            else:
                sp.wait_ge(ev(m.p + "down"), i * 2 - 2)
            if r < 2:
                m.load_gu(sp, slot, i * 2 + r, ev(f"w_in{slot}"))
            else:
                for h in range(2):
                    m.load_d(sp, slot, h, i * 2 + h, ev(f"w_in{slot}"))
    steps(sp, m.N, pair)

    def extra(o, q, par):
        sp.wait_ge(ev(f"{m.p}o_free{par}"), q + 1)
        experts = [listed(sp, m, o, h)[0] for h in range(2)]
        for h in range(2):
            m.load_gu(sp, m.slots[par][h], experts[h], ev(f"{m.p}o_w{par}"))
        for h in range(2):
            m.load_d(sp, m.slots[par][2], h, experts[h], ev(f"{m.p}o_w{par}"))
    overflow(sp, m, ev, extra)
    sp.wait_ge(ev(m.p + "acc"), 1)


def moe_pool(pool, m, ev):
    def gather(par, name):
        pool.tensor_tensor(m.idxf[:, par:par + 1], m.sc[:, par, 0:1], m.off, ALU.add)
        pool.drain()
        pool.tensor_copy(m.idx[:, par:par + 1], m.idxf[:, par:par + 1])
        pool.drain()
        pool.indirect_dma_start(out=m.xs[:, par, :], out_offset=None, in_=m.rows,
                                in_offset=bass.IndirectOffsetOnAxis(ap=m.idx[:, par:par + 1], axis=0),
                                bounds_check=T - 1, oob_is_err=False).then_inc(ev(name), 16)

    pool.wait_ge(ev(m.p + "rows"), 16)
    pool.wait_ge(ev(m.p + "xs_clear"), 1)
    for j in range(2):
        pool.wait_ge(ev(m.p + "sc"), j + 1)
        gather(j, f"{m.p}gath{j}")

    def step(i, par, it=0):
        if here(i, m.N, 2):
            pool.wait_ge(ev(m.p + "T"), i * 2 + 2)
            pool.wait_ge(ev(m.p + "sc"), i + 3)
            gather(par, f"{m.p}gath{par}")
    steps(pool, m.N, step)

    def extra(o, q, par):
        pool.wait_ge(ev(m.p + "o_sc"), o + 1)
        gather(0, m.p + "o_gath")
    overflow(pool, m, ev, extra)


def moe_act(act, m, ev, ps):
    def rows_out(name, at, r):
        act.wait_ge(ev(name + "T"), at)
        act.copy(m.xsT[:, 4 * r:4 * r + 4, :].rearrange("p a b -> p (a b)"), ps[:, BT, :]).then_inc(ev(name + "Te"), 1)

    def silu(name, i):
        act.wait_ge(ev(name + "gu"), i + 1)
        act.activation(m.sg, ps[:, BG, 0:256], ACT.Silu).then_inc(ev(name + "silu"), 1)

    def y_out(name, at):
        act.wait_ge(ev(name + "down"), at)
        act.copy(m.ys[:, 0:512], ps[:, BD, :]).then_inc(ev(name + "ya"), 1)

    rows_out(m.p, 1, 0)
    rows_out(m.p, 2, 1)

    def step(i, par, it=0):
        wait_if(act, ev(m.p + "hid"), i)
        silu(m.p, i)
        if here(i, m.N, 1):
            rows_out(m.p, i * 2 + 3, 0)
            rows_out(m.p, i * 2 + 4, 1)
        wait_if(act, ev(m.p + "comb"), i)
        y_out(m.p, i * 2 + 1)
    steps(act, m.N, step)

    def extra(o, q, par):
        rows_out(m.p + "o_", o * 2 + 1, 0)
        rows_out(m.p + "o_", o * 2 + 2, 1)
        silu(m.p + "o_", o)
        y_out(m.p + "o_", o * 2 + 1)
    overflow(act, m, ev, extra)


def moe_dve(dve, m, ev, ps):
    def onehot(e, name):
        dve.tensor_copy(m.tgs, m.tg[:, :, bass.ds(e * 2, 4)])
        dve.tensor_tensor(m.oneh, m.iota[:, 0:SLOTS].unsqueeze(1).unsqueeze(1).to_broadcast([P, TT, 2, SLOTS]),
                          m.pos[:, :, bass.ds(e, 2)].unsqueeze(3).to_broadcast([P, TT, 2, SLOTS]),
                          ALU.is_equal).then_inc(ev(name), 1)

    def spread(par, name):
        dve.tensor_scalar(m.S[:, par, :], m.iota[:, 5 * SLOTS:5 * SLOTS + T], m.sc[:, par, 0:1], m.sc[:, par, 1:2],
                          ALU.is_equal, ALU.mult).then_inc(ev(name), 1)

    dve.memset(m.xs, 0.0).then_inc(ev(m.p + "xs_clear"), 1)
    for j in range(2):
        onehot(2 * j, m.p + "oneh")
        dve.wait_ge(ev(m.p + "ip"), j + 1)
        dve.tensor_copy(m.sc[:, j, :], ps[:, BG, 256:258]).then_inc(ev(m.p + "sc"), 1)
    dve.drain()
    spread(0, m.p + "S")

    def step(i, par, it=0):
        if here(i, m.N, 2):
            wait_if(dve, ev(m.p + "hT"), i)
            onehot(i * 2 + 4, m.p + "oneh")
        dve.wait_ge(ev(m.p + "silu"), i + 1)
        dve.tensor_tensor(m.hid, m.sg, ps[:, BG, 256:512], ALU.mult).then_inc(ev(m.p + "hid"), 1)
        dve.wait_ge(ev(m.p + "hT"), i + 1)
        dve.tensor_copy(m.hidT.rearrange("p a b -> p (a b)"), ps[:, BG, 0:256])
        if here(i, m.N, 2):
            dve.tensor_copy(m.sc[:, par, :], ps[:, BG, 256:258]).then_inc(ev(m.p + "sc"), 1)
        dve.drain().then_inc(ev(m.p + "hTe"), 1)
        if here(i, m.N, 1):
            spread(1 - par, m.p + "S")
        dve.wait_ge(ev(m.p + "down"), i * 2 + 2)
        dve.tensor_copy(m.ys[:, 512:1024], ps[:, BD + 1, :]).then_inc(ev(m.p + "yv"), 1)
    steps(dve, m.N, step)

    def extra(o, q, par):
        dve.wait_ge(ev(m.p + "o_comb"), o + 1)
        for h in range(2):
            e, c = listed(dve, m, o, h)
            dve.tensor_copy(m.tgs[:, :, 2 * h:2 * h + 2], m.tg[:, :, bass.ds(e * 2, 2)])
            for t in range(TT):
                dve.tensor_tensor(m.oneh[:, t, h, :], m.iota[:, bass.ds(c, SLOTS)],
                                  m.pos[:, t, bass.ds(e, 1)].to_broadcast([P, SLOTS]), ALU.is_equal)
        dve.drain().then_inc(ev(m.p + "o_oneh"), 1)
        dve.wait_ge(ev(m.p + "o_ip"), o + 1)
        dve.tensor_copy(m.sc[:, 0, :], ps[:, BG, 256:258]).then_inc(ev(m.p + "o_sc"), 1)
        dve.drain()
        spread(0, m.p + "o_S")
        dve.wait_ge(ev(m.p + "o_silu"), o + 1)
        dve.tensor_tensor(m.hid, m.sg, ps[:, BG, 256:512], ALU.mult).then_inc(ev(m.p + "o_hid"), 1)
        dve.wait_ge(ev(m.p + "o_hT"), o + 1)
        dve.tensor_copy(m.hidT.rearrange("p a b -> p (a b)"), ps[:, BG, 0:256]).then_inc(ev(m.p + "o_hTe"), 1)
        dve.wait_ge(ev(m.p + "o_down"), o * 2 + 2)
        dve.tensor_copy(m.ys[:, 512:1024], ps[:, BD + 1, :]).then_inc(ev(m.p + "o_yv"), 1)
    overflow(dve, m, ev, extra)


def moe_pe(pe, m, ev, ps):
    def slots(name):
        for h in range(2):
            for t in range(TT):
                last = pe.matmul(ps[64 * h:64 * h + 64, BG, 256:258], m.oneh[:, t, h, :], m.tgs[:, t, 2 * h:2 * h + 2],
                                 start=(t == 0), stop=(t == TT - 1), skip_group_check=True)
        if name:
            last.then_inc(ev(name), 1)

    def transpose(par, r, name):
        for c in range(4):
            last = pe.transpose(ps[:, BT, c * P:(c + 1) * P], m.xs[:, par, (4 * r + c) * P:(4 * r + c + 1) * P], m.ident)
        last.then_inc(ev(name + "T"), 1)

    def gate_up(w, name):
        for k in range(KC):
            for h in range(2):
                last = pe.matmul(ps[64 * h:64 * h + 64, BG, :], m.xsT[:, k, 64 * h:64 * h + 64], w[h][:, k, :],
                                 start=(k == 0), stop=(k == KC - 1), skip_group_check=True)
        last.then_inc(ev(name + "gu"), 1)

    def hidden(name):
        for k in range(2):
            last = pe.transpose(ps[:, BG, k * P:(k + 1) * P], m.hid[:, k * P:(k + 1) * P], m.ident)
        last.then_inc(ev(name + "hT"), 1)

    def down(w, name):
        for n in range(2):
            for k in range(2):
                for h in range(2):
                    last = pe.matmul(ps[64 * h:64 * h + 64, BD + n, :], m.hidT[:, k, 64 * h:64 * h + 64],
                                     w[:, 2 * h + k, n * 512:(n + 1) * 512], start=(k == 0), stop=(k == 1),
                                     skip_group_check=True)
            last.then_inc(ev(name + "down"), 1)

    def combine(par, name):
        for t in range(TT):
            for n in range(2):
                last = pe.matmul(ps[:, ACC + 2 * t + n, :], m.S[:, par, t * P:(t + 1) * P], m.ys[:, n * 512:(n + 1) * 512],
                                 start=False, stop=True, skip_group_check=True)
        last.then_inc(ev(name + "comb"), 1)

    def arrived(i, par, it, r):
        first, per = m.totals[par][r]
        value = first + per * (i // 2 + 1) if isinstance(i, int) else it * per + (first + per)
        pe.wait_ge(ev(f"w_in{m.slots[par][r]}"), value)

    for j in range(2):
        pe.wait_ge(ev(m.p + "oneh"), j + 1)
        if j:
            pe.wait_ge(ev(m.p + "sc"), 1)
        slots(m.p + "ip")
    pe.wait_ge(ev(m.p + "gath0"), 16)
    transpose(0, 0, m.p)
    pe.wait_ge(ev(m.p + "Te"), 1)
    transpose(0, 1, m.p)
    pe.wait_ge(ev(m.p + "sc"), 2)

    def step(i, par, it=0):
        pe.wait_ge(ev(m.p + "Te"), i * 2 + 2)
        wait_if(pe, ev(m.p + "hTe"), i)
        for r in range(2):
            arrived(i, par, it, r)
        gate_up([m.view_gu(m.slots[par][0]), m.view_gu(m.slots[par][1])], m.p)
        if here(i, m.N, 1):
            half = (i + 1) // 2 if isinstance(i, int) else it + par
            pe.wait_ge(ev(f"{m.p}gath{1 - par}"), half * 16 + 16)
            transpose(1 - par, 0, m.p)
        if here(i, m.N, -1):
            for n in ("ya", "yv", "S"):
                pe.wait_ge(ev(m.p + n), i)
            combine(1 - par, m.p)
        if here(i, m.N, 1):
            pe.wait_ge(ev(m.p + "Te"), i * 2 + 3)
            transpose(1 - par, 1, m.p)
        pe.wait_ge(ev(m.p + "hid"), i + 1)
        if here(i, m.N, 2):
            pe.wait_ge(ev(m.p + "oneh"), i + 3)
            slots(None)
        hidden(m.p)
        pe.wait_ge(ev(m.p + "hTe"), i + 1)
        arrived(i, par, it, 2)
        down(m.view_d(m.slots[par][2]), m.p)
    steps(pe, m.N, step)
    for n in ("ya", "yv", "S"):
        pe.wait_ge(ev(m.p + n), m.N)
    combine(1, m.p)
    pe.drain().then_inc(ev(m.p + "o_comb"), 1)
    for par in range(2):
        pe.drain().then_inc(ev(f"{m.p}o_free{par}"), 1)

    def extra(o, q, par):
        name = m.p + "o_"
        pe.wait_ge(ev(name + "oneh"), o + 1)
        slots(name + "ip")
        pe.wait_ge(ev(name + "gath"), o * 16 + 16)
        transpose(0, 0, name)
        pe.wait_ge(ev(name + "Te"), o * 2 + 1)
        transpose(0, 1, name)
        pe.wait_ge(ev(name + "Te"), o * 2 + 2)
        pe.wait_ge(ev(f"{name}w{par}"), q * m.pair_inc + m.pair_inc)
        gate_up([m.view_gu(m.slots[par][0]), m.view_gu(m.slots[par][1])], name)
        pe.wait_ge(ev(name + "hid"), o + 1)
        hidden(name)
        pe.wait_ge(ev(name + "hTe"), o + 1)
        down(m.view_d(m.slots[par][2]), name)
        for n in ("ya", "yv", "S"):
            pe.wait_ge(ev(name + n), o + 1)
        combine(0, name)
        pe.drain().then_inc(ev(f"{name}free{par}"), 1)
    overflow(pe, m, ev, extra)
    pe.drain().then_inc(ev(m.p + "acc"), 1)


def route_lists_pe(pe, m, ev, ps):
    pe.wait_ge(ev(m.p + "mask"), 1)
    E = m.E
    b = ps[:, BG, :]
    pe.matmul(b[:, 0:E], m.before_tri, m.mask[:, 0, :], start=True, stop=True)
    pe.matmul(b[:, E:2 * E], m.ones, m.mask[:, 0, :], start=True, stop=False)
    pe.matmul(b[:, E:2 * E], m.before_tri, m.mask[:, 1, :], start=False, stop=True)
    pe.matmul(b[:, 2 * E:3 * E], m.ones, m.mask[:, 0, :], start=True, stop=False)
    pe.matmul(b[:, 2 * E:3 * E], m.ones, m.mask[:, 1, :], start=False, stop=True).then_inc(ev(m.p + "posp"), 1)
    pe.wait_ge(ev(m.p + "chunks"), 1)
    for j in range(2):
        last = pe.matmul(ps[0:1, BT, j * P:(j + 1) * P], m.chunk[:, j:j + 1], m.ident, start=True, stop=True)
    last.then_inc(ev(m.p + "chunkr"), 1)


def route_lists_dve(dve, m, ev, ps):
    E = m.E
    dve.drain().then_inc(ev(m.p + "mask"), 1)
    tg = m.tg.rearrange("p t (e c) -> p t e c", c=2)
    for t in range(TT):
        dve.tensor_copy(tg[:, t, :, 0], m.tok[:, t:t + 1].to_broadcast([P, E]))
    dve.tensor_copy(tg[:, :, :, 1], m.gate)
    dve.wait_ge(ev(m.p + "posp"), 1)
    b = ps[:, BG, :]
    dve.scalar_tensor_tensor(m.pos, b[:, 0:2 * E].rearrange("p (t e) -> p t e", t=TT), 1.0, m.mask, ALU.add, ALU.mult)
    for c in range(3):
        dve.tensor_scalar(m.flag[:, c, :], b[:, 2 * E:3 * E], float(SLOTS * (c + 1)), None, ALU.is_gt)
    dve.drain()
    dve.tensor_scalar(m.pos, m.pos, -1.0, None, ALU.add)
    flat = m.flag.rearrange("p c e -> p (c e)")
    dve.tensor_tensor_scan(m.rank, m.one3, flat, 0.0, ALU.mult, ALU.add)
    dve.drain()
    dve.scalar_tensor_tensor(m.sel, m.rank, m.part1, flat, ALU.is_equal, ALU.mult)
    dve.drain()
    for j, code in enumerate((m.code_e, m.code_c)):
        dve.tensor_tensor(m.code_t, m.sel, code, ALU.mult)
        dve.drain()
        dve.tensor_reduce(m.chunk[:, j:j + 1], m.code_t, AX.X, ALU.add)
        dve.drain()
    dve.tensor_scalar(m.chunk[:, 1:2], m.chunk[:, 1:2], float(4 * SLOTS), None, ALU.add)
    dve.drain().then_inc(ev(m.p + "chunks"), 1)
    dve.wait_ge(ev(m.p + "chunkr"), 1)
    dve.tensor_copy(m.lst[0:1, 0:2 * P], ps[0:1, BT, 0:2 * P])
    dve.tensor_copy(m.lst[0:1, 2 * P:2 * P + 1], m.rank[0:1, 3 * E - 1:3 * E])
    dve.drain().then_inc(ev(m.p + "list"), 1)


def build_program(nc, A, out):
    ctx = contextlib.ExitStack()
    with ctx:
        def sb(name, shape, dt=F32):
            return ctx.enter_context(nc.sbuf_tensor(name, shape, dt))

        sems = {}

        def ev(name):
            if name not in sems:
                sems[name] = nc.alloc_semaphore(name=name)
            return sems[name]

        def renew():
            old = [name for name in sems if not name.startswith("w_in")]
            nc.clear_and_free_semaphores([sems.pop(name) for name in old])

        BIG, FAR = 1e30, 3e38
        loose = dict(allow_small_or_imprecise_dtypes=True)

        ring = sb("ring", [P, RING, SLOT])
        x_tm = sb("x_tm", [P, TT, D])
        hn_tm = sb("hn_tm", [P, TT, D])
        hT = sb("hT", [P, KC, T])
        ident = sb("ident", [P, P])
        ntri = sb("ntri", [P, P])
        nones = sb("nones", [P, P])
        sel4 = sb("sel4", [MLH, MLH, P])
        selq = sb("selq", [P, P])
        rows = sb("rows", [N_ROWS, P])
        cols = sb("cols", [P, N_ROWS])
        rows96 = sb("rows96", [40, MLD])
        cols96 = sb("cols96", [MLD, 40])
        gate_w = sb("gate_w", [P, KC, 2 * MLH])
        gate_b = sb("gate_b", [MLH, 2])
        stat = sb("stat", [P, 64])
        eps_c = sb("eps_c", [P, 1])
        EPSC = eps_c[:, 0:1]
        scratch = sb("scratch", [P, TT, D])
        bada = sb("bada", [12, 512])
        modst = sb("modst", [1, 512])
        mod = nc.dram_tensor("mod", [1, 6 * D], F32, kind="Internal").ap()
        hrows = nc.dram_tensor("hrows", [T, D], F32, kind="Internal").ap()
        cact = sb("cact", [P, KC])
        crep = sb("crep", [P, KC, 32])
        adap = sb("adap", [P, 512])

        iota = sb("iota", [P, 5 * SLOTS + T])
        tok = sb("tok", [P, TT])
        off = sb("off", [P, 1])
        idxf = sb("idxf", [P, 2])
        part1 = sb("part1", [P, 1])
        ones = sb("ones", [P, 192])
        zero = sb("zero", [P, P])
        tri = sb("tri", [P, P])
        idx = sb("idx", [P, 2], I32)
        lst = sb("lst", [1, 2 * P + 1], I32)

        ps = ctx.enter_context(nc.psum_tensor("ps", [P, 8, 512], F32))

        WORK = 15808
        work = sb("work", [P, WORK])

        def carver(at=0):
            at = [at]
            def take(name, shape):
                n = 1
                for d in shape[1:]:
                    n *= d
                v = work[0:shape[0], at[0]:at[0] + n]
                at[0] += n
                assert at[0] <= WORK, (name, at[0])
                if len(shape) == 3:
                    v = v.rearrange("p (a b) -> p a b", a=shape[1])
                if len(shape) == 4:
                    v = v.rearrange("p (a b c) -> p a b c", a=shape[1], b=shape[2])
                return v
            return take
        mb = carver()
        qaT = mb("qaT", [P, 3, T])
        kaT = mb("kaT", [P, 3, T])
        va = mb("va", [P, TT, SBW])
        convbuf = mb("convbuf", [P, 2 * MLH * (T + CONV_K - 1)])
        cT = convbuf[0:MLD].rearrange("p (j t) -> p j t", j=2 * MLH)
        qkT = mb("qkT", [MLD, 2 * MLH, T])
        sg8 = hn_tm[0:MLD].rearrange("p a b -> p (a b)").rearrange("p (j t) -> p j t", j=2 * MLH)
        vba = mb("vba", [P, TT, MLH, MLD + 1])
        ob = mb("ob", [P, TT, MLW])
        uv = mb("uv", [P, TT, 2, SGW])
        gT = scratch[0:MLH].rearrange("p a b -> p (a b)").rearrange("p (r t) -> p r t", r=8)
        gcol = mb("gcol", [P, TT, 8])
        sgw = convbuf[:, 0:512].rearrange("p (g s) -> p g s", g=SGG)
        sgwT = convbuf[:, 512:1024].rearrange("p (g s) -> p g s", g=SGG)
        lnb = convbuf[:, 1024:1536].rearrange("p (a c) -> p a c", a=2)
        spb = mb("spb", [P, 2, 3 * P])
        spt = mb("spt", [P, 2, 3 * P])
        amt = mb("amt", [P, 2, 3 * P])
        dmt = spt

        def moe_buffers(prefix, E, chunks, rows_ap):
            m = Moe()
            take = carver()
            m.p, m.E, m.N = prefix, E, E // 2
            m.NOV = 2 * (-(-chunks // 4))
            m.rows, m.idx, m.lst, m.iota, m.tok, m.part1 = rows_ap, idx[:], lst, iota[:], tok, part1[:]
            m.off, m.idxf = off[:], idxf[:]
            m.ident, m.ones, m.before_tri, m.one3 = ident[:], ones[:, 0:P], tri[:], ones[:, 0:3 * E]
            m.tg = take("tg", [P, TT, 2 * E])
            m.pos = take("pos", [P, TT, E])
            m.mask = take("mask", [P, TT, E])
            m.gate = take("gate", [P, TT, E])
            m.flag = take("flag", [P, 3, E])
            m.rank, m.sel, m.code_t = (take(n, [P, 3 * E]) for n in ("rank", "sel", "code_t"))
            m.code_e, m.code_c = (take(n, [P, 3 * E]) for n in ("code_e", "code_c"))
            m.chunk = take("chunk", [P, 2])
            m.oneh = take("oneh", [P, TT, 2, SLOTS])
            m.tgs = take("tgs", [P, TT, 4])
            m.xs = take("xs", [P, 2, D])
            m.xsT = take("xsT", [P, KC, P])
            m.sg = take("sg", [P, 256])
            m.hid = take("hid", [P, 256])
            m.hidT = take("hidT", [P, 2, P])
            m.ys = take("ys", [P, D])
            m.S = take("S", [P, 2, T])
            m.sc = take("sc", [P, 2, 2])
            m.take = take
            m.view_gu = lambda slot: slot_view(slot, KC, 512)
            m.view_d = lambda slot: slot_view(slot, 4, D)
            return m

        m1 = moe_buffers("a_", 32, T * 2 // (SLOTS + 1), hrows)
        m1.incs = (32, 32, 32)
        m1.pair_inc = 96
        rw = m1.take("rw", [P, KC, 36])
        rb = m1.take("rb", [P, 36])
        bc1 = m1.take("bc1", [P, D])
        gl = m1.take("gl", [P, TT, 8])
        gv = m1.take("gv", [P, TT, 8])
        gr = m1.take("gr", [P, TT, 8])
        gm = m1.take("gm", [P, TT, 4])
        el = m1.take("el", [P, TT, 32])
        er = m1.take("er", [P, TT, 32])
        v8 = m1.take("v8", [P, TT, 8])
        p_tm = m1.take("p_tm", [P, TT, 256])
        pT = m1.take("pT", [P, 2, T])

        def load_gu1(eng, slot, e, sem):
            for j, w in enumerate((A["w_gate"], A["w_up"])):
                eng.dma_start(slot_view(slot, KC, 512)[:, :, 256 * j:256 * j + 256],
                              w[0][bass.ds(e, 1)].rearrange("o (k p) n -> p (o k) n", p=P)).then_inc(sem, 16)
        def load_d(w):
            def load(eng, slot, h, e, sem):
                eng.dma_start(slot_view(slot, 4, D)[:, 2 * h:2 * h + 2, :],
                              w[bass.ds(e, 1)].rearrange("o (k p) n -> p (o k) n", p=P)).then_inc(sem, 16)
            return load
        m1.load_gu, m1.load_d = load_gu1, load_d(A["w_down"][0])

        mc = carver()
        UPAD = TAPS - 1
        uT = mc("uT", [P, KC, UPAD + T])
        convT = mc("convT", [P, KC, T])
        qT = mc("qT", [P, AH, T])
        kT = mc("kT", [P, AH, T])
        v_tm = mc("v_tm", [P, TT, D])
        gc = mc("gc", [P, TT, D])
        pbuf = mc("pbuf", [P, 2, 2, 3 * P])
        dwc = mc("dwc", [P, KC, TAPS])
        cc = mc("cc", [P, 3 * KC])
        cmask = mc("cmask", [P, 3 * P])
        qg = mc("qg", [P, 2, AD])
        subg = mc("subg", [P, 2 * AD])
        lqk = mc("lqk", [P, 4, AD])
        st2 = mc("st2", [P, 128])
        rot = mc("rot", [P, 2, TT, 8])
        lnm = mc("lnm", [P, T])
        aT = adap[:, 0:3 * P]
        ga, q_tm, k_tm, o_tm = hn_tm, scratch, hn_tm, scratch
        drows = kT.rearrange("p a b -> p (a b)")[0:124, 0:2 * P].rearrange("p (a b) -> p a b", a=2)
        crows = kT.rearrange("p a b -> p (a b)")[0:3 * KC, 2 * P:3 * P]
        bcu = uT.rearrange("p a b -> p (a b)")[:, 0:2 * D].rearrange("p (a b) -> p a b", a=2)
        bcn = convT.rearrange("p a b -> p (a b)")
        bcs = qT.rearrange("p a b -> p (a b)")[:, 0:D]
        posi = sb("posi", [P, TT], I32)
        roti = sb("roti", [P, TT * 8], I32)
        invf = sb("invf", [P, 8])

        m2 = moe_buffers("b_", 64, T * 8 // (SLOTS + 1), hrows)
        m2.incs = (16, 16, 32)
        m2.pair_inc = 64
        bc2 = m2.take("bc2", [P, 3, D])
        rw2 = m2.take("rw2", [P, KC, 64])
        rb2 = m2.take("rb2", [P, 64])
        scr = m2.take("scr", [P, TT, 64])
        cho = m2.take("cho", [P, TT, 64])
        chm = m2.take("chm", [P, TT, 64])
        g8 = m2.take("g8", [P, TT, 8, 8])
        g1v = m2.take("g1v", [P, TT, 5, 8])
        shs = m2.take("shs", [P, 2, T])
        shT = m2.take("shT", [P, 2, T])
        out_tm = hn_tm

        def load_gu2(eng, slot, e, sem):
            eng.dma_start(slot_view(slot, KC, 512), A["w_exp_gu_2"][0][bass.ds(e, 1)].rearrange(
                "o (k p) n -> p (o k) n", p=P)).then_inc(sem, 16)
        m2.load_gu, m2.load_d = load_gu2, load_d(A["w_exp_down_2"][0])

        def colblock(w, c0, n):
            return w[:, c0:c0 + n].rearrange("(k p) n -> p k n", p=P)

        w_in = A["w_in"][0]
        slot_total = [0] * RING
        slot_user = [None] * RING
        n_loads = 0
        loads = []

        def slot_view(slot, k, n):
            return ring[:, slot, 0:k * n].rearrange("p (k n) -> p k n", k=k)

        def add_load(src, k, n, by, value):
            nonlocal n_loads
            slot = n_loads % RING
            slot_total[slot] += 16
            loads.append(dict(dst=slot_view(slot, k, n), src=src, slot=slot, free=slot_user[slot], here=slot_total[slot]))
            slot_user[slot] = (by, value)
            n_loads += 1
            return len(loads) - 1

        def add_moe(m):
            nonlocal n_loads
            m.slots = [[(n_loads + 3 * par + r) % RING for r in range(3)] for par in range(2)]
            m.before = [[slot_user[x] for x in row] for row in m.slots]
            m.totals = [[(slot_total[x], m.incs[r]) for r, x in enumerate(row)] for row in m.slots]
            for par in range(2):
                for r, x in enumerate(m.slots[par]):
                    slot_total[x] += m.incs[r] * m.N // 2
                    slot_user[x] = (m.p + "acc", 1)
            n_loads += 3 * m.N

        L_IN = [add_load(colblock(w_in, c * 384, 384), KC, 384, "proj", n)
                for c, n in enumerate((5, 8, 10, 14, 18, 20, 22))]
        L_IN.append(add_load(colblock(w_in, 2696, 512), KC, 512, "proj", 24))
        L_ADA = [add_load(colblock(A["w_ada_2"][0], n * 512, 512), KC, 512, "ada_part", n + 1) for n in range(12)]
        L_OUT = [add_load(colblock(A["w_out"][0], n * 512, 512), KC, 512, "o_proj", 2 * n + 2) for n in range(2)]
        N_MIX = len(loads)
        add_moe(m1)
        L_PLE = [add_load(colblock(A["ple_gate_w"][0], n * 512, 512), KC, 512, "ple_g", 2 * n + 2) for n in range(2)]
        L_PROJ = add_load(A["ple_proj_w"][0].rearrange("(k p) n -> p k n", p=P), 2, D, "ple_p", 4)
        w_in2 = A["w_in_2"][0]
        def cols2(c, by, value):
            return add_load(colblock(w_in2, 512 * c, 512), KC, 512, by, value)
        L_A = [cols2(c, "u_proj", v) for c, v in ((0, 8), (2, 8), (1, 16), (3, 16))]
        L_QKV = [cols2(4 + c, "qkv", 2 * c + 2) for c in range(6)]
        L_G = [cols2(10 + c, "gates2", 2 * c + 2) for c in range(4)]
        L_PW = [add_load(colblock(A["w_pw2_2"][0], n * 512, 512), KC, 512, "pw", 2 * n + 2) for n in range(2)]
        L_O2 = [add_load(colblock(A["w_out_2"][0], n * 512, 512), KC, 512, "o2", 2 * n + 2) for n in range(2)]
        L_SGU = add_load(colblock(A["w_sh_gu_2"][0], 0, 512), KC, 512, "sh_gu", 4)
        L_SD = add_load(A["w_sh_down_2"][0].rearrange("(k p) n -> p k n", p=P), 2, D, "sh_d", 1)
        add_moe(m2)
        NUM = (7, 3)

        def load(sp, i):
            x = loads[i]
            if x["free"]:
                sp.wait_ge(ev(x["free"][0]), x["free"][1])
            sp.dma_start(x["dst"], x["src"]).then_inc(ev(f"w_in{x['slot']}"), 16)

        def codes(pool, m):
            pool.iota(m.code_e, pattern=[[0, 3], [1, m.E]], base=0, channel_multiplier=0, **loose)
            pool.iota(m.code_c, pattern=[[SLOTS, 3], [0, m.E]], base=-3 * SLOTS, channel_multiplier=0,
                      **loose)
            pool.drain().then_inc(ev(m.p + "codes"), 1)

        def norm(act, ready, name):
            if ready:
                act.wait_ge(ev(ready), 1)
            for t in range(TT):
                act.activation(scratch[:, t, :], x_tm[:, t, :], ACT.Square, accum_out=stat[:, t:t + 1])
            act.drain()
            act.activation(stat[:, 2:4], stat[:, 0:2], ACT.Ln, scale=1.0 / D, bias=EPSC)
            act.drain()
            act.activation(stat[:, 4:6], stat[:, 2:4], ACT.Exp, scale=-0.5).then_inc(ev(name), 1)

        def chunks_out(act, name, done, gain=None):
            for c in range(KC):
                act.wait_ge(ev(name), c // 2 + 1)
                kw = {} if gain is None else dict(scale=cols[:, gain + c:gain + c + 1])
                act.activation(hT[:, c, :], ps[:, 4 + c // 2, (c % 2) * T:(c % 2 + 1) * T], ACT.Copy, **kw)
            act.drain().then_inc(ev(done), 1)

        def scale_rows(dve, name, gain=None, out=hn_tm):
            dve.wait_ge(ev(name), 1)
            for t in range(TT):
                if gain is None:
                    dve.tensor_scalar(out[:, t, :], x_tm[:, t, :], stat[:, 4 + t:5 + t], None, ALU.mult)
                else:
                    dve.scalar_tensor_tensor(out[:, t, :], x_tm[:, t, :], stat[:, 4 + t:5 + t], gain, ALU.mult,
                                             ALU.mult)

        def arrived(pe, i):
            pe.wait_ge(ev(f"w_in{loads[i]['slot']}"), loads[i]["here"])

        def transposes(pe, src, bank0, name):
            for c in range(KC):
                for t in range(TT):
                    last = pe.transpose(ps[:, bank0 + c // 2, (c % 2) * T + t * P:(c % 2) * T + (t + 1) * P],
                                        src[:, t, c * P:(c + 1) * P], ident[:])
                if c % 2:
                    last.then_inc(ev(name), 1)

        with nc.Block() as first:
            @first.sync
            def _(sp):
                xv = A["x"][0].rearrange("(t p) d -> p t d", p=P)
                for t in range(TT):
                    sp.dma_start(x_tm[:, t, :], xv[:, t, :]).then_inc(ev("x_in"), 16)

                def rowdma(dst, src):
                    sp.dma_start(dst, src).then_inc(ev("rows_in"), 16)
                rowdma(rows[R_N1:R_N1 + 8, :], A["norm1_g"][0].rearrange("(c p) -> c p", p=P))
                rowdma(rows[R_YG:R_YG + 3, :], A["sb_out_g"][0].rearrange("(c p) -> c p", p=P))
                rowdma(rows[R_YG + 3:R_YG + 6, :], A["mnorm_g"][0].rearrange("(c p) -> c p", p=P))
                rowdma(rows[R_YG + 6:R_YG + 8, :], A["sgu_out_g"][0].rearrange("(c p) -> c p", p=P))
                rowdma(rows[R_PLE:R_PLE + 8, :], A["ple_norm_g"][0].rearrange("(c p) -> c p", p=P))
                rowdma(rows[R_SGB:R_SGB + 4, :], A["sgu_b"][0])
                rowdma(rows[R_C:R_C + 8, :], A["c_2"][0].rearrange("(c p) -> c p", p=P))
                rowdma(rows96[0:32, :], A["conv_w"][0].rearrange("k (j c) -> (k j) c", c=MLD))
                rowdma(rows96[32:40, :], A["conv_b"][0].rearrange("(j c) -> j c", c=MLD))
                sp.dma_start(gate_w[:], colblock(w_in, 2688, 8)).then_inc(ev("gatew_in"), 16)
                sp.dma_start(gate_b[:, 0:1], A["igate_b"].rearrange("a h -> h a")).then_inc(ev("gatew_in"), 16)
                sp.dma_start(gate_b[:, 1:2], A["fgate_b"].rearrange("a h -> h a")).then_inc(ev("gatew_in"), 16)

                for i in range(RING):
                    load(sp, i)
                sp.dma_start(bada[:], A["b_ada_2"][0].rearrange("(n c) -> n c", c=512)).then_inc(ev("bada_in"), 16)
                for i in range(RING, N_MIX):
                    load(sp, i)
                sp.wait_ge(ev("proj_all"), 1)
                sp.wait_ge(ev("h1_ready"), 1)
                sp.dma_start(bc1, A["norm2_g"].to_broadcast([P, D])).then_inc(ev("n2_in"), 16)
                sp.dma_start(rw[:, :, 0:4], A["router_gw"][0].rearrange("(k p) n -> p k n", p=P)).then_inc(ev("rw_in"), 16)
                sp.dma_start(rw[:, :, 4:36], A["router_ew"][0].rearrange("(k p) n -> p k n", p=P)).then_inc(ev("rw_in"), 16)
                sp.dma_start(rb[:, 0:4], A["router_gb"].to_broadcast([P, 4])).then_inc(ev("rw_in"), 16)
                sp.dma_start(rb[:, 4:36], A["router_eb"].to_broadcast([P, 32])).then_inc(ev("rw_in"), 16)
                sp.dma_start(p_tm, A["p"][0, 0].rearrange("(t p) d -> p t d", p=P)).then_inc(ev("p_in"), 16)
                sp.wait_ge(ev("h2_ready"), 1)
                sp.dma_start(hrows.rearrange("(t p) d -> p t d", p=P), hn_tm[:]).then_inc(ev("a_rows"), 16)
                sp.dma_start(bc1, A["final_g"].rearrange("(a d) -> a d", a=1).to_broadcast([P, D])).then_inc(ev("fg_in"), 16)
                moe_sp(sp, m1, ev)
                for i in L_PLE + [L_PROJ]:
                    load(sp, i)
                for i in (L_A + L_QKV)[:RING]:
                    load(sp, i)

            @first.gpsimd
            def _(pool):
                pool.memset(ident[:], 0.0)
                pool.memset(ntri[:], -1.0)
                pool.memset(nones[:], -1.0)
                pool.memset(sel4[:], 0.0)
                pool.memset(selq[:], 0.0)
                pool.memset(eps_c[:], EPS)
                pool.drain()
                pool.affine_select(out=ident[:], in_=ident[:], compare_op=ALU.not_equal, fill=1.0, base=0,
                                   pattern=[[-1, P]], channel_multiplier=1)
                pool.affine_select(out=ntri[:], in_=ntri[:], compare_op=ALU.is_ge, fill=0.0, base=0,
                                   pattern=[[-1, P]], channel_multiplier=1)
                pool.affine_select(out=sel4[:], in_=sel4[:], compare_op=ALU.not_equal, fill=1.0, base=0,
                                   pattern=[[-1, MLH], [0, P]], channel_multiplier=1)
                sq = selq[:].rearrange("p (a c) -> p a c", a=4)
                pool.affine_select(out=selq[:], in_=selq[:], compare_op=ALU.not_equal, fill=1.0, base=0,
                                   pattern=[[0, P]], channel_multiplier=1)
                for j in range(1, 4):
                    pool.drain()
                    pool.affine_select(out=selq[:], in_=selq[:], compare_op=ALU.not_equal, fill=1.0, base=-32 * j,
                                       pattern=[[0, P]], channel_multiplier=1)
                pool.memset(cT[:, :, 0:CONV_K - 1], 0.0)
                pool.memset(vba[:, :, :, MLD:MLD + 1], 1.0)
                pool.memset(ones[:], 1.0)
                pool.memset(zero[:], 0.0)
                pool.memset(off[:], float(OFF))
                pool.iota(iota[:, 0:5 * SLOTS], pattern=[[1, 5 * SLOTS]], base=0, channel_multiplier=0, **loose)
                pool.iota(iota[:, 5 * SLOTS:], pattern=[[1, T]], base=-OFF, channel_multiplier=0, **loose)
                pool.iota(tok[:], pattern=[[P, TT]], base=-OFF, channel_multiplier=1, **loose)
                pool.iota(part1[:], pattern=[[0, 1]], base=1, channel_multiplier=1, **loose)
                pool.drain()
                pool.affine_select(out=tri[:], in_=ones[:, 0:P], compare_op=ALU.is_ge, fill=0.0, base=-1,
                                   pattern=[[1, P]], channel_multiplier=-1)
                pool.drain().then_inc(ev("consts"), 1)

                def keep_causal(buf, strict):
                    blk = buf.rearrange("p (a c) -> p a c", a=3)[:, 0:3:2, :]
                    pool.affine_select(out=blk, in_=blk, compare_op=ALU.is_ge, fill=0.0, base=-1 if strict else 0,
                                       pattern=[[0, 2], [1, P]], channel_multiplier=-1).then_inc(
                                           ev("sb_masked") if strict else ev("ml_masked"), 1)

                def mod_row(n):
                    pool.wait_ge(ev("ada_out"), n + 1)
                    pool.dma_start(mod[:, n * 512:(n + 1) * 512], modst[:]).then_inc(ev("mod_out"), 16)

                for h in range(SBH):
                    pool.wait_ge(ev("sb_softplus"), h + 1)
                    keep_causal(spb[:, h % 2, :], True)
                    mod_row(2 * h)
                    pool.wait_ge(ev("sb_weights"), h + 1)
                    keep_causal(amt[:, h % 2, :], True)
                    mod_row(2 * h + 1)
                for h in range(MLH):
                    pool.wait_ge(ev("ml_decay"), h + 1)
                    keep_causal(dmt[:, h % 2, :], False)
                pool.wait_ge(ev("h1_ready"), 1)
                codes(pool, m1)
                moe_pool(pool, m1, ev)

            @first.scalar
            def _(act):
                act.wait_ge(ev("consts"), 1)
                act.wait_ge(ev("x_in"), 32)
                for t in range(TT):
                    act.activation(scratch[:, t, :], x_tm[:, t, :], ACT.Square, accum_out=stat[:, t:t + 1])
                act.drain()
                act.activation(stat[:, 2:4], stat[:, 0:2], ACT.Ln, scale=1.0 / D, bias=EPSC)
                act.drain()
                act.activation(stat[:, 4:6], stat[:, 2:4], ACT.Exp, scale=-0.5).then_inc(ev("rstd1"), 1)
                act.wait_ge(ev("rows_T"), 1)
                act.copy(cols[:], ps[:, 7, 0:N_ROWS])
                act.copy(cols96[:], ps[0:MLD, 7, 64:104])
                act.drain().then_inc(ev("cols_ready"), 1)
                for c in range(KC):
                    act.wait_ge(ev("h_T"), c // 2 + 1)
                    act.activation(hT[:, c, :], ps[:, c // 2, (c % 2) * T:(c % 2 + 1) * T], ACT.Copy,
                                   scale=cols[:, R_N1 + c:R_N1 + c + 1])
                act.drain().then_inc(ev("hT_ready"), 1)
                act.activation(stat[:, 16:24], cols[:, R_C:R_C + 8], ACT.Exp, scale=-1.0).then_inc(ev("c_exp"), 1)

                g = 0
                def take(dst, view, func=ACT.Copy, **kw):
                    nonlocal g
                    act.wait_ge(ev("proj"), g + 1)
                    act.activation(dst, view(ps[:, g % 4, :]), func, **kw).then_inc(ev("proj_evac"), 1)
                    g += 1
                for j in range(2):
                    take(gT[:, j, :], lambda b: b[0:MLH, 0:T], ACT.Identity, bias=gate_b[:, j:j + 1])
                for c in range(3):
                    take(qaT[:, c, :], lambda b: b[:, 0:T], ACT.Copy, scale=SBD ** -0.5)
                for c in range(3):
                    take(kaT[:, c, :], lambda b: b[:, 0:T])
                for t in range(TT):
                    take(va[:, t, :], lambda b: b[:, 0:SBW])
                for j in range(2 * MLH):
                    take(cT[:, j, CONV_K - 1:], lambda b: b[0:MLD, 0:T])
                for t in range(TT):
                    take(vba[:, t, :, 0:MLD], lambda b: b[:, 0:MLW].rearrange("p (h d) -> p h d", h=MLH))
                for t in range(TT):
                    take(ob[:, t, :], lambda b: b[:, 0:MLW], ACT.Exp, scale=-1.0)
                for t in range(TT):
                    take(uv[:, t, :, :].rearrange("p a c -> p (a c)"), lambda b: b[:, :], ACT.Gelu_apprx_tanh)
                act.drain().then_inc(ev("proj_all"), 1)

                act.wait_ge(ev("conv"), 1)
                act.activation(sg8, qkT, ACT.Exp, scale=-1.0).then_inc(ev("conv_exp"), 1)
                act.dma_start(sgw, A["sgu_w"][0].rearrange("g t s -> t g s")).then_inc(ev("sgu_in"), 16)
                act.dma_start(lnb[:, 0, :], A["sgu_ln_g"].to_broadcast([P, SGW])).then_inc(ev("sgu_in"), 16)
                act.dma_start(lnb[:, 1, :], A["sgu_ln_b"].to_broadcast([P, SGW])).then_inc(ev("sgu_in"), 16)
                act.activation(gT[:, 2, :], gT[:, 1, :], ACT.Abs)
                act.drain()
                act.activation(gT[:, 3, :], gT[:, 2, :], ACT.Exp, scale=-1.0)
                act.drain()
                act.activation(gT[:, 4, :], gT[:, 3, :], ACT.Ln, bias=1.0).then_inc(ev("f_ln"), 1)
                act.wait_ge(ev("g_scan"), 1)
                act.activation(gT[:, 6, :], gT[:, 6, :], ACT.Exp).then_inc(ev("g_exp"), 1)
                act.wait_ge(ev("g_T"), 1)
                act.copy(gcol, ps[:, 3, 0:16].rearrange("p (t c) -> p t c", t=TT)).then_inc(ev("gcol_ready"), 1)

                def ada(n):
                    act.wait_ge(ev("ada_part"), n + 1)
                    if n >= 1:
                        act.wait_ge(ev("ada_bc"), n)
                    act.copy(adap[:], ps[:, 2, :]).then_inc(ev("ada_row"), 1)
                for h in range(SBH):
                    zb = ps[:, 4 + h % 2, 0:3 * P]
                    act.wait_ge(ev("sb_z"), h + 1)
                    if h >= 2:
                        act.wait_ge(ev("sb_softplus"), h - 1)
                    act.activation(spt[:, h % 2, :], zb, ACT.Abs)
                    act.drain()
                    act.activation(spt[:, h % 2, :], spt[:, h % 2, :], ACT.Exp, scale=-1.0)
                    act.drain()
                    act.activation(spt[:, h % 2, :], spt[:, h % 2, :], ACT.Ln, bias=1.0).then_inc(ev("sb_ln"), 1)
                    ada(2 * h)
                    act.wait_ge(ev("sb_r"), h + 1)
                    if h >= 2:
                        act.wait_ge(ev("sb_y"), h - 1)
                    act.activation(amt[:, h % 2, :], zb, ACT.Exp).then_inc(ev("sb_weights"), 1)
                    ada(2 * h + 1)
                def rstd(n, ready, name, width):
                    act.wait_ge(ev(ready), 1)
                    act.activation(stat[:, 24:24 + n], stat[:, 24:24 + n], ACT.Ln, scale=1.0 / width, bias=EPSC)
                    act.drain()
                    act.activation(stat[:, 24:24 + n], stat[:, 24:24 + n], ACT.Exp, scale=-0.5).then_inc(ev(name), 1)
                for h in range(MLH):
                    if h == 2:
                        rstd(8, "sgu_var", "sgu_rstd", SGD)
                    act.wait_ge(ev("ml_m"), h // 2 + 1)
                    if h >= 2:
                        act.wait_ge(ev("ml_p"), h - 1)
                    bb = ps[:, 6, (h % 2) * T:(h % 2 + 1) * T]
                    act.activation(dmt[:, h % 2, 0:T], bb, ACT.Exp, bias=gcol[:, 0, h:h + 1])
                    act.activation(dmt[:, h % 2, T:T + P], bb[:, P:T], ACT.Exp, bias=gcol[:, 1, h:h + 1])
                    act.drain().then_inc(ev("ml_decay"), 1)
                rstd(2, "yc_ss", "yc_rstd", SGW)
                rstd(2, "ya_ss", "ya_rstd", SBW)
                rstd(8, "yb_ss", "yb_rstd", MLD)
                for c in range(KC):
                    act.wait_ge(ev("y_T"), c // 2 + 1)
                    act.activation(hT[:, c, :], ps[:, 4 + c // 2, (c % 2) * T:(c % 2 + 1) * T], ACT.Copy,
                                   scale=cols[:, R_YG + c:R_YG + c + 1])
                act.drain().then_inc(ev("yT_ready"), 1)



                norm(act, "h1_ready", "rstd2")
                chunks_out(act, "h2_T", "h2T_ready")
                act.wait_ge(ev("g_shift"), 1)
                for t in range(TT):
                    act.activation(gr[:, t, :], gl[:, t, :], ACT.Exp, accum_out=stat[:, 16 + t:17 + t])
                act.drain().then_inc(ev("g_expd"), 1)
                act.wait_ge(ev("e_shift"), 1)
                act.activation(er, er, ACT.Exp).then_inc(ev("e_expd"), 1)
                moe_act(act, m1, ev, ps)
                norm(act, "h3_ready", "rstd3")
                chunks_out(act, "h3_T", "h3T_ready", R_PLE)
                act.wait_ge(ev("p_T"), 1)
                act.copy(pT.rearrange("p a b -> p (a b)"), ps[:, 0, :]).then_inc(ev("pT_ready"), 1)
                for n in range(2):
                    for t in range(TT):
                        act.wait_ge(ev("ple_g"), 2 * n + t + 1)
                        act.activation(scratch[:, t, n * 512:(n + 1) * 512], ps[:, 4 + 2 * n + t, :], ACT.Sigmoid).then_inc(
                            ev("ple_sig"), 1)
                norm(act, "h4_ready", "rstd4")

            @first.vector
            def _(dve):
                def bc(ap, shape):
                    return ap.to_broadcast(shape)
                dve.wait_ge(ev("rstd1"), 1)
                dve.memset(gT[:, 7, :], 1.0)
                for t in range(TT):
                    dve.tensor_scalar(hn_tm[:, t, :], x_tm[:, t, :], stat[:, 4 + t:5 + t], None,
                                      ALU.mult).then_inc(ev("hn1"), 1)
                dve.wait_ge(ev("c_exp"), 1)
                dve.tensor_scalar_add(stat[:, 16:24], stat[:, 16:24], 1.0)
                dve.drain()
                dve.reciprocal(stat[:, 16:24], stat[:, 16:24])
                dve.drain()
                dve.tensor_tensor(cact[:], cols[:, R_C:R_C + 8], stat[:, 16:24], ALU.mult)
                dve.drain()
                dve.tensor_copy(crep[:], cact[:].unsqueeze(2).to_broadcast([P, KC, 32])).then_inc(ev("crep_ready"), 1)

                dve.wait_ge(ev("proj_evac"), 2 + 3 + 3 + 2 + 8)
                for j in range(2 * MLH):
                    dve.tensor_scalar(qkT[:, j, :], cT[:, j, 0:T], cols96[:, j:j + 1], cols96[:, 32 + j:33 + j],
                                      ALU.mult, ALU.add)
                for k in range(1, CONV_K):
                    dve.drain()
                    for j in range(2 * MLH):
                        last = dve.scalar_tensor_tensor(qkT[:, j, :], cT[:, j, k:k + T], cols96[:, 8 * k + j:8 * k + j + 1],
                                                        qkT[:, j, :], ALU.mult, ALU.add)
                last.then_inc(ev("conv"), 1)
                dve.wait_ge(ev("conv_exp"), 1)
                dve.tensor_scalar_add(sg8, sg8, 1.0)
                dve.drain()
                dve.reciprocal(sg8, sg8)
                dve.drain()
                dve.tensor_tensor(qkT, qkT, sg8, ALU.mult).then_inc(ev("qk_ready"), 1)
                dve.wait_ge(ev("f_ln"), 1)
                dve.scalar_tensor_tensor(gT[:, 1, :], gT[:, 1, :], 0.0, gT[:, 4, :], ALU.min, ALU.subtract)
                dve.drain()
                dve.tensor_tensor_scan(gT[:, 2, :], gT[:, 7, :], gT[:, 1, :], 0.0, ALU.mult, ALU.add)
                dve.drain()
                dve.tensor_tensor(gT[:, 3, :], gT[:, 0, :], gT[:, 2, :], ALU.subtract)
                dve.drain()
                dve.tensor_tensor_scan(gT[:, 4, :], gT[:, 3, :], gT[:, 3, :], 0.0, ALU.max, ALU.max)
                dve.drain()
                dve.tensor_scalar(gT[:, 5, :], gT[:, 4, :], -1.0, None, ALU.mult)
                dve.drain()
                dve.tensor_tensor(gT[:, 6, :], gT[:, 5, :], gT[:, 2, :], ALU.subtract).then_inc(ev("g_scan"), 1)

                def ada(n):
                    dve.wait_ge(ev("ada_bc"), n + 1)
                    if n:
                        dve.wait_ge(ev("mod_out"), 16 * n)
                    dve.tensor_copy(modst[:], ps[0:1, 3, :]).then_inc(ev("ada_out"), 1)
                for h in range(SBH):
                    dve.wait_ge(ev("sb_ln"), h + 1)
                    if h >= 2:
                        dve.wait_ge(ev("sb_r"), h - 1)
                    dve.scalar_tensor_tensor(spb[:, h % 2, :], ps[:, 4 + h % 2, 0:3 * P], 0.0, spt[:, h % 2, :],
                                             ALU.max, ALU.add).then_inc(ev("sb_softplus"), 1)
                    ada(2 * h)
                    ada(2 * h + 1)

                dve.wait_ge(ev("proj_all"), 1)
                dve.wait_ge(ev("sgu_in"), 48)
                v4 = uv[:, :, 1, :].rearrange("p t (g c) -> p t g c", g=SGG)
                mean = stat[:, 32:40].rearrange("p (t g) -> p t g", t=TT)
                var = stat[:, 24:32].rearrange("p (t g) -> p t g", t=TT)
                sq = hn_tm[:, 0, 0:TT * SGW].rearrange("p (t g c) -> p t g c", t=TT, g=SGG)
                full = [P, TT, SGG, SGD]
                dve.tensor_reduce(mean, v4, AX.X, ALU.add)
                dve.drain()
                dve.tensor_scalar(mean, mean, 1.0 / SGD, None, ALU.mult)
                dve.drain()
                dve.tensor_tensor(v4, v4, mean.unsqueeze(3).to_broadcast(full), ALU.subtract)
                dve.drain()
                dve.tensor_tensor(sq, v4, v4, ALU.mult)
                dve.drain()
                dve.tensor_reduce(var, sq, AX.X, ALU.add).then_inc(ev("sgu_var"), 1)
                dve.wait_ge(ev("sgu_rstd"), 1)
                dve.tensor_tensor(v4, v4, var.unsqueeze(3).to_broadcast(full), ALU.mult)
                v3 = uv[:, :, 1, :]
                dve.drain()
                dve.tensor_tensor(v3, v3, lnb[:, 0:1, :].to_broadcast([P, TT, SGW]), ALU.mult)
                dve.drain()
                dve.tensor_tensor(v3, v3, lnb[:, 1:2, :].to_broadcast([P, TT, SGW]), ALU.add).then_inc(ev("sgu_v"), 1)
                dve.wait_ge(ev("sgw_T"), 1)
                dve.tensor_copy(sgwT.rearrange("p g t -> p (g t)"), ps[:, 3, :])
                dve.drain()
                dve.memset(sgwT[64:P, :, 0:64], 0.0).then_inc(ev("sgw_ready"), 1)

                for h in range(MLH):
                    dve.wait_ge(ev("ml_s"), h + 1)
                    dve.wait_ge(ev("ml_masked"), h + 1)
                    if h >= 2:
                        dve.wait_ge(ev("ml_y"), h - 1)
                    dve.scalar_tensor_tensor(spb[:, h % 2, :], ps[:, 4 + h % 2, 0:3 * P], MLD ** -0.5,
                                             dmt[:, h % 2, :], ALU.mult, ALU.mult).then_inc(ev("ml_p"), 1)

                def sumsq(dst, src, junk, shape3):
                    dve.tensor_tensor(junk, src, src, ALU.mult)
                    dve.drain()
                    return dve.tensor_reduce(dst, junk, AX.X, ALU.add)

                dve.wait_ge(ev("sgu_mix"), 1)
                mixed = ps[:, 2, :].rearrange("p (t g c) -> p t g c", t=TT, g=SGG)
                bcol = cols[:, R_SGB:R_SGB + SGG].unsqueeze(1).unsqueeze(3).to_broadcast(full)
                yc = hn_tm[:, :, SBW + MLW:D]
                yc4 = yc.rearrange("p t (g c) -> p t g c", g=SGG)
                for t in range(TT):
                    dve.tensor_tensor(sq[:, t], mixed[:, t], bcol[:, t], ALU.add)
                dve.drain()
                dve.tensor_tensor(yc, uv[:, :, 0, :], sq.rearrange("p t g c -> p t (g c)"), ALU.mult)
                dve.drain()
                sumsq(stat[:, 24:26], yc, hn_tm[:, :, 0:SGW], None).then_inc(ev("yc_ss"), 1)
                dve.wait_ge(ev("yc_rstd"), 1)
                for t in range(TT):
                    dve.tensor_scalar(yc[:, t, :], yc[:, t, :], stat[:, 24 + t:25 + t], None, ALU.mult)
                dve.drain()
                dve.wait_ge(ev("sb_y"), SBH)
                ya = hn_tm[:, :, 0:SBW]
                for t in range(TT):
                    dve.tensor_copy(ya[:, t, :], ps[:, t, 0:SBW])
                dve.drain()
                sumsq(stat[:, 24:26], ya, hn_tm[:, :, SBW:SBW + MLW], None).then_inc(ev("ya_ss"), 1)
                dve.wait_ge(ev("ya_rstd"), 1)
                for t in range(TT):
                    dve.tensor_scalar(ya[:, t, :], ya[:, t, :], stat[:, 24 + t:25 + t], None, ALU.mult)
                dve.drain().then_inc(ev("ya_done"), 1)
                dve.wait_ge(ev("ml_y"), MLH)
                hb = hn_tm[:, :, SBW:SBW + MLW].rearrange("p t (h d) -> p t h d", h=MLH)
                den = stat[:, 40:48].rearrange("p (t h) -> p t h", t=TT)
                num = [ps[:, NUM[t], 0:MLH * (MLD + 1)].rearrange("p (h d) -> p h d", h=MLH) for t in range(TT)]
                for t in range(TT):
                    dve.tensor_copy(den[:, t, :], num[t][:, :, MLD])
                dve.drain()
                dve.scalar_tensor_tensor(den, den, -1.0, den, ALU.mult, ALU.max)
                dve.drain()
                dve.tensor_tensor(den, den, gcol[:, :, MLH:2 * MLH], ALU.max)
                dve.drain()
                dve.reciprocal(stat[:, 40:48], stat[:, 40:48])
                dve.drain()
                for t in range(TT):
                    dve.tensor_tensor(hb[:, t], num[t][:, :, 0:MLD], den[:, t, :].unsqueeze(2).to_broadcast([P, MLH, MLD]),
                                      ALU.mult)
                dve.drain()
                for t in range(TT):
                    dve.tensor_tensor(scratch[:, t, 0:MLW], hn_tm[:, t, SBW:SBW + MLW], hn_tm[:, t, SBW:SBW + MLW], ALU.mult)
                dve.drain()
                for t in range(TT):
                    dve.tensor_reduce(stat[:, 24 + 4 * t:28 + 4 * t],
                                      scratch[:, t, 0:MLW].rearrange("p (h d) -> p h d", h=MLH), AX.X, ALU.add)
                dve.tensor_scalar_add(ob, ob, 1.0)
                dve.drain().then_inc(ev("yb_ss"), 1)
                dve.reciprocal(ob, ob)
                dve.wait_ge(ev("yb_rstd"), 1)
                for t in range(TT):
                    dve.tensor_tensor(hb[:, t], hb[:, t],
                                      stat[:, 24 + 4 * t:28 + 4 * t].unsqueeze(2).to_broadcast([P, MLH, MLD]), ALU.mult)
                dve.drain()
                dve.tensor_tensor(hn_tm[:, :, SBW:SBW + MLW], hn_tm[:, :, SBW:SBW + MLW], ob, ALU.mult)
                dve.drain().then_inc(ev("y_ready"), 1)
                for t in range(TT):
                    for n in range(2):
                        dve.wait_ge(ev("o_proj"), 2 * n + t + 1)
                        dve.tensor_tensor(x_tm[:, t, n * 512:(n + 1) * 512], ps[:, 2 * n + t, :],
                                          x_tm[:, t, n * 512:(n + 1) * 512], ALU.add)
                dve.drain().then_inc(ev("h1_ready"), 1)

                dve.wait_ge(ev("n2_in"), 16)
                scale_rows(dve, "rstd2", bc1)
                dve.drain().then_inc(ev("h2_ready"), 1)
                dve.memset(gl[:, :, 4:8], -BIG)
                dve.memset(gv, FAR)
                dve.wait_ge(ev("rw_in"), 64)
                for t in range(TT):
                    dve.wait_ge(ev("router"), t + 1)
                    dve.tensor_tensor(gl[:, t, 0:4], ps[:, 4 + t, 0:4], rb[:, 0:4], ALU.add)
                    dve.tensor_tensor(el[:, t, :], ps[:, 4 + t, 4:36], rb[:, 4:36], ALU.add)
                dve.drain()
                for t in range(TT):
                    dve.max(v8[:, t, :], gl[:, t, :])
                dve.drain()
                dve.tensor_copy(gv[:, :, 0:1], v8[:, :, 0:1])
                dve.drain()
                for t in range(TT):
                    dve.match_replace(gr[:, t, :], gv[:, t, :], gl[:, t, :], -FAR)
                dve.drain()
                dve.tensor_tensor(gm, gr[:, :, 0:4], gl[:, :, 0:4], ALU.not_equal)
                dve.drain()
                dve.tensor_tensor(gl, gl, v8[:, :, 0:1].to_broadcast([P, TT, 8]), ALU.subtract)
                dve.tensor_scalar(gm, gm, BIG, -BIG, ALU.mult, ALU.add)
                dve.drain().then_inc(ev("g_shift"), 1)
                e4 = el.rearrange("p t (g e) -> p t g e", g=4)
                for t in range(TT):
                    dve.tensor_tensor(e4[:, t], e4[:, t], gm[:, t, :].unsqueeze(2).to_broadcast([P, 4, 8]), ALU.add)
                dve.drain()
                for t in range(TT):
                    dve.max(v8[:, t, :], el[:, t, :])
                dve.drain()
                dve.tensor_copy(gv[:, :, 0:2], v8[:, :, 0:2])
                dve.drain()
                for t in range(TT):
                    dve.match_replace(er[:, t, :], gv[:, t, :], el[:, t, :], -FAR)
                dve.drain()
                dve.tensor_tensor(m1.mask, er, el, ALU.not_equal)
                dve.drain()
                dve.tensor_tensor(er, el, v8[:, :, 0:1].to_broadcast([P, TT, 32]), ALU.subtract).then_inc(ev("e_shift"), 1)
                dve.wait_ge(ev("e_expd"), 1)
                dve.wait_ge(ev("g_expd"), 1)
                dve.tensor_tensor(m1.gate, er, m1.mask, ALU.mult)
                dve.drain()
                dve.tensor_reduce(stat[:, 18:20], m1.gate, AX.X, ALU.add)
                dve.drain()
                dve.tensor_tensor(stat[:, 18:20], stat[:, 18:20], stat[:, 16:18], ALU.mult)
                dve.drain()
                dve.reciprocal(stat[:, 18:20], stat[:, 18:20])
                dve.drain()
                for t in range(TT):
                    dve.tensor_scalar(m1.gate[:, t, :], m1.gate[:, t, :], stat[:, 18 + t:19 + t], None, ALU.mult)
                dve.wait_ge(ev("a_codes"), 1)
                route_lists_dve(dve, m1, ev, ps)
                moe_dve(dve, m1, ev, ps)
                dve.wait_ge(ev("a_acc"), 1)
                for t in range(TT):
                    for n in range(2):
                        xx = x_tm[:, t, n * 512:(n + 1) * 512]
                        dve.tensor_tensor(xx, ps[:, 2 * t + n, :], xx, ALU.add)
                dve.drain().then_inc(ev("h3_ready"), 1)
                scale_rows(dve, "rstd3")
                dve.drain().then_inc(ev("hn3_ready"), 1)
                for n in range(2):
                    for t in range(TT):
                        dve.wait_ge(ev("ple_sig"), 2 * n + t + 1)
                        dve.wait_ge(ev("ple_p"), 2 * n + t + 1)
                        g, xx = scratch[:, t, n * 512:(n + 1) * 512], x_tm[:, t, n * 512:(n + 1) * 512]
                        dve.tensor_tensor(g, ps[:, 2 * n + t, :], g, ALU.mult)
                        dve.drain()
                        dve.tensor_tensor(xx, xx, g, ALU.add)
                dve.drain().then_inc(ev("h4_ready"), 1)
                dve.wait_ge(ev("fg_in"), 16)
                scale_rows(dve, "rstd4", bc1, x_tm)
                dve.drain().then_inc(ev("x1_ready"), 1)

            @first.tensor
            def _(pe):
                used = 0
                pe.wait_ge(ev("consts"), 1)
                pe.wait_ge(ev("rows_in"), 16 * 9)
                pe.transpose(ps[:, 7, 0:N_ROWS], rows[:], ident[0:N_ROWS, 0:N_ROWS])
                pe.transpose(ps[0:MLD, 7, 64:104], rows96[:], ident[0:40, 0:40]).then_inc(ev("rows_T"), 1)

                pe.wait_ge(ev("hn1"), 2)
                transposes(pe, hn_tm, 0, "h_T")
                pe.wait_ge(ev("hT_ready"), 1)

                g = 0
                def group(m, n, lhs, rhs):
                    nonlocal g
                    if g >= 4:
                        pe.wait_ge(ev("proj_evac"), g - 3)
                    for k in range(KC):
                        last = pe.matmul(ps[0:m, g % 4, 0:n], lhs(k), rhs(k), start=(k == 0), stop=(k == KC - 1))
                    last.then_inc(ev("proj"), 1)
                    g += 1
                    return last
                pe.wait_ge(ev("gatew_in"), 48)
                for j in range(2):
                    group(MLH, T, lambda k: gate_w[:, k, j * MLH:(j + 1) * MLH], lambda k: hT[:, k, :])
                for i, (kind, m) in enumerate([("T", P), ("T", P), ("tok", 0), ("T", MLD), ("T", MLD), ("tok", 0), ("tok", 0),
                                               ("tok", 0)]):
                    w = loads[L_IN[i]]["dst"]
                    arrived(pe, L_IN[i])
                    if kind == "T":
                        for c in range(384 // m):
                            last = group(m, T, lambda k: w[:, k, c * m:(c + 1) * m], lambda k: hT[:, k, :])
                    else:
                        n = w.shape[2]
                        for t in range(TT):
                            last = group(P, n, lambda k: hT[:, k, t * P:(t + 1) * P], lambda k: w[:, k, :])

                pe.wait_ge(ev("proj_all"), 1)
                pe.wait_ge(ev("g_exp"), 1)
                for t in range(TT):
                    for j, r in enumerate((3, 6)):
                        last = pe.transpose(ps[:, 3, 8 * t + MLH * j:8 * t + MLH * (j + 1)], gT[:, r, t * P:(t + 1) * P],
                                            ident[0:MLH, 0:MLH])
                last.then_inc(ev("g_T"), 1)
                pe.wait_ge(ev("gcol_ready"), 1)
                pe.wait_ge(ev("crep_ready"), 1)
                pe.wait_ge(ev("bada_in"), 16)

                def ada(n):
                    w = loads[L_ADA[n]]["dst"]
                    arrived(pe, L_ADA[n])
                    if n >= 1:
                        pe.wait_ge(ev("ada_row"), n)
                    for k in range(2):
                        for j in range(4):
                            last = pe.matmul(ps[32 * j:32 * j + 32, 2, :], crep[:, 2 * j + k, :], w[:, 2 * j + k, :],
                                      start=(k == 0), stop=(k == 1))
                    last.then_inc(ev("ada_part"), 1)
                    pe.wait_ge(ev("ada_row"), n + 1)
                    if n >= 1:
                        pe.wait_ge(ev("ada_out"), n)
                    pe.matmul(ps[0:1, 3, :], selq[:, 0:1], adap[:], start=True, stop=False)
                    pe.matmul(ps[0:1, 3, :], ident[0:12, n:n + 1], bada[:], start=False, stop=True).then_inc(ev("ada_bc"), 1)

                def sb_z(h):
                    b, c = SBD * (h % 2), h // 2
                    bank = ps[:, 4 + h % 2, :]
                    if h >= 2:
                        pe.wait_ge(ev("sb_weights"), h - 1)
                    kk, qq = kaT[b:b + SBD, c, :], qaT[b:b + SBD, c, :]
                    pe.matmul(bank[:, 0:T], kk[:, 0:P], qq, start=True, stop=True)
                    pe.matmul(bank[:, T:T + P], kk[:, P:T], qq[:, P:T], start=False, stop=True,
                              skip_group_check=True).then_inc(ev("sb_z"), 1)
                def sb_r(h):
                    pe.wait_ge(ev("sb_masked"), 2 * h + 1)
                    bank, s = ps[:, 4 + h % 2, :], spb[:, h % 2, :]
                    kw = dict(start=False, stop=True, skip_group_check=True)
                    pe.matmul(bank[:, 0:T], ntri[:], s[:, 0:T], **kw)
                    pe.matmul(bank[:, P:T], nones[:], s[:, T:T + P], **kw)
                    pe.matmul(bank[:, T:T + P], ntri[:], s[:, T:T + P], **kw).then_inc(ev("sb_r"), 1)
                def sb_y(h):
                    pe.wait_ge(ev("sb_masked"), 2 * h + 2)
                    a = amt[:, h % 2, :]
                    o = slice(h * SBD, (h + 1) * SBD)
                    pe.matmul(ps[:, 0, o], a[:, 0:P], va[:, 0, o], start=True, stop=True)
                    pe.matmul(ps[:, 1, o], a[:, P:T], va[:, 0, o], start=True, stop=False)
                    pe.matmul(ps[:, 1, o], a[:, T:T + P], va[:, 1, o], start=False, stop=True).then_inc(ev("sb_y"), 1)
                sb_z(0)
                for h in range(SBH):
                    if h + 1 < SBH:
                        sb_z(h + 1)
                    ada(2 * h)
                    sb_r(h)
                    ada(2 * h + 1)
                    sb_y(h)

                pe.wait_ge(ev("sgu_in"), 48)
                pe.wait_ge(ev("ada_out"), 12)
                for gg in range(SGG):
                    last = pe.transpose(ps[:, 3, gg * P:(gg + 1) * P], sgw[:, gg, :], ident[:])
                last.then_inc(ev("sgw_T"), 1)
                pe.wait_ge(ev("qk_ready"), 1)
                def ml_m(pair):
                    if pair:
                        pe.wait_ge(ev("ml_decay"), 2)
                    for h in (2 * pair, 2 * pair + 1):
                        last = pe.matmul(ps[:, 6, (h % 2) * T:(h % 2 + 1) * T], sel4[:, h, :], gT[:, 5, :],
                                         start=True, stop=True)
                    last.then_inc(ev("ml_m"), 1)
                def ml_s(h):
                    bank = ps[:, 4 + h % 2, :]
                    if h < 2:
                        pe.wait_ge(ev("sb_weights"), SBH)
                    else:
                        pe.wait_ge(ev("ml_p"), h - 1)
                    kk, qq = qkT[:, MLH + h, :], qkT[:, h, :]
                    pe.matmul(bank[:, 0:T], kk[:, 0:P], qq, start=True, stop=True)
                    pe.matmul(bank[:, T:T + P], kk[:, P:T], qq[:, P:T], start=False, stop=True,
                              skip_group_check=True).then_inc(ev("ml_s"), 1)
                ml_m(0)
                for h in range(2):
                    ml_s(h)
                pe.wait_ge(ev("sgw_ready"), 1)
                pe.wait_ge(ev("sgu_v"), 1)
                for t in range(TT):
                    for gg in range(SGG):
                        c = t * SGW + gg * SGD
                        last = pe.matmul(ps[:, 2, c:c + SGD], sgwT[:, gg, :], uv[:, t, 1, gg * SGD:(gg + 1) * SGD],
                                         start=True, stop=True)
                last.then_inc(ev("sgu_mix"), 1)
                def ml_y(h):
                    a = spb[:, h % 2, :]
                    o = slice(h * (MLD + 1), (h + 1) * (MLD + 1))
                    pe.wait_ge(ev("ml_p"), h + 1)
                    pe.matmul(ps[:, NUM[0], o], a[:, 0:P], vba[:, 0, h, :], start=True, stop=True)
                    pe.matmul(ps[:, NUM[1], o], a[:, P:T], vba[:, 0, h, :], start=True, stop=False)
                    pe.matmul(ps[:, NUM[1], o], a[:, T:T + P], vba[:, 1, h, :], start=False, stop=True).then_inc(ev("ml_y"), 1)
                for h in range(MLH):
                    ml_y(h)
                    if h == 0:
                        ml_m(1)
                    if h + 2 < MLH:
                        ml_s(h + 2)
                pe.wait_ge(ev("y_ready"), 1)
                transposes(pe, hn_tm, 4, "y_T")
                pe.wait_ge(ev("yT_ready"), 1)
                for n in range(2):
                    w = loads[L_OUT[n]]["dst"]
                    arrived(pe, L_OUT[n])
                    for t in range(TT):
                        for k in range(KC):
                            last = pe.matmul(ps[:, 2 * n + t, :], hT[:, k, t * P:(t + 1) * P], w[:, k, :],
                                             start=(k == 0), stop=(k == KC - 1))
                        last.then_inc(ev("o_proj"), 1)

                pe.wait_ge(ev("h2_ready"), 1)
                transposes(pe, hn_tm, 4, "h2_T")
                pe.wait_ge(ev("h2T_ready"), 1)
                pe.wait_ge(ev("rw_in"), 64)
                for t in range(TT):
                    for k in range(KC):
                        last = pe.matmul(ps[:, 4 + t, 0:36], hT[:, k, t * P:(t + 1) * P], rw[:, k, :], start=(k == 0),
                                         stop=(k == KC - 1))
                    last.then_inc(ev("router"), 1)
                for b in range(4):
                    pe.matmul(ps[:, b, :], zero[:], hn_tm[:, 0, 0:512], start=True, stop=True)
                route_lists_pe(pe, m1, ev, ps)
                moe_pe(pe, m1, ev, ps)
                pe.wait_ge(ev("hn3_ready"), 1)
                pe.wait_ge(ev("p_in"), 16)
                for c in range(2):
                    for t in range(TT):
                        last = pe.transpose(ps[:, 0, c * T + t * P:c * T + (t + 1) * P], p_tm[:, t, c * P:(c + 1) * P], ident[:])
                last.then_inc(ev("p_T"), 1)
                transposes(pe, hn_tm, 4, "h3_T")
                pe.wait_ge(ev("h3T_ready"), 1)
                pe.wait_ge(ev("pT_ready"), 1)
                for n in range(2):
                    arrived(pe, L_PLE[n])
                    w = loads[L_PLE[n]]["dst"]
                    for t in range(TT):
                        for k in range(KC):
                            last = pe.matmul(ps[:, 4 + 2 * n + t, :], hT[:, k, t * P:(t + 1) * P], w[:, k, :], start=(k == 0),
                                             stop=(k == KC - 1))
                        last.then_inc(ev("ple_g"), 1)
                arrived(pe, L_PROJ)
                w = loads[L_PROJ]["dst"]
                for n in range(2):
                    for t in range(TT):
                        for k in range(2):
                            last = pe.matmul(ps[:, 2 * n + t, :], pT[:, k, t * P:(t + 1) * P], w[:, k, n * 512:(n + 1) * 512],
                                             start=(k == 0), stop=(k == 1))
                        last.then_inc(ev("ple_p"), 1)

        renew()
        nc.all_engine_barrier()

        with nc.Block() as second:
            @second.sync
            def _(sp):
                def small(dst, src, name="c2_in"):
                    sp.dma_start(dst, src).then_inc(ev(name), 16)
                def vec(v, n=D):
                    return v.to_broadcast([P, n])
                small(bcn[:, 0:D], vec(A["norm1_g_2"]), "n3_in")
                small(bcn[:, D:2 * D], vec(mod[:, D:2 * D]), "n3_in")
                small(bcs, vec(mod[:, 0:D]), "n3_in")
                dw = A["conv_dw_2"][0].rearrange("k (c p) -> (k c) p", p=P)
                for j in range(2):
                    small(drows[:, j, :], dw[124 * j:124 * j + 124, :])
                for j, nm in enumerate(("conv_dw_b_2", "conv_ln_g_2", "conv_ln_b_2")):
                    small(crows[KC * j:KC * j + KC, :], A[nm][0].rearrange("(c p) -> c p", p=P))
                small(qg[:, 0, :], vec(A["q_norm_g_2"], AD))
                small(qg[:, 1, :], vec(A["k_norm_g_2"], AD))
                small(subg, vec(A["subln_g_2"], 2 * AD))
                for j, nm in enumerate(("lambda_q1_2", "lambda_k1_2", "lambda_q2_2", "lambda_k2_2")):
                    small(lqk[:, j, :], vec(A[nm], AD))
                for t in range(TT):
                    small(posi[:, t:t + 1], A["positions_2"][0, t * P:(t + 1) * P].rearrange("(p a) -> p a", a=1))
                for i in (L_A + L_QKV)[RING:]:
                    load(sp, i)
                sp.wait_ge(ev("conv2"), KC)
                sp.dma_start(bcu[:, 0, :], vec(A["b_pw2_2"])).then_inc(ev("bcu_in"), 16)
                sp.dma_start(bcu[:, 1, :], vec(mod[:, 2 * D:3 * D])).then_inc(ev("bcu_in"), 16)
                for i in L_G + L_PW + L_O2 + [L_SGU, L_SD]:
                    load(sp, i)
                sp.wait_ge(ev("h5_ready"), 1)
                small(bc2[:, 0, :], vec(A["norm2_g_2"]), "n4_in")
                small(bc2[:, 1, :], vec(mod[:, 4 * D:5 * D]), "n4_in")
                small(bc2[:, 2, :], vec(mod[:, 3 * D:4 * D]), "n4_in")
                small(rw2, A["w_router_2"][0].rearrange("(k p) n -> p k n", p=P), "rw2_in")
                small(rb2, vec(A["router_bias_2"], 64), "rw2_in")
                sp.wait_ge(ev("h6_ready"), 1)
                sp.dma_start(hrows.rearrange("(t p) d -> p t d", p=P), hn_tm[:]).then_inc(ev("b_rows"), 16)
                sp.dma_start(bc2[:, 0, :], vec(mod[:, 5 * D:6 * D])).then_inc(ev("g2_in"), 16)
                moe_sp(sp, m2, ev)
                for t in range(TT):
                    for n in range(2):
                        sp.wait_ge(ev("out_ready"), 2 * t + n + 1)
                        sp.dma_start(out[0].rearrange("(t p) d -> p t d", p=P)[:, t, n * 512:(n + 1) * 512],
                                     out_tm[:, t, n * 512:(n + 1) * 512]).then_inc(ev("stored"), 16)
                sp.wait_ge(ev("stored"), 64)

            @second.gpsimd
            def _(pool):
                pool.memset(uT[:, :, 0:UPAD], 0.0)
                pool.memset(cmask, 0.0)
                for j in range(ROT):
                    pool.memset(invf[:, j:j + 1], float(np.float32(THETA) ** np.float32(-j / ROT)))
                pool.drain()
                blk = cmask.rearrange("p (a c) -> p a c", a=3)[:, 0:3:2, :]
                pool.affine_select(out=blk, in_=blk, compare_op=ALU.is_ge, fill=-1e30, base=0,
                                   pattern=[[0, 2], [-1, P]], channel_multiplier=1)
                pool.drain().then_inc(ev("c2_consts"), 1)
                pool.wait_ge(ev("h5_ready"), 1)
                codes(pool, m2)
                moe_pool(pool, m2, ev)

            @second.scalar
            def _(act):
                norm(act, None, "rstd5")
                act.wait_ge(ev("dw_T"), 1)
                act.copy(dwc.rearrange("p c k -> p k c"), ps[:, 0, 0:248].rearrange("p (k c) -> p k c", c=KC))
                act.copy(cc, ps[:, 0, 256:280])
                act.drain().then_inc(ev("dw_ready"), 1)
                chunks_out(act, "h5_T", "h5T_ready")
                for c in range(KC):
                    act.wait_ge(ev("u_proj"), 2 * c + 2)
                    if c >= 2:
                        act.wait_ge(ev("u_out"), c - 1)
                    act.activation(pbuf[:, 0, c % 2, 0:T], ps[:, 2 * (c % 2) + 1, 0:T], ACT.Sigmoid).then_inc(ev("u_sig"), 1)
                for g in range(12):
                    act.wait_ge(ev("qkv"), g + 1)
                    dst = (q_tm, k_tm, v_tm)[g // 4]
                    act.copy(dst[:, g % 2, (g % 4) // 2 * 512:(g % 4) // 2 * 512 + 512], ps[:, 4 + g % 4, :]).then_inc(
                        ev("qkv_out"), 1)
                    if g == 3 or g == 7:
                        j = g // 4
                        s32 = st2[:, 32 * j:32 * j + 32]
                        act.wait_ge(ev("qk_ss"), j + 1)
                        act.activation(s32, s32, ACT.Ln, scale=1.0 / AD, bias=EPSC)
                        act.drain()
                        act.activation(s32, s32, ACT.Exp, scale=-0.5).then_inc(ev("qk_rstd"), 1)
                    if g == 4:
                        act.wait_ge(ev("ang"), 1)
                        act.activation(rot.rearrange("p a t j -> p (a t j)"), rot.rearrange("p a t j -> p (a t j)"),
                                       ACT.Sin).then_inc(ev("rot_ready"), 1)
                        act.activation(st2[:, 64:66], st2[:, 64:66], ACT.Exp).then_inc(ev("lam_exp"), 1)
                for j, dst in enumerate((qT, kT)):
                    for c in range(KC):
                        act.wait_ge(ev("qk_T"), 4 * j + c // 2 + 1)
                        act.copy(dst[:, c, :], ps[:, 4 + c // 2, (c % 2) * T:(c % 2 + 1) * T])
                    act.drain().then_inc(ev("qkT_ready"), 1)
                act.wait_ge(ev("cen"), 1)
                act.activation(gc.rearrange("p t d -> p (t d)"), convT.rearrange("p a b -> p (a b)"), ACT.Square).then_inc(
                    ev("c_sq"), 1)
                act.wait_ge(ev("c_ss"), 1)
                act.activation(lnm, ps[:, 1, 0:T], ACT.Ln, scale=1.0 / D, bias=EPSC)
                act.drain()
                act.activation(lnm, lnm, ACT.Exp, scale=-0.5).then_inc(ev("c_rstd"), 1)
                act.wait_ge(ev("c_norm"), 1)
                for c in range(KC):
                    act.activation(convT[:, c, :], convT[:, c, :], ACT.Silu, scale=cc[:, KC + c:KC + c + 1],
                                   bias=cc[:, 2 * KC + c:2 * KC + c + 1])
                act.drain().then_inc(ev("s_ready"), 1)
                def weights(h):
                    act.wait_ge(ev("at_max"), h + 1)
                    for mp in range(2):
                        for t, (a, b) in enumerate(((0, P), (P, 3 * P))):
                            v = pbuf[:, h % 2, mp, a:b]
                            j = 4 * (h % 2) + 2 * mp + t
                            act.activation(v, v, ACT.Exp, scale=AD ** -0.5, bias=st2[:, 72 + j:73 + j],
                                           accum_out=st2[:, 80 + j:81 + j])
                    act.drain().then_inc(ev("at_p"), 1)
                weights(0)
                for h in range(AH):
                    if h + 1 < AH:
                        weights(h + 1)
                    act.wait_ge(ev("gates2"), h + 1)
                    dst = (gc, ga)[h // 4]
                    act.activation(dst[:, h % 2, (h % 4) // 2 * 512:(h % 4) // 2 * 512 + 512], ps[:, h % 2, :], ACT.Exp,
                                   scale=-1.0).then_inc(ev("gates2_out"), 1)
                    act.wait_ge(ev("at_T"), h + 1)
                    act.copy(aT, ps[:, 2, 0:3 * P]).then_inc(ev("at_Te"), 1)
                act.wait_ge(ev("o_ss"), 1)
                act.activation(st2[:, 0:16], st2[:, 0:16], ACT.Ln, scale=1.0 / (2 * AD), bias=EPSC)
                act.drain()
                act.activation(st2[:, 0:16], st2[:, 0:16], ACT.Exp, scale=-0.5).then_inc(ev("o_rstd"), 1)
                chunks_out(act, "y2_T", "y2T_ready")
                norm(act, "h5_ready", "rstd6")
                chunks_out(act, "h6_T", "h6T_ready")
                for t in range(TT):
                    act.wait_ge(ev("router2"), t + 1)
                    act.activation(scr[:, t, :], ps[:, t, 0:64], ACT.Sigmoid).then_inc(ev("scores"), 1)
                for k in range(2):
                    act.wait_ge(ev("sh_gu"), k + 1)
                    act.activation(shs[:, k, :], ps[:, 4 + k, 0:T], ACT.Silu).then_inc(ev("sh_silu"), 1)
                moe_act(act, m2, ev, ps)

            @second.vector
            def _(dve):
                def modulated(name, bc, sc, sh):
                    dve.scalar_tensor_tensor(sc, sc, 1.0, bc, ALU.add, ALU.mult)
                    dve.drain()
                    scale_rows(dve, name, sc)
                    dve.drain()
                    for t in range(TT):
                        dve.tensor_tensor(hn_tm[:, t, :], hn_tm[:, t, :], sh, ALU.add)
                dve.wait_ge(ev("n3_in"), 48)
                modulated("rstd5", bcn[:, 0:D], bcn[:, D:2 * D], bcs)
                dve.drain().then_inc(ev("hn5_ready"), 1)
                dve.wait_ge(ev("c2_in"), 16 * 14)
                dve.wait_ge(ev("c2_consts"), 1)
                posf = st2[:, 66:68]
                dve.tensor_copy(posf, posi[:])
                dve.drain()
                for t in range(TT):
                    dve.tensor_scalar(rot[:, 1, t, :], invf[:], posf[:, t:t + 1], None, ALU.mult)
                dve.drain()
                turns = st2[:, 96:112].rearrange("p (t j) -> p t j", t=TT)
                turni = roti[:].rearrange("p (t j) -> p t j", t=TT)
                C1 = 6.28125
                C2 = float(np.float32(TWO_PI - C1))
                for j, quarter in ((0, 0.25), (1, 0.0)):
                    dve.tensor_scalar(turns, rot[:, 1], 1.0 / TWO_PI, quarter, ALU.mult, ALU.add)
                    dve.drain()
                    dve.tensor_copy(turni, turns)
                    dve.drain()
                    dve.tensor_copy(turns, turni)
                    dve.drain()
                    dve.scalar_tensor_tensor(rot[:, j], turns, -C1, rot[:, 1], ALU.mult, ALU.add)
                    dve.drain()
                    dve.scalar_tensor_tensor(rot[:, j], turns, -C2, rot[:, j], ALU.mult, ALU.add)
                    dve.drain()
                    if j == 0:
                        dve.tensor_scalar(rot[:, j], rot[:, j], math.pi / 2, None, ALU.add)
                        dve.drain()
                flat = rot.rearrange("p a t j -> p (a t j)")
                dve.tensor_scalar(flat, flat, 3.1415925, -3.1415925, ALU.min, ALU.max).then_inc(ev("ang"), 1)
                lp = st2[:, 64:66]
                for j in range(2):
                    dve.tensor_tensor(lqk[:, 2 * j, :], lqk[:, 2 * j, :], lqk[:, 2 * j + 1, :], ALU.mult)
                    dve.drain()
                    dve.tensor_reduce(lp[:, j:j + 1], lqk[:, 2 * j, :], AX.X, ALU.add)
                dve.tensor_scalar(subg, subg, 1.0 - LAMBDA0, None, ALU.mult)
                dve.drain().then_inc(ev("lam_dot"), 1)
                for c in range(KC):
                    dve.wait_ge(ev("u_sig"), c + 1)
                    dve.tensor_tensor(uT[:, c, UPAD:], ps[:, 2 * (c % 2), 0:T], pbuf[:, 0, c % 2, 0:T], ALU.mult).then_inc(
                        ev("u_out"), 1)
                dve.wait_ge(ev("dw_ready"), 1)

                def conv(chunks):
                    for k in range(TAPS):
                        dve.drain()
                        for c in chunks:
                            if k == 0:
                                last = dve.tensor_scalar(convT[:, c, :], uT[:, c, 0:T], dwc[:, c, 0:1], cc[:, c:c + 1],
                                                         ALU.mult, ALU.add)
                            else:
                                last = dve.scalar_tensor_tensor(convT[:, c, :], uT[:, c, k:k + T], dwc[:, c, k:k + 1],
                                                                convT[:, c, :], ALU.mult, ALU.add)
                    dve.drain().then_inc(ev("conv2"), len(chunks))

                def qk_norm(j, x):
                    dve.wait_ge(ev("qkv_out"), 4 * j + 4)
                    xs = x[:].rearrange("p t (g d) -> p (t g) d", d=AD)
                    sq = gc.rearrange("p t (g d) -> p (t g) d", d=AD)
                    s32 = st2[:, 32 * j:32 * j + 32]
                    dve.tensor_tensor(sq, xs, xs, ALU.mult)
                    dve.drain()
                    dve.tensor_reduce(s32, sq, AX.X, ALU.add).then_inc(ev("qk_ss"), 1)
                    dve.wait_ge(ev("qk_rstd"), j + 1)
                    dve.tensor_tensor(xs, xs, s32.unsqueeze(2).to_broadcast([P, 32, AD]), ALU.mult)
                    dve.drain()
                    dve.tensor_tensor(xs, xs, qg[:, j:j + 1, :].to_broadcast([P, 32, AD]), ALU.mult)
                    dve.wait_ge(ev("rot_ready"), 1)
                    dve.drain()
                    g4 = gc.rearrange("p t (r g j) -> p t r g j", g=16, j=ROT)
                    for t in range(TT):
                        xt = x[:, t, :].rearrange("p (g d) -> p g d", d=AD)
                        x1, x2 = xt[:, :, 0:ROT], xt[:, :, ROT:2 * ROT]
                        cos, sin = (rot[:, r, t:t + 1, :].to_broadcast([P, 16, ROT]) for r in range(2))
                        for r, (a, b) in enumerate(((x1, cos), (x2, sin), (x2, cos), (x1, sin))):
                            dve.tensor_tensor(g4[:, t, r], a, b, ALU.mult)
                        dve.drain()
                        dve.tensor_tensor(x1, g4[:, t, 0], g4[:, t, 1], ALU.subtract)
                        dve.tensor_tensor(x2, g4[:, t, 2], g4[:, t, 3], ALU.add)
                    dve.drain().then_inc(ev("k2_ready" if j else "q2_ready"), 1)

                conv((0, 1, 2))
                qk_norm(0, q_tm)
                conv((3, 4, 5))
                qk_norm(1, k_tm)
                conv((6, 7))
                dve.wait_ge(ev("lam_exp"), 1)
                nlam = st2[:, 68:69]
                dve.tensor_tensor(nlam, lp[:, 1:2], lp[:, 0:1], ALU.subtract)
                dve.drain()
                dve.tensor_scalar(nlam, nlam, -LAMBDA0, None, ALU.add)
                dve.wait_ge(ev("c_sum"), 1)
                dve.tensor_scalar(lnm, ps[:, 0, 0:T], 1.0 / D, None, ALU.mult)
                dve.drain()
                dve.tensor_tensor(convT, convT, lnm.unsqueeze(1).to_broadcast([P, KC, T]), ALU.subtract).then_inc(ev("cen"), 1)
                dve.wait_ge(ev("c_rstd"), 1)
                dve.tensor_tensor(convT, convT, lnm.unsqueeze(1).to_broadcast([P, KC, T]), ALU.mult).then_inc(ev("c_norm"), 1)

                def maxima(h):
                    dve.wait_ge(ev("at_s"), h + 1)
                    for mp in range(2):
                        for t, (a, b) in enumerate(((0, P), (P, 3 * P))):
                            j = 4 * (h % 2) + 2 * mp + t
                            dve.tensor_tensor_reduce(out=pbuf[:, h % 2, mp, a:b], in0=ps[:, 4 + 2 * (h % 2) + mp, a:b],
                                                     in1=cmask[:, a:b], scale=1.0, scalar=-3e38, op0=ALU.add, op1=ALU.max,
                                                     accum_out=st2[:, 72 + j:73 + j])
                    j = 72 + 4 * (h % 2)
                    dve.drain()
                    dve.tensor_scalar(st2[:, j:j + 4], st2[:, j:j + 4], -AD ** -0.5, None, ALU.mult).then_inc(ev("at_max"), 1)
                maxima(0)
                for h in range(AH):
                    if h + 1 < AH:
                        if h >= 1:
                            dve.wait_ge(ev("at_T"), h)
                        maxima(h + 1)
                    dve.wait_ge(ev("at_p"), h + 1)
                    j = 80 + 4 * (h % 2)
                    dve.reciprocal(st2[:, j:j + 4], st2[:, j:j + 4])
                    dve.drain()
                    dve.tensor_scalar(st2[:, j + 2:j + 4], st2[:, j + 2:j + 4], nlam, None, ALU.mult)
                    dve.drain()
                    for t, (a, b) in enumerate(((0, P), (P, 3 * P))):
                        p1 = pbuf[:, h % 2, 1, a:b]
                        dve.tensor_scalar(p1, p1, st2[:, j + 2 + t:j + 3 + t], None, ALU.mult)
                    dve.drain()
                    for t, (a, b) in enumerate(((0, P), (P, 3 * P))):
                        p0, p1 = pbuf[:, h % 2, 0, a:b], pbuf[:, h % 2, 1, a:b]
                        last = dve.scalar_tensor_tensor(p0, p0, st2[:, j + t:j + t + 1], p1, ALU.mult, ALU.add)
                    last.then_inc(ev("at_a"), 1)
                    dve.wait_ge(ev("at_o"), h + 1)
                    dve.tensor_copy(o_tm[:, :, h * P:(h + 1) * P], ps[:, 3, 0:2 * P].rearrange("p (t d) -> p t d", t=TT)).then_inc(
                        ev("at_oe"), 1)
                dve.drain()
                of = o_tm[:].rearrange("p t (h d) -> p (t h) d", d=2 * AD)
                junk = qT.rearrange("p h t -> p (h t)").rearrange("p (g d) -> p g d", d=2 * AD)
                dve.tensor_tensor(junk, of, of, ALU.mult)
                dve.drain()
                dve.tensor_reduce(st2[:, 0:16], junk, AX.X, ALU.add).then_inc(ev("o_ss"), 1)
                dve.wait_ge(ev("gates2_out"), 8)
                for gt in (ga[:], gc):
                    dve.tensor_scalar(gt, gt, 1.0, None, ALU.add)
                dve.drain()
                for gt in (ga[:], gc):
                    dve.reciprocal(gt, gt)
                dve.wait_ge(ev("o_rstd"), 1)
                dve.tensor_tensor(of, of, st2[:, 0:16].unsqueeze(2).to_broadcast([P, 16, 2 * AD]), ALU.mult)
                dve.drain()
                dve.tensor_tensor(of, of, subg.unsqueeze(1).to_broadcast([P, 16, 2 * AD]), ALU.mult)
                dve.drain()
                dve.tensor_tensor(o_tm[:], o_tm[:], ga[:], ALU.mult)
                dve.wait_ge(ev("bcu_in"), 32)
                for n in range(2):
                    for t in range(TT):
                        half = slice(n * 512, (n + 1) * 512)
                        tmp = v_tm[:, t, half]
                        dve.wait_ge(ev("pw"), 2 * n + t + 1)
                        dve.tensor_tensor(tmp, ps[:, 2 * n + t, :], bcu[:, 0, half], ALU.add)
                        dve.drain()
                        dve.tensor_tensor(tmp, tmp, gc[:, t, half], ALU.mult)
                        dve.drain()
                        dve.tensor_tensor(gc[:, t, half], tmp, o_tm[:, t, half], ALU.add)
                dve.drain().then_inc(ev("y2_ready"), 1)
                for n in range(2):
                    for t in range(TT):
                        half = slice(n * 512, (n + 1) * 512)
                        dve.wait_ge(ev("o2"), 2 * n + t + 1)
                        dve.tensor_tensor(v_tm[:, t, half], ps[:, 2 * n + t, :], bcu[:, 1, half], ALU.mult)
                        dve.drain()
                        dve.tensor_tensor(x_tm[:, t, half], x_tm[:, t, half], v_tm[:, t, half], ALU.add)
                dve.drain().then_inc(ev("h5_ready"), 1)
                dve.wait_ge(ev("n4_in"), 48)
                modulated("rstd6", bc2[:, 0, :], bc2[:, 1, :], bc2[:, 2, :])
                dve.drain().then_inc(ev("h6_ready"), 1)
                dve.wait_ge(ev("rw2_in"), 32)
                dve.memset(g1v[:, :, 4, :], FAR)
                dve.wait_ge(ev("scores"), 2)
                dve.tensor_tensor(cho, scr, rb2.unsqueeze(1).to_broadcast([P, TT, 64]), ALU.add)
                dve.drain()
                for t in range(TT):
                    for g in range(8):
                        dve.max(g8[:, t, g, :], cho[:, t, 8 * g:8 * g + 8])
                dve.drain()
                gs, gk, gx, gq = (g1v[:, :, r, :] for r in range(4))
                dve.tensor_tensor(gs, g8[:, :, :, 0], g8[:, :, :, 1], ALU.add)
                dve.drain()
                for t in range(TT):
                    dve.max(gk[:, t, :], gs[:, t, :])
                dve.drain()
                dve.tensor_copy(g1v[:, :, 4, 0:4], gk[:, :, 0:4])
                dve.drain()
                for t in range(TT):
                    dve.match_replace(gx[:, t, :], g1v[:, t, 4, :], gs[:, t, :], -FAR)
                dve.drain()
                dve.tensor_tensor(gq, gx, gs, ALU.not_equal)
                dve.drain()
                dve.tensor_scalar(gq, gq, BIG, -BIG, ALU.mult, ALU.add)
                dve.drain()
                for t in range(TT):
                    dve.tensor_tensor(cho[:, t, :].rearrange("p (g e) -> p g e", g=8), cho[:, t, :].rearrange("p (g e) -> p g e", g=8),
                                      gq[:, t, :].unsqueeze(2).to_broadcast([P, 8, 8]), ALU.add)
                dve.drain()
                for t in range(TT):
                    dve.max(gk[:, t, :], cho[:, t, :])
                dve.drain()
                for t in range(TT):
                    dve.match_replace(chm[:, t, :], gk[:, t, :], cho[:, t, :], -FAR)
                dve.drain()
                dve.tensor_tensor(m2.mask, chm, cho, ALU.not_equal)
                dve.drain()
                dve.tensor_tensor(m2.gate, scr, m2.mask, ALU.mult)
                dve.drain()
                dve.tensor_reduce(stat[:, 18:20], m2.gate, AX.X, ALU.add)
                dve.drain()
                dve.reciprocal(stat[:, 18:20], stat[:, 18:20])
                dve.drain()
                for t in range(TT):
                    dve.tensor_scalar(m2.gate[:, t, :], m2.gate[:, t, :], stat[:, 18 + t:19 + t], ROUTED_SCALE, ALU.mult, ALU.mult)
                for k in range(2):
                    dve.wait_ge(ev("sh_silu"), k + 1)
                    dve.wait_ge(ev("sh_gu"), k + 3)
                    dve.tensor_tensor(shT[:, k, :], ps[:, 6 + k, 0:T], shs[:, k, :], ALU.mult)
                dve.drain().then_inc(ev("sh_hid"), 1)
                dve.wait_ge(ev("b_codes"), 1)
                route_lists_dve(dve, m2, ev, ps)
                moe_dve(dve, m2, ev, ps)
                dve.wait_ge(ev("b_acc"), 1)
                dve.wait_ge(ev("g2_in"), 16)
                for t in range(TT):
                    for n in range(2):
                        half = slice(n * 512, (n + 1) * 512)
                        dve.tensor_tensor(out_tm[:, t, half], ps[:, 2 * t + n, :], bc2[:, 0, half], ALU.mult)
                        dve.drain()
                        dve.tensor_tensor(out_tm[:, t, half], out_tm[:, t, half], x_tm[:, t, half], ALU.add).then_inc(
                            ev("out_ready"), 1)

            @second.tensor
            def _(pe):
                def product(bank, lhs, rhs, name=None, kk=KC, start=True):
                    for k in range(kk):
                        last = pe.matmul(bank, lhs(k), rhs(k), start=(k == 0 and start), stop=(k == kk - 1))
                    if name:
                        last.then_inc(ev(name), 1)

                def tok_tile(t):
                    return lambda k: hT[:, k, t * P:(t + 1) * P]

                pe.wait_ge(ev("c2_in"), 16 * 14)
                for j in range(2):
                    pe.transpose(ps[:, 0, 124 * j:124 * j + 124], drows[:, j, :], ident[0:124, 0:124])
                pe.transpose(ps[:, 0, 256:280], crows, ident[0:3 * KC, 0:3 * KC]).then_inc(ev("dw_T"), 1)
                pe.wait_ge(ev("hn5_ready"), 1)
                transposes(pe, hn_tm, 4, "h5_T")
                pe.wait_ge(ev("h5T_ready"), 1)
                for c in range(KC):
                    a, b = loads[L_A[2 * (c // 4)]], loads[L_A[2 * (c // 4) + 1]]
                    if c % 4 == 0:
                        arrived(pe, L_A[2 * (c // 4)])
                        arrived(pe, L_A[2 * (c // 4) + 1])
                    if c >= 2:
                        pe.wait_ge(ev("u_out"), c - 1)
                    for j, w in enumerate((a["dst"], b["dst"])):
                        product(ps[:, 2 * (c % 2) + j, 0:T], lambda k: w[:, k, (c % 4) * P:(c % 4 + 1) * P],
                                lambda k: hT[:, k, :], "u_proj")
                for g in range(12):
                    if g % 2 == 0:
                        arrived(pe, L_QKV[g // 2])
                    if g >= 4:
                        pe.wait_ge(ev("qkv_out"), g - 3)
                    w = loads[L_QKV[g // 2]]["dst"]
                    product(ps[:, 4 + g % 4, :], tok_tile(g % 2), lambda k: w[:, k, :], "qkv")
                pe.wait_ge(ev("qkv_out"), 12)
                for j, x in enumerate((q_tm, k_tm)):
                    pe.wait_ge(ev(("q2_ready", "k2_ready")[j]), 1)
                    if j:
                        pe.wait_ge(ev("qkT_ready"), 1)
                    transposes(pe, x, 4, "qk_T")
                pe.wait_ge(ev("u_out"), KC)
                pe.wait_ge(ev("conv2"), KC)
                product(ps[:, 0, 0:T], lambda k: ones[:, 0:P], lambda k: convT[:, k, :], "c_sum")
                pe.wait_ge(ev("c_sq"), 1)
                sq = gc.rearrange("p t d -> p (t d)").rearrange("p (c t) -> p c t", c=KC)
                product(ps[:, 1, 0:T], lambda k: ones[:, 0:P], lambda k: sq[:, k, :], "c_ss")
                pe.wait_ge(ev("qkT_ready"), 2)

                def scores(h):
                    if h >= 2:
                        pe.wait_ge(ev("at_max"), h - 1)
                    for mp in range(2):
                        b, bank = AD * mp, ps[:, 4 + 2 * (h % 2) + mp, :]
                        q, k = qT[b:b + AD, h, :], kT[b:b + AD, h, :]
                        pe.matmul(bank[:, 0:P], q[:, 0:P], k[:, 0:P], start=True, stop=True)
                        last = pe.matmul(bank[:, P:3 * P], q[:, P:T], k, start=True, stop=True)
                    last.then_inc(ev("at_s"), 1)
                scores(0)
                pe.wait_ge(ev("c_rstd"), 1)
                for h in range(AH):
                    if h + 1 < AH:
                        scores(h + 1)
                    if h % 2 == 0:
                        arrived(pe, L_G[h // 2])
                    if h >= 2:
                        pe.wait_ge(ev("gates2_out"), h - 1)
                    w = loads[L_G[h // 2]]["dst"]
                    product(ps[:, h % 2, :], tok_tile(h % 2), lambda k: w[:, k, :], "gates2")
                    pe.wait_ge(ev("at_a"), h + 1)
                    if h:
                        pe.wait_ge(ev("at_oe"), h)
                    for j in range(3):
                        last = pe.transpose(ps[:, 2, j * P:(j + 1) * P], pbuf[:, h % 2, 0, j * P:(j + 1) * P], ident[:])
                    last.then_inc(ev("at_T"), 1)
                    pe.wait_ge(ev("at_Te"), h + 1)
                    vs = [v_tm[:, t, h * P:(h + 1) * P] for t in range(TT)]
                    pe.matmul(ps[:, 3, 0:P], aT[:, 0:P], vs[0], start=True, stop=True)
                    pe.matmul(ps[:, 3, P:2 * P], aT[:, P:2 * P], vs[0], start=True, stop=False)
                    pe.matmul(ps[:, 3, P:2 * P], aT[:, 2 * P:3 * P], vs[1], start=False, stop=True).then_inc(ev("at_o"), 1)
                pe.wait_ge(ev("gates2_out"), 8)
                pe.wait_ge(ev("at_oe"), AH)
                pe.wait_ge(ev("s_ready"), 1)
                for n in range(2):
                    arrived(pe, L_PW[n])
                    w = loads[L_PW[n]]["dst"]
                    for t in range(TT):
                        product(ps[:, 2 * n + t, :], lambda k: convT[:, k, t * P:(t + 1) * P], lambda k: w[:, k, :], "pw")
                pe.wait_ge(ev("y2_ready"), 1)
                transposes(pe, gc, 4, "y2_T")
                pe.wait_ge(ev("y2T_ready"), 1)
                for n in range(2):
                    arrived(pe, L_O2[n])
                    w = loads[L_O2[n]]["dst"]
                    for t in range(TT):
                        product(ps[:, 2 * n + t, :], tok_tile(t), lambda k: w[:, k, :], "o2")
                pe.wait_ge(ev("h6_ready"), 1)
                transposes(pe, hn_tm, 4, "h6_T")
                pe.wait_ge(ev("h6T_ready"), 1)
                pe.wait_ge(ev("rw2_in"), 32)
                for t in range(TT):
                    product(ps[:, t, 0:64], tok_tile(t), lambda k: rw2[:, k, :], "router2")
                arrived(pe, L_SGU)
                w = loads[L_SGU]["dst"]
                for j in range(4):
                    product(ps[:, 4 + j, 0:T], lambda k: w[:, k, j * P:(j + 1) * P], lambda k: hT[:, k, :], "sh_gu")
                pe.wait_ge(ev("sh_hid"), 1)
                pe.wait_ge(ev("scores"), 2)
                arrived(pe, L_SD)
                w = loads[L_SD]["dst"]
                for t in range(TT):
                    for n in range(2):
                        product(ps[:, 2 * t + n, :], lambda k: shT[:, k, t * P:(t + 1) * P],
                                lambda k: w[:, k, n * 512:(n + 1) * 512], kk=2)
                pe.drain().then_inc(ev("sh_d"), 1)
                route_lists_pe(pe, m2, ev, ps)
                moe_pe(pe, m2, ev, ps)


INPUTS = [
    "x", "p", "norm1_g", "w_in", "conv_w", "conv_b", "igate_b", "fgate_b", "mnorm_g", "sb_out_g", "sgu_ln_g",
    "sgu_ln_b", "sgu_w", "sgu_b", "sgu_out_g", "w_out", "norm2_g", "router_gw", "router_gb", "router_ew",
    "router_eb", "w_gate", "w_up", "w_down", "ple_norm_g", "ple_gate_w", "ple_proj_w", "final_g", "c_2",
    "positions_2", "w_ada_2", "b_ada_2", "norm1_g_2", "w_in_2", "conv_dw_2", "conv_dw_b_2", "conv_ln_g_2",
    "conv_ln_b_2", "w_pw2_2", "b_pw2_2", "q_norm_g_2", "k_norm_g_2", "lambda_q1_2", "lambda_k1_2",
    "lambda_q2_2", "lambda_k2_2", "subln_g_2", "w_out_2", "norm2_g_2", "w_router_2", "router_bias_2",
    "w_exp_gu_2", "w_exp_down_2", "w_sh_gu_2", "w_sh_down_2",
]


def kernel(**inputs):
    import numpy as _np
    import concourse.bacc as _bacc
    from concourse import mybir as _mybir
    from concourse.bass_utils import run_bass_kernel_spmd as _run

    nc = _bacc.Bacc("TRN2", target_bir_lowering=False, num_devices=1)
    arrays, aps = {}, {}
    for name in INPUTS:
        a = _np.ascontiguousarray(inputs[name])
        arrays["in_" + name] = a
        aps[name] = nc.dram_tensor("in_" + name, a.shape, _mybir.dt.from_np(a.dtype), kind="ExternalInput").ap()
    out = nc.dram_tensor("out_x", (1, T, D), F32, kind="ExternalOutput").ap()
    build_program(nc, aps, out)
    r = _run(nc, [arrays], core_ids=[0])
    return r.results[0]["out_x"]
```

```python
import contextlib
import math

import numpy as np

import concourse.bass as bass
from concourse import mybir

F32 = mybir.dt.float32
I32 = mybir.dt.int32
BF16 = mybir.dt.bfloat16
F32R = mybir.dt.float32r
ALU = mybir.AluOpType
ACT = mybir.ActivationFunctionType
AX = mybir.AxisListType

P = 128
T = 256
TT = T // P
D = 1024
KC = D // P
EPS = 1e-6
RING = 6
SLOT = KC * 512

SBW, SBH, SBD = 384, 6, 64
MLW, MLH, MLD = 384, 4, 96
SGW, SGG, SGD = 256, 4, 64
CONV_K = 4
TAPS = 31
AH, AD = 8, 64
ROT = 8
THETA = 500000.0
LAMBDA0 = 0.2
ROUTED_SCALE = 2.5
TWO_PI = 2 * math.pi
R_N1, R_YG, R_PLE, R_SGB, R_C = 0, 8, 16, 24, 28
N_ROWS = 36
OFF = 1024


SLOTS = 64
MAX_EXTRA = T // SLOTS - 1
ACC, BG, BT, BD = 0, 4, 5, 6


class Moe:
    pass


def steps(eng, n, body):
    body(0, 0)
    body(1, 1)
    with eng.Fori(1, n // 2) as it:
        for par in range(2):
            body(it * 2 + par, par, it)


def rounds(eng, m, i, body):
    n = eng.value_load(m.lst[0:1, bass.ds(i, 1)], min_val=0, max_val=MAX_EXTRA)
    g = 0
    if not (isinstance(i, int) and i == 0):
        g = eng.value_load(m.lst[0:1, bass.ds(i + m.N, 1)], min_val=0, max_val=MAX_EXTRA * m.N) + i
    body(g, 0)
    with eng.If(n > 0):
        with eng.Fori(0, MAX_EXTRA) as r:
            with eng.If(n > r):
                body(r + 1 + g, r + 1)


def all_rounds(eng, m):
    before = eng.value_load(m.lst[0:1, 2 * m.N - 1:2 * m.N], min_val=0, max_val=MAX_EXTRA * m.N)
    return before + eng.value_load(m.lst[0:1, m.N - 1:m.N], min_val=0, max_val=MAX_EXTRA) + m.N


def wait_if(eng, sem, value):
    if not isinstance(value, int) or value > 0:
        eng.wait_ge(sem, value)


def moe_sp(sp, m, ev, start=True):
    def pair(i, par, it=0):
        if not isinstance(i, int):
            g = sp.value_load(m.lst[0:1, bass.ds(i + (m.N - 1), 1)], min_val=0, max_val=MAX_EXTRA * m.N) + (i - 1)
        for r in range(3):
            slot = m.slots[par][r]
            if isinstance(i, int) and i < 2:
                if m.before[par][r]:
                    sp.wait_ge(ev(m.before[par][r][0]), m.before[par][r][1])
            elif r == 0:
                sp.wait_ge(ev(m.p + "gu"), g)
            elif r == 2:
                sp.wait_ge(ev(m.p + "down"), g * 2)
            if r < 2:
                m.load_gu(sp, slot, i * 2 + r, ev(f"w_in{slot}"))
            else:
                for h in range(2):
                    m.load_d(sp, slot, h, i * 2 + h, ev(f"w_in{slot}"))
    if start:
        pair(0, 0)
        return
    pair(1, 1)
    sp.wait_ge(ev(m.p + "list"), 1)
    with sp.Fori(1, m.N // 2) as it:
        for par in range(2):
            pair(it * 2 + par, par, it)


def part_out(act, m, ev, part):
    for t in range(TT):
        if part:
            act.wait_ge(ev(m.p + "rest"), 2 * part - 1 + t)
        act.copy(m.tok3[:, part * TT + t, :], m.rest[t] if part else m.tokens[:, t, :]).then_inc(ev(m.p + "tok3"), 1)


def moe_pool(pool, m, ev):
    for part in range(2):
        for t in range(TT):
            pool.wait_ge(ev(m.p + "tok3"), 2 * part + t + 1)
            pool.tensor_tensor(m.rest[t], m.rest[t] if part else m.tokens[:, t, :], m.tok3[:, part * TT + t, :],
                               ALU.subtract)
            pool.drain().then_inc(ev(m.p + "rest"), 1)


def moe_act(act, m, ev, ps):
    def rows_out(at, r):
        act.wait_ge(ev(m.p + "T"), at)
        act.copy(m.xsT[:, 4 * r:4 * r + 4, :].rearrange("p a b -> p (a b)"), ps[:, BT, :]).then_inc(ev(m.p + "Te"), 1)

    act.wait_ge(ev(m.p + "list"), 1)
    rows_out(1, 0)
    rows_out(2, 1)

    def one(g, r):
        wait_if(act, ev(m.p + "hid"), g)
        act.wait_ge(ev(m.p + "gu"), g + 1)
        act.activation(m.sg, ps[:, BG, 0:256], ACT.Silu).then_inc(ev(m.p + "silu"), 1)
        rows_out(g * 2 + 3, 0)
        rows_out(g * 2 + 4, 1)
        wait_if(act, ev(m.p + "split"), g)
        act.wait_ge(ev(m.p + "down"), g * 2 + 1)
        act.activation(m.ys[:, 0:512], ps[:, BD, :], ACT.Copy, scale=m.sc[:, 1:2]).then_inc(ev(m.p + "ya"), 1)
    steps(act, m.N, lambda i, par, it=0: rounds(act, m, i, one))


def moe_dve(dve, m, ev, ps):
    def onehot(pair, first):
        dve.tensor_tensor(m.oneh, m.iota[:, bass.ds(first, SLOTS)].unsqueeze(1).unsqueeze(1).to_broadcast([P, TT, 2, SLOTS]),
                          m.pos[:, :, bass.ds(pair * 2, 2)].unsqueeze(3).to_broadcast([P, TT, 2, SLOTS]),
                          ALU.is_equal)
        dve.tensor_copy(m.tgs, m.tg[:, :, bass.ds(pair * 4, 4)])
        dve.drain()
        dve.tensor_copy(m.oneb, m.oneh.rearrange("p t h s -> p t (h s)"))
        dve.drain().then_inc(ev(m.p + "oneh"), 1)

    onehot(0, 0)
    dve.wait_ge(ev(m.p + "ip"), 1)
    for h in range(2):
        dve.tensor_copy(m.scn[64 * h:64 * h + 64, 0:2], ps[64 * h:64 * h + 64, BG, 256 + 2 * h:258 + 2 * h])
    dve.drain().then_inc(ev(m.p + "sc0"), 1)

    def split(at):
        dve.drain()
        dve.wait_ge(ev(m.p + "ya"), at)
        dve.tensor_copy(m.high, m.ys)
        dve.drain()
        dve.tensor_tensor(m.low, m.ys, m.high.bitcast(F32), ALU.subtract)
        dve.drain().then_inc(ev(m.p + "split"), 1)

    def one(i, g, r):
        e = dve.value_load(m.lst[0:1, bass.ds(i + 2 * m.N + r * m.N, 1)], min_val=0, max_val=m.N - 1)
        c = dve.value_load(m.lst[0:1, bass.ds(i + (3 + MAX_EXTRA) * m.N + r * m.N, 1)], min_val=0, max_val=T - SLOTS)
        if isinstance(g, int):
            dve.wait_ge(ev(m.p + "T"), 2)
        onehot(e, c)
        if not isinstance(g, int):
            split(g)
        dve.tensor_copy(m.sc, m.scn)
        dve.wait_ge(ev(m.p + "silu"), g + 1)
        dve.tensor_tensor(m.hid, m.sg, ps[:, BG, 256:512], ALU.mult).then_inc(ev(m.p + "hid"), 1)
        dve.wait_ge(ev(m.p + "hT"), g + 1)
        dve.tensor_copy(m.hidT.rearrange("p a b -> p (a b)"), ps[:, BG, 0:256])
        for h in range(2):
            dve.tensor_copy(m.scn[64 * h:64 * h + 64, 0:2], ps[64 * h:64 * h + 64, BG, 256 + 2 * h:258 + 2 * h])
        dve.drain().then_inc(ev(m.p + "hTe"), 1)
        wait_if(dve, ev(m.p + "comb"), g)
        dve.tensor_scalar(m.S, m.iota[:, T:2 * T], m.sc[:, 0:1], None, ALU.is_equal).then_inc(ev(m.p + "S"), 1)
        dve.wait_ge(ev(m.p + "down"), g * 2 + 2)
        dve.tensor_scalar(m.ys[:, 512:1024], ps[:, BD + 1, :], m.sc[:, 1:2], None, ALU.mult)
    steps(dve, m.N, lambda i, par, it=0: rounds(dve, m, i, lambda g, r: one(i, g, r)))
    split(all_rounds(dve, m))


def moe_pe(pe, m, ev, ps):
    def slots():
        for t in range(TT):
            last = pe.matmul(ps[:, BG, 256:260], m.oneh[:, t].rearrange("p h s -> p (h s)"), m.tgs[:, t, :],
                             start=(t == 0), stop=(t == TT - 1), skip_group_check=True)
        return last

    def pick(r):
        for c in range(4):
            f = slice((4 * r + c) * P, (4 * r + c + 1) * P)
            for part in range(3):
                for t in range(TT):
                    last = pe.matmul(ps[:, BT, c * P:(c + 1) * P], m.tok3[:, part * TT + t, f], m.oneb[:, t, :],
                                     start=(part + t == 0), stop=(part == 2 and t == TT - 1))
        last.then_inc(ev(m.p + "T"), 1)

    def combine():
        for t in range(TT):
            for n in range(2):
                for part in (m.high, m.low):
                    last = pe.matmul(ps[:, ACC + 2 * t + n, :], m.S[:, t * P:(t + 1) * P],
                                     part[:, n * 512:(n + 1) * 512], start=False, stop=True,
                                     skip_group_check=True)
        last.then_inc(ev(m.p + "comb"), 1)

    def arrived(i, par, it, r):
        first, per = m.totals[par][r]
        value = first + per * (i // 2 + 1) if isinstance(i, int) else it * per + (first + per)
        pe.wait_ge(ev(f"w_in{m.slots[par][r]}"), value)

    pe.wait_ge(ev(m.p + "list"), 1)
    pe.wait_ge(ev(m.p + "tok3"), 3 * TT)
    pe.wait_ge(ev(m.p + "oneh"), 1)
    slots().then_inc(ev(m.p + "ip"), 1)
    pick(0)
    pe.wait_ge(ev(m.p + "Te"), 1)
    pick(1)
    pe.wait_ge(ev(m.p + "sc0"), 1)

    def one(i, par, it, g, r):
        w = [m.view_gu(m.slots[par][0]), m.view_gu(m.slots[par][1])]
        wd = m.view_d(m.slots[par][2])
        first = isinstance(r, int)
        pe.wait_ge(ev(m.p + "Te"), g * 2 + 2)
        wait_if(pe, ev(m.p + "hTe"), g)
        if first:
            arrived(i, par, it, 0)
            arrived(i, par, it, 1)
        for k in range(KC):
            for h in range(2):
                last = pe.matmul(ps[64 * h:64 * h + 64, BG, :], m.xsT[:, k, 64 * h:64 * h + 64], w[h][:, k, :],
                                 start=(k == 0), stop=(k == KC - 1), skip_group_check=True)
        last.then_inc(ev(m.p + "gu"), 1)
        pe.wait_ge(ev(m.p + "oneh"), g + 2)
        pick(0)
        if not isinstance(g, int):
            pe.wait_ge(ev(m.p + "S"), g)
            pe.wait_ge(ev(m.p + "split"), g)
            combine()
        pe.wait_ge(ev(m.p + "hid"), g + 1)
        slots()
        for k in range(2):
            last = pe.transpose(ps[:, BG, k * P:(k + 1) * P], m.hid[:, k * P:(k + 1) * P], m.ident)
        last.then_inc(ev(m.p + "hT"), 1)
        pe.wait_ge(ev(m.p + "Te"), g * 2 + 3)
        pick(1)
        pe.wait_ge(ev(m.p + "hTe"), g + 1)
        if first:
            arrived(i, par, it, 2)
        for n in range(2):
            for k in range(2):
                for h in range(2):
                    last = pe.matmul(ps[64 * h:64 * h + 64, BD + n, :], m.hidT[:, k, 64 * h:64 * h + 64],
                                     wd[:, 2 * h + k, n * 512:(n + 1) * 512], start=(k == 0), stop=(k == 1),
                                     skip_group_check=True)
            last.then_inc(ev(m.p + "down"), 1)

    steps(pe, m.N, lambda i, par, it=0: rounds(pe, m, i, lambda g, r: one(i, par, it, g, r)))
    total = all_rounds(pe, m)
    pe.wait_ge(ev(m.p + "S"), total)
    pe.wait_ge(ev(m.p + "split"), total)
    combine()
    pe.drain().then_inc(ev(m.p + "acc"), 1)


def route_lists_pe(pe, m, ev, ps):
    pe.wait_ge(ev(m.p + "mask"), 1)
    E = m.E
    b = ps[:, BG, :]
    pe.matmul(b[:, 0:E], m.before_tri, m.mask[:, 0, :], start=True, stop=True)
    pe.matmul(b[:, E:2 * E], m.ones, m.mask[:, 0, :], start=True, stop=False)
    pe.matmul(b[:, E:2 * E], m.before_tri, m.mask[:, 1, :], start=False, stop=True)
    pe.matmul(b[:, 2 * E:3 * E], m.ones, m.mask[:, 0, :], start=True, stop=False)
    pe.matmul(b[:, 2 * E:3 * E], m.ones, m.mask[:, 1, :], start=False, stop=True).then_inc(ev(m.p + "posp"), 1)


def route_lists_dve(dve, m, ev, ps):
    E = m.E
    dve.drain().then_inc(ev(m.p + "mask"), 1)
    tg = m.tg.rearrange("p t (e c) -> p t e c", c=2)
    for t in range(TT):
        dve.tensor_copy(tg[:, t, :, 0], m.tok[:, t:t + 1].to_broadcast([P, E]))
    dve.tensor_copy(tg[:, :, :, 1], m.gate)
    dve.wait_ge(ev(m.p + "posp"), 1)
    b = ps[:, BG, :]
    dve.scalar_tensor_tensor(m.pos, b[:, 0:2 * E].rearrange("p (t e) -> p t e", t=TT), 1.0, m.mask, ALU.add, ALU.mult)
    dve.tensor_copy(m.count, b[:, 2 * E:3 * E])
    dve.drain()
    dve.tensor_scalar(m.pos, m.pos, -1.0, None, ALU.add)
    c = m.count.rearrange("p (n h) -> p n h", h=2)
    dve.tensor_tensor(m.most, c[:, :, 0], c[:, :, 1], ALU.max)
    dve.drain()
    dve.tensor_scalar(m.more, m.most, float(SLOTS), None, ALU.is_gt)
    for k in range(2, MAX_EXTRA + 1):
        dve.drain()
        dve.scalar_tensor_tensor(m.more, m.most, float(SLOTS * k), m.more, ALU.is_gt, ALU.add)
    dve.drain()
    dve.tensor_tensor_scan(m.upto, m.one3[:, 0:m.N], m.more, 0.0, ALU.mult, ALU.add)
    dve.drain()
    dve.tensor_tensor(m.upto, m.upto, m.more, ALU.subtract)
    dve.drain()
    dve.tensor_copy(m.lst[0:1, 0:m.N], m.more[0:1, :])
    dve.tensor_copy(m.lst[0:1, m.N:2 * m.N], m.upto[0:1, :])
    dve.drain()
    for r in range(MAX_EXTRA + 1):
        dve.tensor_scalar(m.more, m.most, float(SLOTS * (r + 1)), None, ALU.is_gt)
        dve.drain()
        dve.tensor_scalar(m.upto, m.more, float(SLOTS * (r + 1)), None, ALU.mult)
        dve.drain()
        dve.scalar_tensor_tensor(m.more, m.more, -1.0, m.iota[:, 1:m.N + 1], ALU.mult, ALU.add)
        dve.drain()
        dve.tensor_scalar(m.more, m.more, m.N - 1.0, None, ALU.min)
        dve.drain()
        dve.tensor_copy(m.lst[0:1, (2 + r) * m.N:(3 + r) * m.N], m.more[0:1, :])
        dve.tensor_copy(m.lst[0:1, (3 + MAX_EXTRA + r) * m.N:(4 + MAX_EXTRA + r) * m.N], m.upto[0:1, :])
        dve.drain()
    dve.drain().then_inc(ev(m.p + "list"), 1)


def build_program(nc, A, out):
    ctx = contextlib.ExitStack()
    with ctx:
        def sb(name, shape, dt=F32):
            return ctx.enter_context(nc.sbuf_tensor(name, shape, dt))

        sems = {}

        def ev(name):
            if name not in sems:
                sems[name] = nc.alloc_semaphore(name=name)
            return sems[name]

        def renew():
            old = [name for name in sems if not name.startswith("w_in")]
            nc.clear_and_free_semaphores([sems.pop(name) for name in old])

        BIG, FAR = 1e30, 3e38
        loose = dict(allow_small_or_imprecise_dtypes=True)

        ring = sb("ring", [P, RING, SLOT])
        x_tm = sb("x_tm", [P, TT, D])
        hn_tm = sb("hn_tm", [P, TT, D])
        hT = sb("hT", [P, KC, T])
        ident = sb("ident", [P, P])
        ntri = sb("ntri", [P, P])
        nones = sb("nones", [P, P])
        sel4 = sb("sel4", [MLH, MLH, P])
        selq = sb("selq", [P, P])
        rows = sb("rows", [N_ROWS, P])
        cols = sb("cols", [P, N_ROWS])
        rows96 = sb("rows96", [40, MLD])
        cols96 = sb("cols96", [MLD, 40])
        gate_w = sb("gate_w", [P, KC, 2 * MLH])
        gate_b = sb("gate_b", [MLH, 2])
        stat = sb("stat", [P, 64])
        eps_c = sb("eps_c", [P, 1])
        EPSC = eps_c[:, 0:1]
        parts = sb("parts", [P, TT, D], F32R)
        slot_tok = sb("slot_tok", [P, T], F32R)
        mod = nc.dram_tensor("mod", [1, 6 * D], F32, kind="Internal").ap()
        cact = sb("cact", [P, KC])
        crep = sb("crep", [P, KC, 32])

        iota = sb("iota", [P, 2 * T])
        tok = sb("tok", [P, TT])
        ones = sb("ones", [P, 192])
        zero = sb("zero", [P, P])
        tri = sb("tri", [P, P])
        lst = sb("lst", [1, 320], I32)

        ps = ctx.enter_context(nc.psum_tensor("ps", [P, 8, 512], F32))

        WORK = 16032
        work = sb("work", [P, WORK])

        def carver(at=0):
            at = [at]
            def take(name, shape):
                n = 1
                for d in shape[1:]:
                    n *= d
                v = work[0:shape[0], at[0]:at[0] + n]
                at[0] += n
                assert at[0] <= WORK, (name, at[0])
                if len(shape) == 3:
                    v = v.rearrange("p (a b) -> p a b", a=shape[1])
                if len(shape) == 4:
                    v = v.rearrange("p (a b c) -> p a b c", a=shape[1], b=shape[2])
                return v
            return take
        mb = carver()
        qaT = mb("qaT", [P, 3, T])
        kaT = mb("kaT", [P, 3, T])
        va = mb("va", [P, TT, SBW])
        convbuf = mb("convbuf", [P, 2 * MLH * (T + CONV_K - 1)])
        cT = convbuf[0:MLD].rearrange("p (j t) -> p j t", j=2 * MLH)
        qkT = mb("qkT", [MLD, 2 * MLH, T])
        vba = mb("vba", [P, TT, MLH, MLD + 1])
        ob = mb("ob", [P, TT, MLW])
        uv = mb("uv", [P, TT, 2, SGW])
        bada = mb("bada", [12, 512])
        modst = mb("modst", [1, 512])
        adap = mb("adap", [P, 512])
        scratch = mb("scratch", [P, TT, D])
        gT = scratch[0:MLH].rearrange("p a b -> p (a b)").rearrange("p (r t) -> p r t", r=8)
        gcol = mb("gcol", [P, TT, 8])
        sgw = convbuf[:, 0:512].rearrange("p (g s) -> p g s", g=SGG)
        sgwT = convbuf[:, 512:1024].rearrange("p (g s) -> p g s", g=SGG)
        lnb = convbuf[:, 1024:1536].rearrange("p (a c) -> p a c", a=2)
        spb = mb("spb", [P, 2, 3 * P])
        spt = mb("spt", [P, 2, 3 * P])
        amt = mb("amt", [P, 2, 3 * P])
        dmt = spt

        def moe_buffers(prefix, E):
            m = Moe()
            take = carver()
            m.p, m.E, m.N = prefix, E, E // 2
            m.lst, m.iota, m.tok, m.tokens = lst, iota[:], tok, hn_tm[:]
            m.ident, m.ones, m.before_tri, m.one3 = ident[:], ones[:, 0:P], tri[:], ones[:, 0:3 * E]
            m.tg = take("tg", [P, TT, 2 * E])
            m.pos = take("pos", [P, TT, E])
            m.mask = take("mask", [P, TT, E])
            m.gate = take("gate", [P, TT, E])
            m.count = take("count", [P, E])
            m.most, m.more, m.upto = (take(n, [P, m.N]) for n in ("most", "more", "upto"))
            m.oneh = take("oneh", [P, TT, 2, SLOTS])
            m.oneb = take("oneb", [P, TT, SLOTS]).bitcast(BF16)
            m.tok3 = take("tok3", [P, 3 * TT, D // 2]).bitcast(BF16)
            m.tgs = take("tgs", [P, TT, 4])
            m.xsT = take("xsT", [P, KC, P])
            m.sg = take("sg", [P, 256])
            m.hid = take("hid", [P, 256])
            m.hidT = take("hidT", [P, 2, P])
            m.sc, m.scn = take("sc", [P, 2]), take("scn", [P, 2])
            m.S = slot_tok[:]
            m.ys = take("ys", [P, D])
            m.high, m.low = parts[:, 0, :], parts[:, 1, :]
            m.rest = [m.ys, m.xsT.rearrange("p a b -> p (a b)")]
            m.take = take
            m.view_gu = lambda slot: slot_view(slot, KC, 512)
            m.view_d = lambda slot: slot_view(slot, 4, D)
            return m

        m1 = moe_buffers("a_", 32)
        m1.incs = (32, 32, 32)
        rw = m1.take("rw", [P, KC, 36])
        rb = m1.take("rb", [P, 36])
        bc1 = m1.take("bc1", [P, D])
        gl = m1.take("gl", [P, TT, 8])
        gv = m1.take("gv", [P, TT, 8])
        gr = m1.take("gr", [P, TT, 8])
        gm = m1.take("gm", [P, TT, 4])
        el = m1.take("el", [P, TT, 32])
        er = m1.take("er", [P, TT, 32])
        v8 = m1.take("v8", [P, TT, 8])
        p_tm = m1.take("p_tm", [P, TT, 256])
        pT = m1.take("pT", [P, 2, T])
        pg = m1.take("pg", [P, TT, D])

        def load_gu1(eng, slot, e, sem):
            for j, w in enumerate((A["w_gate"], A["w_up"])):
                eng.dma_start(slot_view(slot, KC, 512)[:, :, 256 * j:256 * j + 256],
                              w[0][bass.ds(e, 1)].rearrange("o (k p) n -> p (o k) n", p=P)).then_inc(sem, 16)
        def load_d(w):
            def load(eng, slot, h, e, sem):
                eng.dma_start(slot_view(slot, 4, D)[:, 2 * h:2 * h + 2, :],
                              w[bass.ds(e, 1)].rearrange("o (k p) n -> p (o k) n", p=P)).then_inc(sem, 16)
            return load
        m1.load_gu, m1.load_d = load_gu1, load_d(A["w_down"][0])

        mc = carver()
        UPAD = TAPS - 1
        uT = mc("uT", [P, KC, UPAD + T])
        convT = mc("convT", [P, KC, T])
        qT = mc("qT", [P, AH, T])
        kT = mc("kT", [P, AH, T])
        v_tm = mc("v_tm", [P, TT, D])
        gc = mc("gc", [P, TT, D])
        pbuf = mc("pbuf", [P, 2, 2, 3 * P])
        dwc = mc("dwc", [P, KC, TAPS])
        cc = mc("cc", [P, 3 * KC])
        cmask = mc("cmask", [P, 3 * P])
        qg = mc("qg", [P, 2, AD])
        subg = mc("subg", [P, 2 * AD])
        lqk = mc("lqk", [P, 4, AD])
        st2 = mc("st2", [P, 128])
        rot = mc("rot", [P, 2, TT, 8])
        lnm = mc("lnm", [P, T])
        qk_sq = qT.rearrange("p a b -> p (a b)").rearrange("p (t d) -> p t d", t=TT)
        gc_c = gc.rearrange("p t d -> p (t d)").rearrange("p (c t) -> p c t", c=KC)
        aT = mc("aT", [P, 3 * P])
        q_tm, k_tm, o_tm = kT.rearrange("p a b -> p (a b)").rearrange("p (t d) -> p t d", t=TT), hn_tm, hn_tm
        ga = uT.rearrange("p a b -> p (a b)")[:, 0:TT * D].rearrange("p (t d) -> p t d", t=TT)
        drows = kT.rearrange("p a b -> p (a b)")[0:124, 0:2 * P].rearrange("p (a b) -> p a b", a=2)
        crows = kT.rearrange("p a b -> p (a b)")[0:3 * KC, 2 * P:3 * P]
        bcu = kT.rearrange("p a b -> p (a b)").rearrange("p (a b) -> p a b", a=2)
        bcn = convT.rearrange("p a b -> p (a b)")
        bcs = qT.rearrange("p a b -> p (a b)")[:, 0:D]
        posi = sb("posi", [P, TT], I32)
        roti = sb("roti", [P, TT * 8], I32)
        invf = sb("invf", [P, 8])

        m2 = moe_buffers("b_", 64)
        m2.incs = (16, 16, 32)
        bc2 = m2.take("bc2", [P, 3, D])
        rw2 = m2.take("rw2", [P, KC, 64])
        rb2 = m2.take("rb2", [P, 64])
        scr = m2.take("scr", [P, TT, 64])
        cho = m2.take("cho", [P, TT, 64])
        chm = m2.take("chm", [P, TT, 64])
        g8 = m2.take("g8", [P, TT, 8, 8])
        g1v = m2.take("g1v", [P, TT, 5, 8])
        shs = m2.take("shs", [P, 2, T])
        shT = m2.take("shT", [P, 2, T])
        out_tm = hn_tm

        def load_gu2(eng, slot, e, sem):
            eng.dma_start(slot_view(slot, KC, 512), A["w_exp_gu_2"][0][bass.ds(e, 1)].rearrange(
                "o (k p) n -> p (o k) n", p=P)).then_inc(sem, 16)
        m2.load_gu, m2.load_d = load_gu2, load_d(A["w_exp_down_2"][0])

        def colblock(w, c0, n):
            return w[:, c0:c0 + n].rearrange("(k p) n -> p k n", p=P)

        w_in = A["w_in"][0]
        slot_total = [0] * RING
        slot_user = [None] * RING
        n_loads = 0
        loads = []

        def slot_view(slot, k, n):
            return ring[:, slot, 0:k * n].rearrange("p (k n) -> p k n", k=k)

        def add_load(src, k, n, by, value):
            nonlocal n_loads
            slot = n_loads % RING
            slot_total[slot] += 16
            loads.append(dict(dst=slot_view(slot, k, n), src=src, slot=slot, free=slot_user[slot], here=slot_total[slot]))
            slot_user[slot] = (by, value)
            n_loads += 1
            return len(loads) - 1

        def add_moe(m):
            nonlocal n_loads
            m.slots = [[(n_loads + 3 * par + r) % RING for r in range(3)] for par in range(2)]
            m.before = [[slot_user[x] for x in row] for row in m.slots]
            m.totals = [[(slot_total[x], m.incs[r]) for r, x in enumerate(row)] for row in m.slots]
            for par in range(2):
                for r, x in enumerate(m.slots[par]):
                    slot_total[x] += m.incs[r] * m.N // 2
                    slot_user[x] = (m.p + "acc", 1)
            n_loads += 3 * m.N

        L_IN = [add_load(colblock(w_in, c * 384, 384), KC, 384, "proj", n)
                for c, n in enumerate((5, 8, 10, 14, 18, 20, 22))]
        L_IN.append(add_load(colblock(w_in, 2696, 512), KC, 512, "proj", 24))
        L_ADA = [add_load(colblock(A["w_ada_2"][0], n * 512, 512), KC, 512, "ada_part", n + 1) for n in range(12)]
        L_OUT = [add_load(colblock(A["w_out"][0], n * 512, 512), KC, 512, "o_proj", 2 * n + 2) for n in range(2)]
        N_MIX = len(loads)
        add_moe(m1)
        L_PLE = [add_load(colblock(A["ple_gate_w"][0], n * 512, 512), KC, 512, "ple_g", 2 * n + 2) for n in range(2)]
        L_PROJ = add_load(A["ple_proj_w"][0].rearrange("(k p) n -> p k n", p=P), 2, D, "ple_p", 4)
        w_in2 = A["w_in_2"][0]
        def cols2(c, by, value):
            return add_load(colblock(w_in2, 512 * c, 512), KC, 512, by, value)
        L_A = [cols2(c, "u_proj", v) for c, v in ((0, 8), (2, 8), (1, 16), (3, 16))]
        L_QKV = [cols2(4 + c, "qkv", 2 * c + 2) for c in range(6)]
        L_G = [cols2(10 + c, "gates2", 2 * c + 2) for c in range(4)]
        L_PW = [add_load(colblock(A["w_pw2_2"][0], n * 512, 512), KC, 512, "pw", 2 * n + 2) for n in range(2)]
        L_O2 = [add_load(colblock(A["w_out_2"][0], n * 512, 512), KC, 512, "o2", 2 * n + 2) for n in range(2)]
        L_SGU = add_load(colblock(A["w_sh_gu_2"][0], 0, 512), KC, 512, "sh_gu", 4)
        L_SD = add_load(A["w_sh_down_2"][0].rearrange("(k p) n -> p k n", p=P), 2, D, "sh_d", 1)
        add_moe(m2)
        NUM = (7, 3)

        def load(sp, i):
            x = loads[i]
            if x["free"]:
                sp.wait_ge(ev(x["free"][0]), x["free"][1])
            sp.dma_start(x["dst"], x["src"]).then_inc(ev(f"w_in{x['slot']}"), 16)

        def norm(act, ready, name):
            act.preload_act_table(ACT.Ln)
            if ready:
                act.wait_ge(ev(ready), 1)
            for t in range(TT):
                act.activation(parts[:, t, :], x_tm[:, t, :], ACT.Square, accum_out=stat[:, t:t + 1])
            act.drain()
            act.activation(stat[:, 2:4], stat[:, 0:2], ACT.Ln, scale=1.0 / D, bias=EPSC)
            act.drain()
            act.activation(stat[:, 4:6], stat[:, 2:4], ACT.Exp, scale=-0.5).then_inc(ev(name), 1)

        def chunks_out(act, name, done, gain=None):
            for c in range(KC):
                act.wait_ge(ev(name), c // 2 + 1)
                kw = {} if gain is None else dict(scale=cols[:, gain + c:gain + c + 1])
                act.activation(hT[:, c, :], ps[:, 4 + c // 2, (c % 2) * T:(c % 2 + 1) * T], ACT.Copy, **kw)
            act.drain().then_inc(ev(done), 1)

        def scale_rows(dve, name, gain=None, out=hn_tm):
            dve.wait_ge(ev(name), 1)
            for t in range(TT):
                if gain is None:
                    dve.tensor_scalar(out[:, t, :], x_tm[:, t, :], stat[:, 4 + t:5 + t], None, ALU.mult)
                else:
                    dve.scalar_tensor_tensor(out[:, t, :], x_tm[:, t, :], stat[:, 4 + t:5 + t], gain, ALU.mult,
                                             ALU.mult)

        def arrived(pe, i):
            pe.wait_ge(ev(f"w_in{loads[i]['slot']}"), loads[i]["here"])

        def transposes(pe, src, bank0, name):
            for c in range(KC):
                for t in range(TT):
                    last = pe.transpose(ps[:, bank0 + c // 2, (c % 2) * T + t * P:(c % 2) * T + (t + 1) * P],
                                        src[:, t, c * P:(c + 1) * P], ident[:])
                if c % 2:
                    last.then_inc(ev(name), 1)

        with nc.Block() as first:
            @first.sync
            def _(sp):
                xv = A["x"][0].rearrange("(t p) d -> p t d", p=P)
                for t in range(TT):
                    sp.dma_start(x_tm[:, t, :], xv[:, t, :]).then_inc(ev("x_in"), 16)

                def rowdma(dst, src):
                    sp.dma_start(dst, src).then_inc(ev("rows_in"), 16)
                rowdma(rows[R_N1:R_N1 + 8, :], A["norm1_g"][0].rearrange("(c p) -> c p", p=P))
                rowdma(rows[R_YG:R_YG + 3, :], A["sb_out_g"][0].rearrange("(c p) -> c p", p=P))
                rowdma(rows[R_YG + 3:R_YG + 6, :], A["mnorm_g"][0].rearrange("(c p) -> c p", p=P))
                rowdma(rows[R_YG + 6:R_YG + 8, :], A["sgu_out_g"][0].rearrange("(c p) -> c p", p=P))
                rowdma(rows[R_PLE:R_PLE + 8, :], A["ple_norm_g"][0].rearrange("(c p) -> c p", p=P))
                rowdma(rows[R_SGB:R_SGB + 4, :], A["sgu_b"][0])
                rowdma(rows[R_C:R_C + 8, :], A["c_2"][0].rearrange("(c p) -> c p", p=P))
                rowdma(rows96[0:32, :], A["conv_w"][0].rearrange("k (j c) -> (k j) c", c=MLD))
                rowdma(rows96[32:40, :], A["conv_b"][0].rearrange("(j c) -> j c", c=MLD))
                sp.dma_start(gate_w[:], colblock(w_in, 2688, 8)).then_inc(ev("gatew_in"), 16)
                sp.dma_start(gate_b[:, 0:1], A["igate_b"].rearrange("a h -> h a")).then_inc(ev("gatew_in"), 16)
                sp.dma_start(gate_b[:, 1:2], A["fgate_b"].rearrange("a h -> h a")).then_inc(ev("gatew_in"), 16)

                for i in range(RING):
                    load(sp, i)
                sp.dma_start(bada[:], A["b_ada_2"][0].rearrange("(n c) -> n c", c=512)).then_inc(ev("bada_in"), 16)
                for i in range(RING, N_MIX):
                    load(sp, i)
                moe_sp(sp, m1, ev)
                sp.wait_ge(ev("proj_all"), 1)
                sp.wait_ge(ev("h1_ready"), 1)
                sp.dma_start(bc1, A["norm2_g"].to_broadcast([P, D])).then_inc(ev("n2_in"), 16)
                sp.dma_start(rw[:, :, 0:4], A["router_gw"][0].rearrange("(k p) n -> p k n", p=P)).then_inc(ev("rw_in"), 16)
                sp.dma_start(rw[:, :, 4:36], A["router_ew"][0].rearrange("(k p) n -> p k n", p=P)).then_inc(ev("rw_in"), 16)
                sp.dma_start(rb[:, 0:4], A["router_gb"].to_broadcast([P, 4])).then_inc(ev("rw_in"), 16)
                sp.dma_start(rb[:, 4:36], A["router_eb"].to_broadcast([P, 32])).then_inc(ev("rw_in"), 16)
                sp.dma_start(p_tm, A["p"][0, 0].rearrange("(t p) d -> p t d", p=P)).then_inc(ev("p_in"), 16)
                sp.wait_ge(ev("h2_ready"), 1)
                sp.dma_start(bc1, A["final_g"].rearrange("(a d) -> a d", a=1).to_broadcast([P, D])).then_inc(ev("fg_in"), 16)
                moe_sp(sp, m1, ev, False)
                for i in L_PLE + [L_PROJ]:
                    load(sp, i)
                for i in (L_A + L_QKV)[:RING]:
                    load(sp, i)

            @first.gpsimd
            def _(pool):
                pool.memset(ident[:], 0.0)
                pool.memset(ntri[:], -1.0)
                pool.memset(nones[:], -1.0)
                pool.memset(sel4[:], 0.0)
                pool.memset(selq[:], 0.0)
                pool.memset(eps_c[:], EPS)
                pool.drain()
                pool.affine_select(out=ident[:], in_=ident[:], compare_op=ALU.not_equal, fill=1.0, base=0,
                                   pattern=[[-1, P]], channel_multiplier=1)
                pool.affine_select(out=ntri[:], in_=ntri[:], compare_op=ALU.is_ge, fill=0.0, base=0,
                                   pattern=[[-1, P]], channel_multiplier=1)
                pool.affine_select(out=sel4[:], in_=sel4[:], compare_op=ALU.not_equal, fill=1.0, base=0,
                                   pattern=[[-1, MLH], [0, P]], channel_multiplier=1)
                sq = selq[:].rearrange("p (a c) -> p a c", a=4)
                pool.affine_select(out=selq[:], in_=selq[:], compare_op=ALU.not_equal, fill=1.0, base=0,
                                   pattern=[[0, P]], channel_multiplier=1)
                for j in range(1, 4):
                    pool.drain()
                    pool.affine_select(out=selq[:], in_=selq[:], compare_op=ALU.not_equal, fill=1.0, base=-32 * j,
                                       pattern=[[0, P]], channel_multiplier=1)
                pool.memset(cT[:, :, 0:CONV_K - 1], 0.0)
                pool.memset(vba[:, :, :, MLD:MLD + 1], 1.0)
                pool.memset(ones[:], 1.0)
                pool.memset(zero[:], 0.0)
                pool.iota(iota[:, 0:T], pattern=[[1, T]], base=0, channel_multiplier=0, **loose)
                pool.iota(iota[:, T:], pattern=[[1, T]], base=-OFF, channel_multiplier=0, **loose)
                pool.iota(tok[:], pattern=[[P, TT]], base=-OFF, channel_multiplier=1, **loose)
                pool.drain()
                pool.affine_select(out=tri[:], in_=ones[:, 0:P], compare_op=ALU.is_ge, fill=0.0, base=-1,
                                   pattern=[[1, P]], channel_multiplier=-1)
                pool.drain().then_inc(ev("consts"), 1)

                def keep_causal(buf, strict):
                    blk = buf.rearrange("p (a c) -> p a c", a=3)[:, 0:3:2, :]
                    pool.affine_select(out=blk, in_=blk, compare_op=ALU.is_ge, fill=0.0, base=-1 if strict else 0,
                                       pattern=[[0, 2], [1, P]], channel_multiplier=-1).then_inc(
                                           ev("sb_masked") if strict else ev("ml_masked"), 1)

                def mod_row(n):
                    pool.wait_ge(ev("ada_out"), n + 1)
                    pool.dma_start(mod[:, n * 512:(n + 1) * 512], modst[:]).then_inc(ev("mod_out"), 16)

                for h in range(SBH):
                    pool.wait_ge(ev("sb_softplus"), h + 1)
                    keep_causal(spb[:, h % 2, :], True)
                    mod_row(2 * h)
                    pool.wait_ge(ev("sb_weights"), h + 1)
                    keep_causal(amt[:, h % 2, :], True)
                    mod_row(2 * h + 1)
                for h in range(MLH):
                    pool.wait_ge(ev("ml_decay"), h + 1)
                    keep_causal(dmt[:, h % 2, :], False)
                pool.wait_ge(ev("h2_ready"), 1)
                moe_pool(pool, m1, ev)

            @first.scalar
            def _(act):
                act.wait_ge(ev("consts"), 1)
                act.wait_ge(ev("x_in"), 32)
                for t in range(TT):
                    act.activation(parts[:, t, :], x_tm[:, t, :], ACT.Square, accum_out=stat[:, t:t + 1])
                act.drain()
                act.activation(stat[:, 2:4], stat[:, 0:2], ACT.Ln, scale=1.0 / D, bias=EPSC)
                act.drain()
                act.activation(stat[:, 4:6], stat[:, 2:4], ACT.Exp, scale=-0.5).then_inc(ev("rstd1"), 1)
                act.wait_ge(ev("rows_T"), 1)
                act.copy(cols[:], ps[:, 7, 0:N_ROWS])
                act.copy(cols96[:], ps[0:MLD, 7, 64:104])
                act.drain().then_inc(ev("cols_ready"), 1)
                for c in range(KC):
                    act.wait_ge(ev("h_T"), c // 2 + 1)
                    act.activation(hT[:, c, :], ps[:, c // 2, (c % 2) * T:(c % 2 + 1) * T], ACT.Copy,
                                   scale=cols[:, R_N1 + c:R_N1 + c + 1])
                act.drain().then_inc(ev("hT_ready"), 1)
                act.activation(stat[:, 16:24], cols[:, R_C:R_C + 8], ACT.Exp, scale=-1.0).then_inc(ev("c_exp"), 1)

                g = 0
                def take(dst, view, func=ACT.Copy, **kw):
                    nonlocal g
                    act.wait_ge(ev("proj"), g + 1)
                    act.activation(dst, view(ps[:, g % 4, :]), func, **kw).then_inc(ev("proj_evac"), 1)
                    g += 1
                for j in range(2):
                    take(gT[:, j, :], lambda b: b[0:MLH, 0:T], ACT.Identity, bias=gate_b[:, j:j + 1])
                for c in range(3):
                    take(qaT[:, c, :], lambda b: b[:, 0:T], ACT.Copy, scale=SBD ** -0.5)
                for c in range(3):
                    take(kaT[:, c, :], lambda b: b[:, 0:T])
                for t in range(TT):
                    take(va[:, t, :], lambda b: b[:, 0:SBW])
                for j in range(2 * MLH):
                    take(cT[:, j, CONV_K - 1:], lambda b: b[0:MLD, 0:T])
                for t in range(TT):
                    take(vba[:, t, :, 0:MLD], lambda b: b[:, 0:MLW].rearrange("p (h d) -> p h d", h=MLH))
                for t in range(TT):
                    take(ob[:, t, :], lambda b: b[:, 0:MLW], ACT.Sigmoid)
                for t in range(TT):
                    take(uv[:, t, :, :].rearrange("p a c -> p (a c)"), lambda b: b[:, :], ACT.Gelu_apprx_tanh)
                act.drain().then_inc(ev("proj_all"), 1)

                def conv_silu():
                    act.wait_ge(ev("conv"), 1)
                    act.activation(qkT, qkT, ACT.Silu).then_inc(ev("qk_ready"), 1)
                    act.dma_start(sgw, A["sgu_w"][0].rearrange("g t s -> t g s")).then_inc(ev("sgu_in"), 16)
                    act.dma_start(lnb[:, 0, :], A["sgu_ln_g"].to_broadcast([P, SGW])).then_inc(ev("sgu_in"), 16)
                    act.dma_start(lnb[:, 1, :], A["sgu_ln_b"].to_broadcast([P, SGW])).then_inc(ev("sgu_in"), 16)

                def gate_ln():
                    act.activation(gT[:, 2, :], gT[:, 1, :], ACT.Abs)
                    act.drain()
                    act.activation(gT[:, 3, :], gT[:, 2, :], ACT.Exp, scale=-1.0)
                    act.drain()
                    act.activation(gT[:, 4, :], gT[:, 3, :], ACT.Ln, bias=1.0).then_inc(ev("f_ln"), 1)

                def ada(n):
                    act.wait_ge(ev("ada_part"), n + 1)
                    if n >= 1:
                        act.wait_ge(ev("ada_bc"), n)
                    act.copy(adap[:], ps[:, 2, :]).then_inc(ev("ada_row"), 1)
                for h in range(SBH):
                    zb = ps[:, 4 + h % 2, 0:3 * P]
                    act.wait_ge(ev("sb_z"), h + 1)
                    if h >= 2:
                        act.wait_ge(ev("sb_softplus"), h - 1)
                    act.activation(spt[:, h % 2, :], zb, ACT.Abs)
                    act.drain()
                    act.activation(spt[:, h % 2, :], spt[:, h % 2, :], ACT.Exp, scale=-1.0)
                    act.drain()
                    act.activation(spt[:, h % 2, :], spt[:, h % 2, :], ACT.Ln, bias=1.0).then_inc(ev("sb_ln"), 1)
                    ada(2 * h)
                    act.wait_ge(ev("sb_r"), h + 1)
                    if h >= 2:
                        act.wait_ge(ev("sb_y"), h - 1)
                    act.activation(amt[:, h % 2, :], zb, ACT.Exp).then_inc(ev("sb_weights"), 1)
                    ada(2 * h + 1)
                    if h == 1:
                        gate_ln()
                    if h == 2:
                        conv_silu()
                    if h == 4:
                        act.wait_ge(ev("g_scan"), 1)
                        act.activation(gT[:, 6, :], gT[:, 6, :], ACT.Exp).then_inc(ev("g_exp"), 1)
                act.wait_ge(ev("g_T"), 1)
                act.copy(gcol, ps[:, 2, 0:16].rearrange("p (t c) -> p t c", t=TT))
                act.drain().then_inc(ev("gcol_ready"), 1)
                def rstd(n, ready, name, width):
                    act.preload_act_table(ACT.Ln)
                    act.wait_ge(ev(ready), 1)
                    act.activation(stat[:, 24:24 + n], stat[:, 24:24 + n], ACT.Ln, scale=1.0 / width, bias=EPSC)
                    act.drain()
                    act.activation(stat[:, 24:24 + n], stat[:, 24:24 + n], ACT.Exp, scale=-0.5).then_inc(ev(name), 1)
                for h in range(MLH):
                    if h == 2:
                        rstd(8, "sgu_var", "sgu_rstd", SGD)
                    act.wait_ge(ev("ml_m"), h // 2 + 1)
                    if h >= 2:
                        act.wait_ge(ev("ml_p"), h - 1)
                    bb = ps[:, 6, (h % 2) * T:(h % 2 + 1) * T]
                    act.activation(dmt[:, h % 2, 0:T], bb, ACT.Exp, bias=gcol[:, 0, h:h + 1])
                    act.activation(dmt[:, h % 2, T:T + P], bb[:, P:T], ACT.Exp, bias=gcol[:, 1, h:h + 1])
                    act.drain().then_inc(ev("ml_decay"), 1)
                rstd(2, "yc_ss", "yc_rstd", SGW)
                rstd(2, "ya_ss", "ya_rstd", SBW)
                rstd(8, "yb_ss", "yb_rstd", MLD)
                for c in range(KC):
                    act.wait_ge(ev("y_T"), c // 2 + 1)
                    act.activation(hT[:, c, :], ps[:, 4 + c // 2, (c % 2) * T:(c % 2 + 1) * T], ACT.Copy,
                                   scale=cols[:, R_YG + c:R_YG + c + 1])
                act.drain().then_inc(ev("yT_ready"), 1)



                norm(act, "h1_ready", "rstd2")
                chunks_out(act, "h2_T", "h2T_ready")
                part_out(act, m1, ev, 0)
                act.wait_ge(ev("g_shift"), 1)
                for t in range(TT):
                    act.activation(gr[:, t, :], gl[:, t, :], ACT.Exp, accum_out=stat[:, 16 + t:17 + t])
                act.drain().then_inc(ev("g_expd"), 1)
                part_out(act, m1, ev, 1)
                act.wait_ge(ev("e_shift"), 1)
                act.activation(er, er, ACT.Exp).then_inc(ev("e_expd"), 1)
                part_out(act, m1, ev, 2)
                moe_act(act, m1, ev, ps)
                norm(act, "h3_ready", "rstd3")
                chunks_out(act, "h3_T", "h3T_ready", R_PLE)
                act.wait_ge(ev("p_T"), 1)
                act.copy(pT.rearrange("p a b -> p (a b)"), ps[:, 0, :]).then_inc(ev("pT_ready"), 1)
                for n in range(2):
                    for t in range(TT):
                        act.wait_ge(ev("ple_g"), 2 * n + t + 1)
                        act.activation(pg[:, t, n * 512:(n + 1) * 512], ps[:, 4 + 2 * n + t, :], ACT.Sigmoid).then_inc(
                            ev("ple_sig"), 1)
                norm(act, "h4_ready", "rstd4")

            @first.vector
            def _(dve):
                dve.wait_ge(ev("rstd1"), 1)
                dve.memset(gT[:, 7, :], 1.0)
                for t in range(TT):
                    dve.tensor_scalar(hn_tm[:, t, :], x_tm[:, t, :], stat[:, 4 + t:5 + t], None,
                                      ALU.mult).then_inc(ev("hn1"), 1)
                dve.wait_ge(ev("c_exp"), 1)
                dve.tensor_scalar_add(stat[:, 16:24], stat[:, 16:24], 1.0)
                dve.drain()
                dve.reciprocal(stat[:, 16:24], stat[:, 16:24])
                dve.drain()
                dve.tensor_tensor(cact[:], cols[:, R_C:R_C + 8], stat[:, 16:24], ALU.mult)
                dve.drain()
                dve.tensor_copy(crep[:], cact[:].unsqueeze(2).to_broadcast([P, KC, 32])).then_inc(ev("crep_ready"), 1)

                def conv_taps(taps):
                    for k in taps:
                        dve.drain()
                        for j in range(2 * MLH):
                            if k == 0:
                                last = dve.tensor_scalar(qkT[:, j, :], cT[:, j, 0:T], cols96[:, j:j + 1],
                                                         cols96[:, 32 + j:33 + j], ALU.mult, ALU.add)
                            else:
                                last = dve.scalar_tensor_tensor(qkT[:, j, :], cT[:, j, k:k + T],
                                                                cols96[:, 8 * k + j:8 * k + j + 1], qkT[:, j, :],
                                                                ALU.mult, ALU.add)
                    return last

                def gate_scans():
                    dve.wait_ge(ev("f_ln"), 1)
                    dve.scalar_tensor_tensor(gT[:, 1, :], gT[:, 1, :], 0.0, gT[:, 4, :], ALU.min, ALU.subtract)
                    dve.drain()
                    dve.tensor_tensor_scan(gT[:, 2, :], gT[:, 7, :], gT[:, 1, :], 0.0, ALU.mult, ALU.add)
                    dve.drain()
                    dve.tensor_tensor(gT[:, 3, :], gT[:, 0, :], gT[:, 2, :], ALU.subtract)
                    dve.drain()
                    dve.tensor_tensor_scan(gT[:, 4, :], gT[:, 3, :], gT[:, 3, :], 0.0, ALU.max, ALU.max)
                    dve.drain()
                    dve.tensor_scalar(gT[:, 5, :], gT[:, 4, :], -1.0, None, ALU.mult)
                    dve.drain()
                    dve.tensor_tensor(gT[:, 6, :], gT[:, 5, :], gT[:, 2, :], ALU.subtract)
                    dve.drain().then_inc(ev("g_scan"), 1)

                def ada(n):
                    dve.wait_ge(ev("ada_bc"), n + 1)
                    if n:
                        dve.wait_ge(ev("mod_out"), 16 * n)
                    dve.tensor_copy(modst[:], ps[0:1, 3, :]).then_inc(ev("ada_out"), 1)
                for h in range(SBH):
                    dve.wait_ge(ev("sb_ln"), h + 1)
                    if h >= 2:
                        dve.wait_ge(ev("sb_r"), h - 1)
                    dve.scalar_tensor_tensor(spb[:, h % 2, :], ps[:, 4 + h % 2, 0:3 * P], 0.0, spt[:, h % 2, :],
                                             ALU.max, ALU.add).then_inc(ev("sb_softplus"), 1)
                    ada(2 * h)
                    ada(2 * h + 1)
                    if h == 0:
                        dve.wait_ge(ev("proj_evac"), 2 + 3 + 3 + 2 + 8)
                        conv_taps((0, 1))
                    if h == 1:
                        conv_taps((2, 3)).then_inc(ev("conv"), 1)
                    if h == 2:
                        gate_scans()

                dve.wait_ge(ev("proj_all"), 1)
                dve.wait_ge(ev("sgu_in"), 48)
                v4 = uv[:, :, 1, :].rearrange("p t (g c) -> p t g c", g=SGG)
                mean = stat[:, 32:40].rearrange("p (t g) -> p t g", t=TT)
                var = stat[:, 24:32].rearrange("p (t g) -> p t g", t=TT)
                sq = hn_tm[:, 0, 0:TT * SGW].rearrange("p (t g c) -> p t g c", t=TT, g=SGG)
                full = [P, TT, SGG, SGD]
                dve.tensor_reduce(mean, v4, AX.X, ALU.add)
                dve.drain()
                dve.tensor_scalar(mean, mean, 1.0 / SGD, None, ALU.mult)
                dve.drain()
                dve.tensor_tensor(v4, v4, mean.unsqueeze(3).to_broadcast(full), ALU.subtract)
                dve.drain()
                dve.tensor_tensor(sq, v4, v4, ALU.mult)
                dve.drain()
                dve.tensor_reduce(var, sq, AX.X, ALU.add).then_inc(ev("sgu_var"), 1)
                dve.wait_ge(ev("sgu_rstd"), 1)
                dve.tensor_tensor(v4, v4, var.unsqueeze(3).to_broadcast(full), ALU.mult)
                v3 = uv[:, :, 1, :]
                dve.drain()
                dve.tensor_tensor(v3, v3, lnb[:, 0:1, :].to_broadcast([P, TT, SGW]), ALU.mult)
                dve.drain()
                dve.tensor_tensor(v3, v3, lnb[:, 1:2, :].to_broadcast([P, TT, SGW]), ALU.add).then_inc(ev("sgu_v"), 1)
                dve.wait_ge(ev("sgw_T"), 1)
                dve.tensor_copy(sgwT.rearrange("p g t -> p (g t)"), ps[:, 3, :])
                dve.drain()
                dve.memset(sgwT[64:P, :, 0:64], 0.0).then_inc(ev("sgw_ready"), 1)

                for h in range(MLH):
                    dve.wait_ge(ev("ml_s"), h + 1)
                    dve.wait_ge(ev("ml_masked"), h + 1)
                    if h >= 2:
                        dve.wait_ge(ev("ml_y"), h - 1)
                    dve.scalar_tensor_tensor(spb[:, h % 2, :], ps[:, 4 + h % 2, 0:3 * P], MLD ** -0.5,
                                             dmt[:, h % 2, :], ALU.mult, ALU.mult).then_inc(ev("ml_p"), 1)

                def sumsq(dst, src, junk, shape3):
                    dve.tensor_tensor(junk, src, src, ALU.mult)
                    dve.drain()
                    return dve.tensor_reduce(dst, junk, AX.X, ALU.add)

                dve.wait_ge(ev("sgu_mix"), 1)
                mixed = ps[:, 2, :].rearrange("p (t g c) -> p t g c", t=TT, g=SGG)
                bcol = cols[:, R_SGB:R_SGB + SGG].unsqueeze(1).unsqueeze(3).to_broadcast(full)
                yc = hn_tm[:, :, SBW + MLW:D]
                yc4 = yc.rearrange("p t (g c) -> p t g c", g=SGG)
                for t in range(TT):
                    dve.tensor_tensor(sq[:, t], mixed[:, t], bcol[:, t], ALU.add)
                dve.drain()
                dve.tensor_tensor(yc, uv[:, :, 0, :], sq.rearrange("p t g c -> p t (g c)"), ALU.mult)
                dve.drain()
                sumsq(stat[:, 24:26], yc, hn_tm[:, :, 0:SGW], None).then_inc(ev("yc_ss"), 1)
                dve.wait_ge(ev("yc_rstd"), 1)
                for t in range(TT):
                    dve.tensor_scalar(yc[:, t, :], yc[:, t, :], stat[:, 24 + t:25 + t], None, ALU.mult)
                dve.drain()
                dve.wait_ge(ev("sb_y"), SBH)
                ya = hn_tm[:, :, 0:SBW]
                for t in range(TT):
                    dve.tensor_copy(ya[:, t, :], ps[:, t, 0:SBW])
                dve.drain()
                sumsq(stat[:, 24:26], ya, hn_tm[:, :, SBW:SBW + MLW], None).then_inc(ev("ya_ss"), 1)
                dve.wait_ge(ev("ya_rstd"), 1)
                for t in range(TT):
                    dve.tensor_scalar(ya[:, t, :], ya[:, t, :], stat[:, 24 + t:25 + t], None, ALU.mult)
                dve.drain().then_inc(ev("ya_done"), 1)
                dve.wait_ge(ev("ml_y"), MLH)
                hb = hn_tm[:, :, SBW:SBW + MLW].rearrange("p t (h d) -> p t h d", h=MLH)
                den = stat[:, 40:48].rearrange("p (t h) -> p t h", t=TT)
                num = [ps[:, NUM[t], 0:MLH * (MLD + 1)].rearrange("p (h d) -> p h d", h=MLH) for t in range(TT)]
                for t in range(TT):
                    dve.tensor_copy(den[:, t, :], num[t][:, :, MLD])
                dve.drain()
                dve.scalar_tensor_tensor(den, den, -1.0, den, ALU.mult, ALU.max)
                dve.drain()
                dve.tensor_tensor(den, den, gcol[:, :, MLH:2 * MLH], ALU.max)
                dve.drain()
                dve.reciprocal(stat[:, 40:48], stat[:, 40:48])
                dve.drain()
                for t in range(TT):
                    dve.tensor_tensor(hb[:, t], num[t][:, :, 0:MLD], den[:, t, :].unsqueeze(2).to_broadcast([P, MLH, MLD]),
                                      ALU.mult)
                dve.drain()
                for t in range(TT):
                    dve.tensor_tensor(scratch[:, t, 0:MLW], hn_tm[:, t, SBW:SBW + MLW], hn_tm[:, t, SBW:SBW + MLW], ALU.mult)
                dve.drain()
                for t in range(TT):
                    dve.tensor_reduce(stat[:, 24 + 4 * t:28 + 4 * t],
                                      scratch[:, t, 0:MLW].rearrange("p (h d) -> p h d", h=MLH), AX.X, ALU.add)
                dve.drain().then_inc(ev("yb_ss"), 1)
                dve.wait_ge(ev("yb_rstd"), 1)
                for t in range(TT):
                    dve.tensor_tensor(hb[:, t], hb[:, t],
                                      stat[:, 24 + 4 * t:28 + 4 * t].unsqueeze(2).to_broadcast([P, MLH, MLD]), ALU.mult)
                dve.drain()
                dve.tensor_tensor(hn_tm[:, :, SBW:SBW + MLW], hn_tm[:, :, SBW:SBW + MLW], ob, ALU.mult)
                dve.drain().then_inc(ev("y_ready"), 1)
                for t in range(TT):
                    for n in range(2):
                        dve.wait_ge(ev("o_proj"), 2 * n + t + 1)
                        dve.tensor_tensor(x_tm[:, t, n * 512:(n + 1) * 512], ps[:, 2 * n + t, :],
                                          x_tm[:, t, n * 512:(n + 1) * 512], ALU.add)
                dve.drain().then_inc(ev("h1_ready"), 1)

                dve.wait_ge(ev("n2_in"), 16)
                scale_rows(dve, "rstd2", bc1)
                dve.drain().then_inc(ev("h2_ready"), 1)
                dve.memset(gl[:, :, 4:8], -BIG)
                dve.memset(gv, FAR)
                dve.wait_ge(ev("rw_in"), 64)
                for t in range(TT):
                    dve.wait_ge(ev("router"), t + 1)
                    dve.tensor_tensor(gl[:, t, 0:4], ps[:, 4 + t, 0:4], rb[:, 0:4], ALU.add)
                    dve.tensor_tensor(el[:, t, :], ps[:, 4 + t, 4:36], rb[:, 4:36], ALU.add)
                dve.drain()
                for t in range(TT):
                    dve.max(v8[:, t, :], gl[:, t, :])
                dve.drain()
                dve.tensor_copy(gv[:, :, 0:1], v8[:, :, 0:1])
                dve.drain()
                for t in range(TT):
                    dve.match_replace(gr[:, t, :], gv[:, t, :], gl[:, t, :], -FAR)
                dve.drain()
                dve.tensor_tensor(gm, gr[:, :, 0:4], gl[:, :, 0:4], ALU.not_equal)
                dve.drain()
                dve.tensor_tensor(gl, gl, v8[:, :, 0:1].to_broadcast([P, TT, 8]), ALU.subtract)
                dve.tensor_scalar(gm, gm, BIG, -BIG, ALU.mult, ALU.add)
                dve.drain().then_inc(ev("g_shift"), 1)
                e4 = el.rearrange("p t (g e) -> p t g e", g=4)
                for t in range(TT):
                    dve.tensor_tensor(e4[:, t], e4[:, t], gm[:, t, :].unsqueeze(2).to_broadcast([P, 4, 8]), ALU.add)
                dve.drain()
                for t in range(TT):
                    dve.max(v8[:, t, :], el[:, t, :])
                dve.drain()
                dve.tensor_copy(gv[:, :, 0:2], v8[:, :, 0:2])
                dve.drain()
                for t in range(TT):
                    dve.match_replace(er[:, t, :], gv[:, t, :], el[:, t, :], -FAR)
                dve.drain()
                dve.tensor_tensor(m1.mask, er, el, ALU.not_equal)
                dve.drain()
                dve.tensor_tensor(er, el, v8[:, :, 0:1].to_broadcast([P, TT, 32]), ALU.subtract).then_inc(ev("e_shift"), 1)
                dve.wait_ge(ev("e_expd"), 1)
                dve.wait_ge(ev("g_expd"), 1)
                dve.tensor_tensor(m1.gate, er, m1.mask, ALU.mult)
                dve.drain()
                dve.tensor_reduce(stat[:, 18:20], m1.gate, AX.X, ALU.add)
                dve.drain()
                dve.tensor_tensor(stat[:, 18:20], stat[:, 18:20], stat[:, 16:18], ALU.mult)
                dve.drain()
                dve.reciprocal(stat[:, 18:20], stat[:, 18:20])
                dve.drain()
                for t in range(TT):
                    dve.tensor_scalar(m1.gate[:, t, :], m1.gate[:, t, :], stat[:, 18 + t:19 + t], None, ALU.mult)
                route_lists_dve(dve, m1, ev, ps)
                moe_dve(dve, m1, ev, ps)
                dve.wait_ge(ev("a_acc"), 1)
                for t in range(TT):
                    for n in range(2):
                        xx = x_tm[:, t, n * 512:(n + 1) * 512]
                        dve.tensor_tensor(xx, ps[:, 2 * t + n, :], xx, ALU.add)
                dve.drain().then_inc(ev("h3_ready"), 1)
                scale_rows(dve, "rstd3")
                dve.drain().then_inc(ev("hn3_ready"), 1)
                for n in range(2):
                    for t in range(TT):
                        dve.wait_ge(ev("ple_sig"), 2 * n + t + 1)
                        dve.wait_ge(ev("ple_p"), 2 * n + t + 1)
                        g, xx = pg[:, t, n * 512:(n + 1) * 512], x_tm[:, t, n * 512:(n + 1) * 512]
                        dve.tensor_tensor(g, ps[:, 2 * n + t, :], g, ALU.mult)
                        dve.drain()
                        dve.tensor_tensor(xx, xx, g, ALU.add)
                dve.drain().then_inc(ev("h4_ready"), 1)
                dve.wait_ge(ev("fg_in"), 16)
                scale_rows(dve, "rstd4", bc1, x_tm)
                dve.drain().then_inc(ev("x1_ready"), 1)

            @first.tensor
            def _(pe):
                pe.wait_ge(ev("consts"), 1)
                pe.wait_ge(ev("rows_in"), 16 * 9)
                pe.transpose(ps[:, 7, 0:N_ROWS], rows[:], ident[0:N_ROWS, 0:N_ROWS])
                pe.transpose(ps[0:MLD, 7, 64:104], rows96[:], ident[0:40, 0:40]).then_inc(ev("rows_T"), 1)

                pe.wait_ge(ev("hn1"), 2)
                transposes(pe, hn_tm, 0, "h_T")
                pe.wait_ge(ev("hT_ready"), 1)

                g = 0
                def group(m, n, lhs, rhs):
                    nonlocal g
                    if g >= 4:
                        pe.wait_ge(ev("proj_evac"), g - 3)
                    for k in range(KC):
                        last = pe.matmul(ps[0:m, g % 4, 0:n], lhs(k), rhs(k), start=(k == 0), stop=(k == KC - 1))
                    last.then_inc(ev("proj"), 1)
                    g += 1
                    return last
                pe.wait_ge(ev("gatew_in"), 48)
                for j in range(2):
                    group(MLH, T, lambda k: gate_w[:, k, j * MLH:(j + 1) * MLH], lambda k: hT[:, k, :])
                for i, (kind, m) in enumerate([("T", P), ("T", P), ("tok", 0), ("T", MLD), ("T", MLD), ("tok", 0), ("tok", 0),
                                               ("tok", 0)]):
                    w = loads[L_IN[i]]["dst"]
                    arrived(pe, L_IN[i])
                    if kind == "T":
                        for c in range(384 // m):
                            last = group(m, T, lambda k: w[:, k, c * m:(c + 1) * m], lambda k: hT[:, k, :])
                    else:
                        n = w.shape[2]
                        for t in range(TT):
                            last = group(P, n, lambda k: hT[:, k, t * P:(t + 1) * P], lambda k: w[:, k, :])

                pe.wait_ge(ev("proj_all"), 1)
                pe.wait_ge(ev("crep_ready"), 1)
                pe.wait_ge(ev("bada_in"), 16)

                def ada(n):
                    w = loads[L_ADA[n]]["dst"]
                    arrived(pe, L_ADA[n])
                    if n >= 1:
                        pe.wait_ge(ev("ada_row"), n)
                    for k in range(2):
                        for j in range(4):
                            last = pe.matmul(ps[32 * j:32 * j + 32, 2, :], crep[:, 2 * j + k, :], w[:, 2 * j + k, :],
                                      start=(k == 0), stop=(k == 1))
                    last.then_inc(ev("ada_part"), 1)
                    pe.wait_ge(ev("ada_row"), n + 1)
                    if n >= 1:
                        pe.wait_ge(ev("ada_out"), n)
                    pe.matmul(ps[0:1, 3, :], selq[:, 0:1], adap[:], start=True, stop=False)
                    pe.matmul(ps[0:1, 3, :], ident[0:12, n:n + 1], bada[:], start=False, stop=True).then_inc(ev("ada_bc"), 1)

                def sb_z(h):
                    b, c = SBD * (h % 2), h // 2
                    bank = ps[:, 4 + h % 2, :]
                    if h >= 2:
                        pe.wait_ge(ev("sb_weights"), h - 1)
                    kk, qq = kaT[b:b + SBD, c, :], qaT[b:b + SBD, c, :]
                    pe.matmul(bank[:, 0:T], kk[:, 0:P], qq, start=True, stop=True)
                    pe.matmul(bank[:, T:T + P], kk[:, P:T], qq[:, P:T], start=False, stop=True,
                              skip_group_check=True).then_inc(ev("sb_z"), 1)
                def sb_r(h):
                    pe.wait_ge(ev("sb_masked"), 2 * h + 1)
                    bank, s = ps[:, 4 + h % 2, :], spb[:, h % 2, :]
                    kw = dict(start=False, stop=True, skip_group_check=True)
                    pe.matmul(bank[:, 0:T], ntri[:], s[:, 0:T], **kw)
                    pe.matmul(bank[:, P:T], nones[:], s[:, T:T + P], **kw)
                    pe.matmul(bank[:, T:T + P], ntri[:], s[:, T:T + P], **kw).then_inc(ev("sb_r"), 1)
                def sb_y(h):
                    pe.wait_ge(ev("sb_masked"), 2 * h + 2)
                    a = amt[:, h % 2, :]
                    o = slice(h * SBD, (h + 1) * SBD)
                    pe.matmul(ps[:, 0, o], a[:, 0:P], va[:, 0, o], start=True, stop=True)
                    pe.matmul(ps[:, 1, o], a[:, P:T], va[:, 0, o], start=True, stop=False)
                    pe.matmul(ps[:, 1, o], a[:, T:T + P], va[:, 1, o], start=False, stop=True).then_inc(ev("sb_y"), 1)
                sb_z(0)
                for h in range(SBH):
                    if h + 1 < SBH:
                        sb_z(h + 1)
                    ada(2 * h)
                    sb_r(h)
                    ada(2 * h + 1)
                    sb_y(h)

                pe.wait_ge(ev("g_exp"), 1)
                pe.wait_ge(ev("ada_row"), 12)
                for t in range(TT):
                    for j, r in enumerate((3, 6)):
                        last = pe.transpose(ps[:, 2, 8 * t + MLH * j:8 * t + MLH * (j + 1)], gT[:, r, t * P:(t + 1) * P],
                                            ident[0:MLH, 0:MLH])
                last.then_inc(ev("g_T"), 1)
                pe.wait_ge(ev("sgu_in"), 48)
                pe.wait_ge(ev("ada_out"), 12)
                for gg in range(SGG):
                    last = pe.transpose(ps[:, 3, gg * P:(gg + 1) * P], sgw[:, gg, :], ident[:])
                last.then_inc(ev("sgw_T"), 1)
                pe.wait_ge(ev("qk_ready"), 1)
                def ml_m(pair):
                    if pair:
                        pe.wait_ge(ev("ml_decay"), 2)
                    for h in (2 * pair, 2 * pair + 1):
                        last = pe.matmul(ps[:, 6, (h % 2) * T:(h % 2 + 1) * T], sel4[:, h, :], gT[:, 5, :],
                                         start=True, stop=True)
                    last.then_inc(ev("ml_m"), 1)
                def ml_s(h):
                    bank = ps[:, 4 + h % 2, :]
                    if h < 2:
                        pe.wait_ge(ev("sb_weights"), SBH)
                    else:
                        pe.wait_ge(ev("ml_p"), h - 1)
                    kk, qq = qkT[:, MLH + h, :], qkT[:, h, :]
                    pe.matmul(bank[:, 0:T], kk[:, 0:P], qq, start=True, stop=True)
                    pe.matmul(bank[:, T:T + P], kk[:, P:T], qq[:, P:T], start=False, stop=True,
                              skip_group_check=True).then_inc(ev("ml_s"), 1)
                ml_m(0)
                for h in range(2):
                    ml_s(h)
                pe.wait_ge(ev("sgw_ready"), 1)
                pe.wait_ge(ev("sgu_v"), 1)
                for t in range(TT):
                    for gg in range(SGG):
                        c = t * SGW + gg * SGD
                        last = pe.matmul(ps[:, 2, c:c + SGD], sgwT[:, gg, :], uv[:, t, 1, gg * SGD:(gg + 1) * SGD],
                                         start=True, stop=True)
                last.then_inc(ev("sgu_mix"), 1)
                def ml_y(h):
                    a = spb[:, h % 2, :]
                    o = slice(h * (MLD + 1), (h + 1) * (MLD + 1))
                    pe.wait_ge(ev("ml_p"), h + 1)
                    pe.matmul(ps[:, NUM[0], o], a[:, 0:P], vba[:, 0, h, :], start=True, stop=True)
                    pe.matmul(ps[:, NUM[1], o], a[:, P:T], vba[:, 0, h, :], start=True, stop=False)
                    pe.matmul(ps[:, NUM[1], o], a[:, T:T + P], vba[:, 1, h, :], start=False, stop=True).then_inc(ev("ml_y"), 1)
                for h in range(MLH):
                    ml_y(h)
                    if h == 0:
                        ml_m(1)
                    if h + 2 < MLH:
                        ml_s(h + 2)
                pe.wait_ge(ev("y_ready"), 1)
                transposes(pe, hn_tm, 4, "y_T")
                pe.wait_ge(ev("yT_ready"), 1)
                for n in range(2):
                    w = loads[L_OUT[n]]["dst"]
                    arrived(pe, L_OUT[n])
                    for t in range(TT):
                        for k in range(KC):
                            last = pe.matmul(ps[:, 2 * n + t, :], hT[:, k, t * P:(t + 1) * P], w[:, k, :],
                                             start=(k == 0), stop=(k == KC - 1))
                        last.then_inc(ev("o_proj"), 1)

                pe.wait_ge(ev("h2_ready"), 1)
                transposes(pe, hn_tm, 4, "h2_T")
                pe.wait_ge(ev("h2T_ready"), 1)
                pe.wait_ge(ev("rw_in"), 64)
                for t in range(TT):
                    for k in range(KC):
                        last = pe.matmul(ps[:, 4 + t, 0:36], hT[:, k, t * P:(t + 1) * P], rw[:, k, :], start=(k == 0),
                                         stop=(k == KC - 1))
                    last.then_inc(ev("router"), 1)
                for b in range(4):
                    pe.matmul(ps[:, b, :], zero[:], hn_tm[:, 0, 0:512], start=True, stop=True)
                route_lists_pe(pe, m1, ev, ps)
                moe_pe(pe, m1, ev, ps)
                pe.wait_ge(ev("hn3_ready"), 1)
                pe.wait_ge(ev("p_in"), 16)
                for c in range(2):
                    for t in range(TT):
                        last = pe.transpose(ps[:, 0, c * T + t * P:c * T + (t + 1) * P], p_tm[:, t, c * P:(c + 1) * P], ident[:])
                last.then_inc(ev("p_T"), 1)
                transposes(pe, hn_tm, 4, "h3_T")
                pe.wait_ge(ev("h3T_ready"), 1)
                pe.wait_ge(ev("pT_ready"), 1)
                for n in range(2):
                    arrived(pe, L_PLE[n])
                    w = loads[L_PLE[n]]["dst"]
                    for t in range(TT):
                        for k in range(KC):
                            last = pe.matmul(ps[:, 4 + 2 * n + t, :], hT[:, k, t * P:(t + 1) * P], w[:, k, :], start=(k == 0),
                                             stop=(k == KC - 1))
                        last.then_inc(ev("ple_g"), 1)
                arrived(pe, L_PROJ)
                w = loads[L_PROJ]["dst"]
                for n in range(2):
                    for t in range(TT):
                        for k in range(2):
                            last = pe.matmul(ps[:, 2 * n + t, :], pT[:, k, t * P:(t + 1) * P], w[:, k, n * 512:(n + 1) * 512],
                                             start=(k == 0), stop=(k == 1))
                        last.then_inc(ev("ple_p"), 1)

        renew()
        nc.all_engine_barrier()

        with nc.Block() as second:
            @second.sync
            def _(sp):
                def small(dst, src, name="c2_in"):
                    sp.dma_start(dst, src).then_inc(ev(name), 16)
                def vec(v, n=D):
                    return v.to_broadcast([P, n])
                small(bcn[:, 0:D], vec(A["norm1_g_2"]), "n3_in")
                small(bcn[:, D:2 * D], vec(mod[:, D:2 * D]), "n3_in")
                small(bcs, vec(mod[:, 0:D]), "n3_in")
                dw = A["conv_dw_2"][0].rearrange("k (c p) -> (k c) p", p=P)
                for j in range(2):
                    small(drows[:, j, :], dw[124 * j:124 * j + 124, :])
                for j, nm in enumerate(("conv_dw_b_2", "conv_ln_g_2", "conv_ln_b_2")):
                    small(crows[KC * j:KC * j + KC, :], A[nm][0].rearrange("(c p) -> c p", p=P))
                small(qg[:, 0, :], vec(A["q_norm_g_2"], AD))
                small(qg[:, 1, :], vec(A["k_norm_g_2"], AD))
                small(subg, vec(A["subln_g_2"], 2 * AD))
                for j, nm in enumerate(("lambda_q1_2", "lambda_k1_2", "lambda_q2_2", "lambda_k2_2")):
                    small(lqk[:, j, :], vec(A[nm], AD))
                for t in range(TT):
                    small(posi[:, t:t + 1], A["positions_2"][0, t * P:(t + 1) * P].rearrange("(p a) -> p a", a=1))
                for i in (L_A + L_QKV)[RING:]:
                    load(sp, i)
                for i in L_G:
                    load(sp, i)
                sp.wait_ge(ev("at_s"), AH)
                sp.dma_start(bcu[:, 0, :], vec(A["b_pw2_2"])).then_inc(ev("bcu_in"), 16)
                sp.dma_start(bcu[:, 1, :], vec(mod[:, 2 * D:3 * D])).then_inc(ev("bcu_in"), 16)
                for i in L_PW + L_O2 + [L_SGU, L_SD]:
                    load(sp, i)
                moe_sp(sp, m2, ev)
                sp.wait_ge(ev("h5_ready"), 1)
                small(bc2[:, 0, :], vec(A["norm2_g_2"]), "n4_in")
                small(bc2[:, 1, :], vec(mod[:, 4 * D:5 * D]), "n4_in")
                small(bc2[:, 2, :], vec(mod[:, 3 * D:4 * D]), "n4_in")
                small(rw2, A["w_router_2"][0].rearrange("(k p) n -> p k n", p=P), "rw2_in")
                small(rb2, vec(A["router_bias_2"], 64), "rw2_in")
                sp.wait_ge(ev("h6_ready"), 1)
                sp.dma_start(bc2[:, 0, :], vec(mod[:, 5 * D:6 * D])).then_inc(ev("g2_in"), 16)
                moe_sp(sp, m2, ev, False)
                for t in range(TT):
                    for n in range(2):
                        sp.wait_ge(ev("out_ready"), 2 * t + n + 1)
                        sp.dma_start(out[0].rearrange("(t p) d -> p t d", p=P)[:, t, n * 512:(n + 1) * 512],
                                     out_tm[:, t, n * 512:(n + 1) * 512]).then_inc(ev("stored"), 16)
                sp.wait_ge(ev("stored"), 64)

            @second.gpsimd
            def _(pool):
                pool.memset(uT[:, :, 0:UPAD], 0.0)
                pool.memset(cmask, 0.0)
                for j in range(ROT):
                    pool.memset(invf[:, j:j + 1], float(np.float32(THETA) ** np.float32(-j / ROT)))
                pool.drain()
                blk = cmask.rearrange("p (a c) -> p a c", a=3)[:, 0:3:2, :]
                pool.affine_select(out=blk, in_=blk, compare_op=ALU.is_ge, fill=-1e30, base=0,
                                   pattern=[[0, 2], [-1, P]], channel_multiplier=1)
                pool.drain().then_inc(ev("c2_consts"), 1)
                pool.wait_ge(ev("h6_ready"), 1)
                moe_pool(pool, m2, ev)

            @second.scalar
            def _(act):
                norm(act, None, "rstd5")
                act.wait_ge(ev("dw_T"), 1)
                act.copy(dwc.rearrange("p c k -> p k c"), ps[:, 0, 0:248].rearrange("p (k c) -> p k c", c=KC))
                act.copy(cc, ps[:, 0, 256:280])
                act.drain().then_inc(ev("dw_ready"), 1)
                chunks_out(act, "h5_T", "h5T_ready")
                for c in range(KC):
                    act.wait_ge(ev("u_proj"), 2 * c + 2)
                    act.activation(gc_c[:, c, :], ps[:, 2 * (c % 2) + 1, 0:T], ACT.Sigmoid)
                    act.copy(uT[:, c, UPAD:], ps[:, 2 * (c % 2), 0:T])
                    act.drain().then_inc(ev("u_out"), 1)
                for g in range(12):
                    act.wait_ge(ev("qkv"), g + 1)
                    dst = (q_tm, k_tm, v_tm)[g // 4]
                    act.copy(dst[:, g % 2, (g % 4) // 2 * 512:(g % 4) // 2 * 512 + 512], ps[:, 4 + g % 4, :]).then_inc(
                        ev("qkv_out"), 1)
                    if g == 3:
                        act.drain()
                        act.activation(qk_sq, q_tm, ACT.Square).then_inc(ev("qk_sq"), 1)
                act.drain()
                act.wait_ge(ev("ang"), 1)
                act.activation(rot.rearrange("p a t j -> p (a t j)"), rot.rearrange("p a t j -> p (a t j)"),
                               ACT.Sin).then_inc(ev("rot_ready"), 1)
                act.wait_ge(ev("lam_dot"), 1)
                act.activation(st2[:, 64:66], st2[:, 64:66], ACT.Exp).then_inc(ev("lam_exp"), 1)
                for j in range(2):
                    s32 = st2[:, 32 * j:32 * j + 32]
                    act.preload_act_table(ACT.Ln)
                    act.wait_ge(ev("qk_ss"), j + 1)
                    if j == 0:
                        act.activation(qk_sq, k_tm[:], ACT.Square).then_inc(ev("qk_sq"), 1)
                    act.activation(s32, s32, ACT.Ln, scale=1.0 / AD, bias=EPSC)
                    act.drain()
                    act.activation(s32, s32, ACT.Exp, scale=-0.5).then_inc(ev("qk_rstd"), 1)
                for j, dst in enumerate((qT, kT)):
                    for c in range(KC):
                        act.wait_ge(ev("qk_T"), 4 * j + c // 2 + 1)
                        act.copy(dst[:, c, :], ps[:, 4 + c // 2, (c % 2) * T:(c % 2 + 1) * T])
                    act.drain().then_inc(ev("qkT_ready"), 1)
                def weights(h):
                    act.wait_ge(ev("at_max"), h + 1)
                    for mp in range(2):
                        for t, (a, b) in enumerate(((0, P), (P, 3 * P))):
                            v = pbuf[:, h % 2, mp, a:b]
                            j = 4 * (h % 2) + 2 * mp + t
                            act.activation(v, v, ACT.Exp, scale=AD ** -0.5, bias=st2[:, 72 + j:73 + j],
                                           accum_out=st2[:, 80 + j:81 + j])
                    act.drain().then_inc(ev("at_p"), 1)
                def gate_out(g):
                    act.wait_ge(ev("gates2"), g + 1)
                    dst = (gc, ga)[g // 4]
                    act.copy(dst[:, g % 2, (g % 4) // 2 * 512:(g % 4) // 2 * 512 + 512], ps[:, g % 2, :]).then_inc(
                        ev("gates2_out"), 1)
                weights(0)
                act.wait_ge(ev("cen"), 1)
                act.activation(gc_c, convT, ACT.Square).then_inc(ev("c_sq"), 1)
                for h in range(AH):
                    if h + 1 < AH:
                        weights(h + 1)
                    if h == 0:
                        act.wait_ge(ev("c_ss"), 1)
                        act.activation(lnm, ps[:, 1, 0:T], ACT.Ln, scale=1.0 / D, bias=EPSC)
                        act.drain()
                        act.activation(lnm, lnm, ACT.Exp, scale=-0.5).then_inc(ev("c_rstd"), 1)
                    gate_out(h)
                    act.wait_ge(ev("at_T"), h + 1)
                    act.copy(aT, ps[:, 2, 0:3 * P]).then_inc(ev("at_Te"), 1)
                    if h == 0:
                        act.wait_ge(ev("c_norm"), 1)
                        for c in range(KC):
                            act.activation(convT[:, c, :], convT[:, c, :], ACT.Silu, scale=cc[:, KC + c:KC + c + 1],
                                           bias=cc[:, 2 * KC + c:2 * KC + c + 1])
                        act.drain().then_inc(ev("s_ready"), 1)
                act.wait_ge(ev("o_ss"), 1)
                act.activation(st2[:, 0:16], st2[:, 0:16], ACT.Ln, scale=1.0 / (2 * AD), bias=EPSC)
                act.drain()
                act.activation(st2[:, 0:16], st2[:, 0:16], ACT.Exp, scale=-0.5).then_inc(ev("o_rstd"), 1)
                for gt in (ga, gc):
                    act.activation(gt, gt, ACT.Sigmoid).then_inc(ev("gates_sig"), 1)
                chunks_out(act, "y2_T", "y2T_ready")
                norm(act, "h5_ready", "rstd6")
                chunks_out(act, "h6_T", "h6T_ready")
                part_out(act, m2, ev, 0)
                for t in range(TT):
                    act.wait_ge(ev("router2"), t + 1)
                    act.activation(scr[:, t, :], ps[:, t, 0:64], ACT.Sigmoid).then_inc(ev("scores"), 1)
                part_out(act, m2, ev, 1)
                for k in range(2):
                    act.wait_ge(ev("sh_gu"), k + 1)
                    act.activation(shs[:, k, :], ps[:, 4 + k, 0:T], ACT.Silu).then_inc(ev("sh_silu"), 1)
                part_out(act, m2, ev, 2)
                moe_act(act, m2, ev, ps)

            @second.vector
            def _(dve):
                def modulated(name, bc, sc, sh):
                    dve.scalar_tensor_tensor(sc, sc, 1.0, bc, ALU.add, ALU.mult)
                    dve.drain()
                    scale_rows(dve, name, sc)
                    dve.drain()
                    for t in range(TT):
                        dve.tensor_tensor(hn_tm[:, t, :], hn_tm[:, t, :], sh, ALU.add)
                dve.wait_ge(ev("n3_in"), 48)
                modulated("rstd5", bcn[:, 0:D], bcn[:, D:2 * D], bcs)
                dve.drain().then_inc(ev("hn5_ready"), 1)
                dve.wait_ge(ev("c2_in"), 16 * 14)
                dve.wait_ge(ev("c2_consts"), 1)
                posf = st2[:, 66:68]
                dve.tensor_copy(posf, posi[:])
                dve.drain()
                for t in range(TT):
                    dve.tensor_scalar(rot[:, 1, t, :], invf[:], posf[:, t:t + 1], None, ALU.mult)
                dve.drain()
                turns = st2[:, 96:112].rearrange("p (t j) -> p t j", t=TT)
                turni = roti[:].rearrange("p (t j) -> p t j", t=TT)
                C1 = 6.28125
                C2 = float(np.float32(TWO_PI - C1))
                for j, quarter in ((0, 0.25), (1, 0.0)):
                    dve.tensor_scalar(turns, rot[:, 1], 1.0 / TWO_PI, quarter, ALU.mult, ALU.add)
                    dve.drain()
                    dve.tensor_copy(turni, turns)
                    dve.drain()
                    dve.tensor_copy(turns, turni)
                    dve.drain()
                    dve.scalar_tensor_tensor(rot[:, j], turns, -C1, rot[:, 1], ALU.mult, ALU.add)
                    dve.drain()
                    dve.scalar_tensor_tensor(rot[:, j], turns, -C2, rot[:, j], ALU.mult, ALU.add)
                    dve.drain()
                    if j == 0:
                        dve.tensor_scalar(rot[:, j], rot[:, j], math.pi / 2, None, ALU.add)
                        dve.drain()
                flat = rot.rearrange("p a t j -> p (a t j)")
                dve.tensor_scalar(flat, flat, 3.1415925, -3.1415925, ALU.min, ALU.max).then_inc(ev("ang"), 1)
                lp = st2[:, 64:66]
                for j in range(2):
                    dve.tensor_tensor(lqk[:, 2 * j, :], lqk[:, 2 * j, :], lqk[:, 2 * j + 1, :], ALU.mult)
                    dve.drain()
                    dve.tensor_reduce(lp[:, j:j + 1], lqk[:, 2 * j, :], AX.X, ALU.add)
                dve.tensor_scalar(subg, subg, 1.0 - LAMBDA0, None, ALU.mult)
                dve.drain().then_inc(ev("lam_dot"), 1)
                def conv(*chunks):
                    dve.wait_ge(ev("u_out"), chunks[-1] + 1)
                    for c in chunks:
                        dve.tensor_tensor(uT[:, c, UPAD:], uT[:, c, UPAD:], gc_c[:, c, :], ALU.mult)
                    for k in range(TAPS):
                        dve.drain()
                        for c in chunks:
                            if k == 0:
                                dve.tensor_scalar(convT[:, c, :], uT[:, c, 0:T], dwc[:, c, 0:1], cc[:, c:c + 1],
                                                  ALU.mult, ALU.add)
                            else:
                                dve.scalar_tensor_tensor(convT[:, c, :], uT[:, c, k:k + T], dwc[:, c, k:k + 1],
                                                         convT[:, c, :], ALU.mult, ALU.add)

                def qk_norm(j, x):
                    dve.wait_ge(ev("qkv_out"), 4 * j + 4)
                    xs = x[:].rearrange("p t (g d) -> p (t g) d", d=AD)
                    s32 = st2[:, 32 * j:32 * j + 32]
                    dve.wait_ge(ev("qk_sq"), j + 1)
                    dve.tensor_reduce(s32, qk_sq.rearrange("p t (g d) -> p (t g) d", d=AD), AX.X, ALU.add).then_inc(
                        ev("qk_ss"), 1)
                    dve.wait_ge(ev("qk_rstd"), j + 1)
                    dve.tensor_tensor(xs, xs, s32.unsqueeze(2).to_broadcast([P, 32, AD]), ALU.mult)
                    dve.drain()
                    dve.tensor_tensor(xs, xs, qg[:, j:j + 1, :].to_broadcast([P, 32, AD]), ALU.mult)
                    dve.wait_ge(ev("rot_ready"), 1)
                    dve.drain()
                    g4 = gc.rearrange("p t (r g j) -> p t r g j", g=16, j=ROT)
                    for t in range(TT):
                        xt = x[:, t, :].rearrange("p (g d) -> p g d", d=AD)
                        x1, x2 = xt[:, :, 0:ROT], xt[:, :, ROT:2 * ROT]
                        cos, sin = (rot[:, r, t:t + 1, :].to_broadcast([P, 16, ROT]) for r in range(2))
                        for r, (a, b) in enumerate(((x1, cos), (x2, sin), (x2, cos), (x1, sin))):
                            dve.tensor_tensor(g4[:, t, r], a, b, ALU.mult)
                        dve.drain()
                        dve.tensor_tensor(x1, g4[:, t, 0], g4[:, t, 1], ALU.subtract)
                        dve.tensor_tensor(x2, g4[:, t, 2], g4[:, t, 3], ALU.add)
                    dve.drain().then_inc(ev("k2_ready" if j else "q2_ready"), 1)

                dve.wait_ge(ev("dw_ready"), 1)
                conv(0, 1)
                conv(2, 3)
                conv(4, 5)
                conv(6, 7)
                dve.drain().then_inc(ev("conv2"), 1)
                qk_norm(0, q_tm)
                qk_norm(1, k_tm)
                dve.wait_ge(ev("lam_exp"), 1)
                nlam = st2[:, 68:69]
                dve.tensor_tensor(nlam, lp[:, 1:2], lp[:, 0:1], ALU.subtract)
                dve.drain()
                dve.tensor_scalar(nlam, nlam, -LAMBDA0, None, ALU.add)
                dve.drain()

                def maxima(h):
                    dve.wait_ge(ev("at_s"), h + 1)
                    for mp in range(2):
                        for t, (a, b) in enumerate(((0, P), (P, 3 * P))):
                            j = 4 * (h % 2) + 2 * mp + t
                            dve.tensor_tensor_reduce(out=pbuf[:, h % 2, mp, a:b], in0=ps[:, 4 + 2 * (h % 2) + mp, a:b],
                                                     in1=cmask[:, a:b], scale=1.0, scalar=-3e38, op0=ALU.add, op1=ALU.max,
                                                     accum_out=st2[:, 72 + j:73 + j])
                    j = 72 + 4 * (h % 2)
                    dve.drain()
                    dve.tensor_scalar(st2[:, j:j + 4], st2[:, j:j + 4], -AD ** -0.5, None, ALU.mult).then_inc(ev("at_max"), 1)
                maxima(0)
                dve.wait_ge(ev("c_sum"), 1)
                dve.tensor_scalar(lnm, ps[:, 0, 0:T], 1.0 / D, None, ALU.mult)
                dve.drain()
                dve.tensor_tensor(convT, convT, lnm.unsqueeze(1).to_broadcast([P, KC, T]), ALU.subtract)
                dve.drain().then_inc(ev("cen"), 1)
                for h in range(AH):
                    if h + 1 < AH:
                        if h >= 1:
                            dve.wait_ge(ev("at_T"), h)
                        maxima(h + 1)
                    if h == 0:
                        dve.wait_ge(ev("c_rstd"), 1)
                        dve.tensor_tensor(convT, convT, lnm.unsqueeze(1).to_broadcast([P, KC, T]), ALU.mult)
                        dve.drain().then_inc(ev("c_norm"), 1)
                    dve.wait_ge(ev("at_p"), h + 1)
                    j = 80 + 4 * (h % 2)
                    dve.reciprocal(st2[:, j:j + 4], st2[:, j:j + 4])
                    dve.drain()
                    dve.tensor_scalar(st2[:, j + 2:j + 4], st2[:, j + 2:j + 4], nlam, None, ALU.mult)
                    dve.drain()
                    for t, (a, b) in enumerate(((0, P), (P, 3 * P))):
                        p1 = pbuf[:, h % 2, 1, a:b]
                        dve.tensor_scalar(p1, p1, st2[:, j + 2 + t:j + 3 + t], None, ALU.mult)
                    dve.drain()
                    for t, (a, b) in enumerate(((0, P), (P, 3 * P))):
                        p0, p1 = pbuf[:, h % 2, 0, a:b], pbuf[:, h % 2, 1, a:b]
                        last = dve.scalar_tensor_tensor(p0, p0, st2[:, j + t:j + t + 1], p1, ALU.mult, ALU.add)
                    last.then_inc(ev("at_a"), 1)
                    dve.wait_ge(ev("at_o"), h + 1)
                    ot = o_tm[:, :, h * P:(h + 1) * P]
                    dve.tensor_copy(ot, ps[:, 3, 0:2 * P].rearrange("p (t d) -> p t d", t=TT)).then_inc(ev("at_oe"), 1)
                    dve.drain()
                    osq = lnm.rearrange("p (t d) -> p t d", t=TT)
                    dve.tensor_tensor(osq, ot, ot, ALU.mult)
                    dve.drain()
                    dve.tensor_reduce(st2[:, 0:16].rearrange("p (t h) -> p t h", t=TT)[:, :, h], osq, AX.X, ALU.add)
                dve.drain().then_inc(ev("o_ss"), 1)
                of = o_tm[:].rearrange("p t (h d) -> p (t h) d", d=2 * AD)
                gf = ga[:].rearrange("p t (h d) -> p (t h) d", d=2 * AD)
                dve.wait_ge(ev("o_rstd"), 1)
                dve.tensor_tensor(of, of, st2[:, 0:16].unsqueeze(2).to_broadcast([P, 16, 2 * AD]), ALU.mult)
                dve.drain()
                dve.tensor_tensor(of, of, subg.unsqueeze(1).to_broadcast([P, 16, 2 * AD]), ALU.mult)
                dve.wait_ge(ev("gates_sig"), 1)
                dve.drain()
                dve.tensor_tensor(of, of, gf, ALU.mult)
                dve.wait_ge(ev("gates_sig"), 2)
                dve.wait_ge(ev("bcu_in"), 32)
                for n in range(2):
                    for t in range(TT):
                        half = slice(n * 512, (n + 1) * 512)
                        tmp = v_tm[:, t, half]
                        dve.wait_ge(ev("pw"), 2 * n + t + 1)
                        dve.tensor_tensor(tmp, ps[:, 2 * n + t, :], bcu[:, 0, half], ALU.add)
                        dve.drain()
                        dve.tensor_tensor(tmp, tmp, gc[:, t, half], ALU.mult)
                        dve.drain()
                        dve.tensor_tensor(gc[:, t, half], tmp, o_tm[:, t, half], ALU.add)
                dve.drain().then_inc(ev("y2_ready"), 1)
                for n in range(2):
                    for t in range(TT):
                        half = slice(n * 512, (n + 1) * 512)
                        dve.wait_ge(ev("o2"), 2 * n + t + 1)
                        dve.tensor_tensor(v_tm[:, t, half], ps[:, 2 * n + t, :], bcu[:, 1, half], ALU.mult)
                        dve.drain()
                        dve.tensor_tensor(x_tm[:, t, half], x_tm[:, t, half], v_tm[:, t, half], ALU.add)
                dve.drain().then_inc(ev("h5_ready"), 1)
                dve.wait_ge(ev("n4_in"), 48)
                modulated("rstd6", bc2[:, 0, :], bc2[:, 1, :], bc2[:, 2, :])
                dve.drain().then_inc(ev("h6_ready"), 1)
                dve.wait_ge(ev("rw2_in"), 32)
                dve.memset(g1v[:, :, 4, :], FAR)
                dve.wait_ge(ev("scores"), 2)
                dve.tensor_tensor(cho, scr, rb2.unsqueeze(1).to_broadcast([P, TT, 64]), ALU.add)
                dve.drain()
                for t in range(TT):
                    for g in range(8):
                        dve.max(g8[:, t, g, :], cho[:, t, 8 * g:8 * g + 8])
                dve.drain()
                gs, gk, gx, gq = (g1v[:, :, r, :] for r in range(4))
                dve.tensor_tensor(gs, g8[:, :, :, 0], g8[:, :, :, 1], ALU.add)
                dve.drain()
                for t in range(TT):
                    dve.max(gk[:, t, :], gs[:, t, :])
                dve.drain()
                dve.tensor_copy(g1v[:, :, 4, 0:4], gk[:, :, 0:4])
                dve.drain()
                for t in range(TT):
                    dve.match_replace(gx[:, t, :], g1v[:, t, 4, :], gs[:, t, :], -FAR)
                dve.drain()
                dve.tensor_tensor(gq, gx, gs, ALU.not_equal)
                dve.drain()
                dve.tensor_scalar(gq, gq, BIG, -BIG, ALU.mult, ALU.add)
                dve.drain()
                for t in range(TT):
                    dve.tensor_tensor(cho[:, t, :].rearrange("p (g e) -> p g e", g=8), cho[:, t, :].rearrange("p (g e) -> p g e", g=8),
                                      gq[:, t, :].unsqueeze(2).to_broadcast([P, 8, 8]), ALU.add)
                dve.drain()
                for t in range(TT):
                    dve.max(gk[:, t, :], cho[:, t, :])
                dve.drain()
                for t in range(TT):
                    dve.match_replace(chm[:, t, :], gk[:, t, :], cho[:, t, :], -FAR)
                dve.drain()
                dve.tensor_tensor(m2.mask, chm, cho, ALU.not_equal)
                dve.drain()
                dve.tensor_tensor(m2.gate, scr, m2.mask, ALU.mult)
                dve.drain()
                dve.tensor_reduce(stat[:, 18:20], m2.gate, AX.X, ALU.add)
                dve.drain()
                dve.reciprocal(stat[:, 18:20], stat[:, 18:20])
                dve.drain()
                for t in range(TT):
                    dve.tensor_scalar(m2.gate[:, t, :], m2.gate[:, t, :], stat[:, 18 + t:19 + t], ROUTED_SCALE, ALU.mult, ALU.mult)
                for k in range(2):
                    dve.wait_ge(ev("sh_silu"), k + 1)
                    dve.wait_ge(ev("sh_gu"), k + 3)
                    dve.tensor_tensor(shT[:, k, :], ps[:, 6 + k, 0:T], shs[:, k, :], ALU.mult)
                dve.drain().then_inc(ev("sh_hid"), 1)
                route_lists_dve(dve, m2, ev, ps)
                moe_dve(dve, m2, ev, ps)
                dve.wait_ge(ev("b_acc"), 1)
                dve.wait_ge(ev("g2_in"), 16)
                for t in range(TT):
                    for n in range(2):
                        half = slice(n * 512, (n + 1) * 512)
                        dve.tensor_tensor(out_tm[:, t, half], ps[:, 2 * t + n, :], bc2[:, 0, half], ALU.mult)
                        dve.drain()
                        dve.tensor_tensor(out_tm[:, t, half], out_tm[:, t, half], x_tm[:, t, half], ALU.add).then_inc(
                            ev("out_ready"), 1)

            @second.tensor
            def _(pe):
                def product(bank, lhs, rhs, name=None, kk=KC, start=True):
                    for k in range(kk):
                        last = pe.matmul(bank, lhs(k), rhs(k), start=(k == 0 and start), stop=(k == kk - 1))
                    if name:
                        last.then_inc(ev(name), 1)

                def tok_tile(t):
                    return lambda k: hT[:, k, t * P:(t + 1) * P]

                pe.wait_ge(ev("c2_in"), 16 * 14)
                for j in range(2):
                    pe.transpose(ps[:, 0, 124 * j:124 * j + 124], drows[:, j, :], ident[0:124, 0:124])
                pe.transpose(ps[:, 0, 256:280], crows, ident[0:3 * KC, 0:3 * KC]).then_inc(ev("dw_T"), 1)
                pe.wait_ge(ev("hn5_ready"), 1)
                transposes(pe, hn_tm, 4, "h5_T")
                pe.wait_ge(ev("h5T_ready"), 1)
                for c in range(KC):
                    a, b = loads[L_A[2 * (c // 4)]], loads[L_A[2 * (c // 4) + 1]]
                    if c % 4 == 0:
                        arrived(pe, L_A[2 * (c // 4)])
                        arrived(pe, L_A[2 * (c // 4) + 1])
                    if c >= 2:
                        pe.wait_ge(ev("u_out"), c - 1)
                    for j, w in enumerate((a["dst"], b["dst"])):
                        product(ps[:, 2 * (c % 2) + j, 0:T], lambda k: w[:, k, (c % 4) * P:(c % 4 + 1) * P],
                                lambda k: hT[:, k, :], "u_proj")
                for g in range(12):
                    if g % 2 == 0:
                        arrived(pe, L_QKV[g // 2])
                    if g >= 4:
                        pe.wait_ge(ev("qkv_out"), g - 3)
                    w = loads[L_QKV[g // 2]]["dst"]
                    product(ps[:, 4 + g % 4, :], tok_tile(g % 2), lambda k: w[:, k, :], "qkv")
                pe.wait_ge(ev("qkv_out"), 12)
                for j, x in enumerate((q_tm, k_tm)):
                    pe.wait_ge(ev(("q2_ready", "k2_ready")[j]), 1)
                    if j:
                        pe.wait_ge(ev("qkT_ready"), 1)
                    transposes(pe, x, 4, "qk_T")
                pe.wait_ge(ev("qkT_ready"), 2)

                def scores(h):
                    if h >= 2:
                        pe.wait_ge(ev("at_max"), h - 1)
                    for mp in range(2):
                        b, bank = AD * mp, ps[:, 4 + 2 * (h % 2) + mp, :]
                        q, k = qT[b:b + AD, h, :], kT[b:b + AD, h, :]
                        pe.matmul(bank[:, 0:P], q[:, 0:P], k[:, 0:P], start=True, stop=True)
                        last = pe.matmul(bank[:, P:3 * P], q[:, P:T], k, start=True, stop=True)
                    last.then_inc(ev("at_s"), 1)

                def gate(g):
                    if g % 2 == 0:
                        arrived(pe, L_G[g // 2])
                    if g >= 2:
                        pe.wait_ge(ev("gates2_out"), g - 1)
                    w = loads[L_G[g // 2]]["dst"]
                    product(ps[:, g % 2, :], tok_tile(g % 2), lambda k: w[:, k, :], "gates2")
                scores(0)
                pe.wait_ge(ev("conv2"), 1)
                product(ps[:, 0, 0:T], lambda k: ones[:, 0:P], lambda k: convT[:, k, :], "c_sum")
                scores(1)
                pe.wait_ge(ev("c_sq"), 1)
                product(ps[:, 1, 0:T], lambda k: ones[:, 0:P], lambda k: gc_c[:, k, :], "c_ss")
                for h in range(AH):
                    if 0 < h < AH - 1:
                        scores(h + 1)
                    if h == 1:
                        pe.wait_ge(ev("c_rstd"), 1)
                    gate(h)
                    pe.wait_ge(ev("at_a"), h + 1)
                    if h:
                        pe.wait_ge(ev("at_oe"), h)
                    for j in range(3):
                        last = pe.transpose(ps[:, 2, j * P:(j + 1) * P], pbuf[:, h % 2, 0, j * P:(j + 1) * P], ident[:])
                    last.then_inc(ev("at_T"), 1)
                    pe.wait_ge(ev("at_Te"), h + 1)
                    vs = [v_tm[:, t, h * P:(h + 1) * P] for t in range(TT)]
                    pe.matmul(ps[:, 3, 0:P], aT[:, 0:P], vs[0], start=True, stop=True)
                    pe.matmul(ps[:, 3, P:2 * P], aT[:, P:2 * P], vs[0], start=True, stop=False)
                    pe.matmul(ps[:, 3, P:2 * P], aT[:, 2 * P:3 * P], vs[1], start=False, stop=True).then_inc(ev("at_o"), 1)
                pe.wait_ge(ev("at_oe"), AH)
                pe.wait_ge(ev("gates2_out"), 8)
                pe.wait_ge(ev("s_ready"), 1)
                for n in range(2):
                    arrived(pe, L_PW[n])
                    w = loads[L_PW[n]]["dst"]
                    for t in range(TT):
                        product(ps[:, 2 * n + t, :], lambda k: convT[:, k, t * P:(t + 1) * P], lambda k: w[:, k, :], "pw")
                pe.wait_ge(ev("y2_ready"), 1)
                transposes(pe, gc, 4, "y2_T")
                pe.wait_ge(ev("y2T_ready"), 1)
                for n in range(2):
                    arrived(pe, L_O2[n])
                    w = loads[L_O2[n]]["dst"]
                    for t in range(TT):
                        product(ps[:, 2 * n + t, :], tok_tile(t), lambda k: w[:, k, :], "o2")
                pe.wait_ge(ev("h6_ready"), 1)
                transposes(pe, hn_tm, 4, "h6_T")
                pe.wait_ge(ev("h6T_ready"), 1)
                pe.wait_ge(ev("rw2_in"), 32)
                for t in range(TT):
                    product(ps[:, t, 0:64], tok_tile(t), lambda k: rw2[:, k, :], "router2")
                arrived(pe, L_SGU)
                w = loads[L_SGU]["dst"]
                for j in range(4):
                    product(ps[:, 4 + j, 0:T], lambda k: w[:, k, j * P:(j + 1) * P], lambda k: hT[:, k, :], "sh_gu")
                pe.wait_ge(ev("sh_hid"), 1)
                pe.wait_ge(ev("scores"), 2)
                arrived(pe, L_SD)
                w = loads[L_SD]["dst"]
                for t in range(TT):
                    for n in range(2):
                        product(ps[:, 2 * t + n, :], lambda k: shT[:, k, t * P:(t + 1) * P],
                                lambda k: w[:, k, n * 512:(n + 1) * 512], kk=2)
                pe.drain().then_inc(ev("sh_d"), 1)
                route_lists_pe(pe, m2, ev, ps)
                moe_pe(pe, m2, ev, ps)


INPUTS = [
    "x", "p", "norm1_g", "w_in", "conv_w", "conv_b", "igate_b", "fgate_b", "mnorm_g", "sb_out_g", "sgu_ln_g",
    "sgu_ln_b", "sgu_w", "sgu_b", "sgu_out_g", "w_out", "norm2_g", "router_gw", "router_gb", "router_ew",
    "router_eb", "w_gate", "w_up", "w_down", "ple_norm_g", "ple_gate_w", "ple_proj_w", "final_g", "c_2",
    "positions_2", "w_ada_2", "b_ada_2", "norm1_g_2", "w_in_2", "conv_dw_2", "conv_dw_b_2", "conv_ln_g_2",
    "conv_ln_b_2", "w_pw2_2", "b_pw2_2", "q_norm_g_2", "k_norm_g_2", "lambda_q1_2", "lambda_k1_2",
    "lambda_q2_2", "lambda_k2_2", "subln_g_2", "w_out_2", "norm2_g_2", "w_router_2", "router_bias_2",
    "w_exp_gu_2", "w_exp_down_2", "w_sh_gu_2", "w_sh_down_2",
]


def kernel(**inputs):
    import numpy as _np
    import concourse.bacc as _bacc
    from concourse import mybir as _mybir
    from concourse.bass_utils import run_bass_kernel_spmd as _run

    nc = _bacc.Bacc("TRN2", target_bir_lowering=False, num_devices=1)
    arrays, aps = {}, {}
    for name in INPUTS:
        a = _np.ascontiguousarray(inputs[name])
        arrays["in_" + name] = a
        aps[name] = nc.dram_tensor("in_" + name, a.shape, _mybir.dt.from_np(a.dtype), kind="ExternalInput").ap()
    out = nc.dram_tensor("out_x", (1, T, D), F32, kind="ExternalOutput").ap()
    build_program(nc, aps, out)
    r = _run(nc, [arrays], core_ids=[0])
    return r.results[0]["out_x"]
```
